# Optimizing a Trainium2 kernel written in Bass

```python
import math
import jax
import jax.numpy as jnp
from jax import lax
import numpy as np

D_MODEL = 1024
BATCH = 1
SEQ = 512
DEPTH = 1

GDN_HEADS = 4
GDN_DK = 64
GDN_DV = 64
GDN_CONV = 4
GDN_CHUNK = 64
MOBA_HEADS = 4
MOBA_HD = 64
MOBA_BLOCK = 256
MOBA_TOPK = 3
MOBA_QCHUNK = 32
MLA_HEADS = 4
MLA_Q_LORA = 192
MLA_KV_LORA = 128
MLA_NOPE = 64
MLA_ROPE = 32
MLA_V = 64
MLA_QBLOCK = 128
ROPE_THETA = 10000.0
S5_GROUP = 16
S5_GROUPS = 16
S5_WIDTH = S5_GROUP * S5_GROUPS
S5_STATE = 64
D_FF = 2816
FFN_CONV = 3
EPS = 1e-6

GDN_W = GDN_HEADS * GDN_DV
MOBA_W = MOBA_HEADS * MOBA_HD
MLA_W = MLA_HEADS * MLA_V
D_MIX = GDN_W + MOBA_W + MLA_W + S5_WIDTH
SPLITS = (GDN_HEADS * GDN_DK, GDN_HEADS * GDN_DK, GDN_W, GDN_W, GDN_HEADS, GDN_HEADS,
          MOBA_W, MOBA_W, MOBA_W,
          MLA_Q_LORA, MLA_KV_LORA, MLA_ROPE,
          S5_WIDTH)
N_IN = sum(SPLITS)

kernel_name = 'hymba_style_hybrid_trunk'

def rmsnorm(x, g):
    xf = x.astype(jnp.float32)
    y = xf * lax.rsqrt(jnp.mean(xf * xf, axis=-1, keepdims=True) + EPS)
    return (y * g.astype(jnp.float32)).astype(x.dtype)

def l2norm(x):
    return x * lax.rsqrt(jnp.sum(x * x, axis=-1, keepdims=True) + EPS)

def causal_dwconv(x, w):
    k, c = w.shape
    return lax.conv_general_dilated(x, w[:, None, :].astype(x.dtype), window_strides=(1,),
                                    padding=[(k - 1, 0)], dimension_numbers=('NWC', 'WIO', 'NWC'),
                                    feature_group_count=c)

def rope(t, cos, sin):
    t1, t2 = jnp.split(t, 2, axis=-1)
    return jnp.concatenate([t1 * cos - t2 * sin, t2 * cos + t1 * sin], axis=-1)

def gated_deltanet(q, k, v, z, a, bgate, conv_w, a_log, dt_bias, norm_g):
    f32 = jnp.float32
    b, l, _ = q.shape
    h, dk, dv, c = GDN_HEADS, GDN_DK, GDN_DV, GDN_CHUNK
    n = l // c
    qkv = jax.nn.silu(causal_dwconv(jnp.concatenate([q, k, v], axis=-1), conv_w)).astype(f32)
    q, k, v = jnp.split(qkv, 3, axis=-1)
    q = l2norm(q.reshape(b, l, h, dk)) * (dk ** -0.5)
    k = l2norm(k.reshape(b, l, h, dk))
    v = v.reshape(b, l, h, dv)
    beta = jax.nn.sigmoid(bgate.astype(f32))
    g = -jnp.exp(a_log.astype(f32)) * jax.nn.softplus(a.astype(f32) + dt_bias.astype(f32))

    def chunk(t, d):
        return t.reshape(b, n, c, h, d).transpose(0, 3, 1, 2, 4)

    q, k, v = chunk(q, dk), chunk(k, dk), chunk(v, dv)
    beta = beta.reshape(b, n, c, h).transpose(0, 3, 1, 2)
    gam = jnp.cumsum(g.reshape(b, n, c, h).transpose(0, 3, 1, 2), axis=-1)
    causal = jnp.tril(jnp.ones((c, c), dtype=bool))
    strict = jnp.tril(jnp.ones((c, c), dtype=bool), -1)
    decay = jnp.exp(jnp.where(causal, gam[..., :, None] - gam[..., None, :], -jnp.inf))
    kk = jnp.einsum('bhnid,bhnjd->bhnij', k, k)
    lower = jnp.where(strict, beta[..., :, None] * kk * decay, 0.0)
    tmat = lower + jnp.eye(c, dtype=f32)
    rhs = jnp.concatenate([beta[..., None] * v, (beta * jnp.exp(gam))[..., None] * k], axis=-1)
    sol = lax.linalg.triangular_solve(tmat, rhs, left_side=True, lower=True, unit_diagonal=True)
    u, w = sol[..., :dv], sol[..., dv:]
    attn = jnp.einsum('bhnid,bhnjd->bhnij', q, k) * decay
    q_dec = q * jnp.exp(gam)[..., None]
    k_dec = k * jnp.exp(gam[..., -1:] - gam)[..., None]
    g_last = jnp.exp(gam[..., -1])

    def step(s, inp):
        u_c, w_c, a_c, qd_c, kd_c, gl_c = inp
        v_new = u_c - jnp.einsum('bhck,bhkv->bhcv', w_c, s)
        o = jnp.einsum('bhck,bhkv->bhcv', qd_c, s) + jnp.einsum('bhij,bhjv->bhiv', a_c, v_new)
        s = gl_c[..., None, None] * s + jnp.einsum('bhck,bhcv->bhkv', kd_c, v_new)
        return s, o

    xs = (jnp.moveaxis(u, 2, 0), jnp.moveaxis(w, 2, 0), jnp.moveaxis(attn, 2, 0),
          jnp.moveaxis(q_dec, 2, 0), jnp.moveaxis(k_dec, 2, 0), jnp.moveaxis(g_last, 2, 0))
    _, o = lax.scan(step, jnp.zeros((b, h, dk, dv), f32), xs)
    o = o.transpose(1, 0, 3, 2, 4).reshape(b, l, h, dv)
    o = o * lax.rsqrt(jnp.mean(o * o, axis=-1, keepdims=True) + EPS) * norm_g.astype(f32)
    o = o * jax.nn.silu(z.astype(f32).reshape(b, l, h, dv))
    return o.reshape(b, l, h * dv).astype(z.dtype)

def moba_attention(q, k, v):
    f32 = jnp.float32
    b, l, h, d = q.shape
    bs, qc = MOBA_BLOCK, MOBA_QCHUNK
    nb = -(-l // bs)
    lp = nb * bs
    padw = ((0, 0), (0, lp - l), (0, 0), (0, 0))
    qh = jnp.pad(q, padw).transpose(0, 2, 1, 3)
    kb = jnp.pad(k, padw).transpose(0, 2, 1, 3).reshape(b, h, nb, bs, d)
    vb = jnp.pad(v, padw).transpose(0, 2, 1, 3).reshape(b, h, nb, bs, d)
    kmean = jnp.mean(kb.astype(f32), axis=3)
    topk = min(MOBA_TOPK, nb - 1)
    scale = d ** -0.5
    bi = jnp.arange(b)[:, None, None, None]
    hi = jnp.arange(h)[None, :, None, None]

    def query_chunk(ci):
        start = ci * qc
        own = start // bs
        q_c = lax.dynamic_slice_in_dim(qh, start, qc, axis=2)
        k_own = lax.dynamic_index_in_dim(kb, own, axis=2, keepdims=False)
        v_own = lax.dynamic_index_in_dim(vb, own, axis=2, keepdims=False)
        qpos = start + jnp.arange(qc)
        kpos = own * bs + jnp.arange(bs)
        s_own = jnp.einsum('bhqd,bhjd->bhqj', q_c, k_own).astype(f32) * scale
        s_own = jnp.where(kpos[None, :] <= qpos[:, None], s_own, -jnp.inf)
        if topk == 0:
            p = jax.nn.softmax(s_own, axis=-1).astype(v.dtype)
            return jnp.einsum('bhqj,bhjd->bhqd', p, v_own)
        gate = jnp.einsum('bhqd,bhnd->bhqn', q_c.astype(f32), kmean)
        gate = jnp.where(jnp.arange(nb) < own, gate, -jnp.inf)
        _, idx = lax.top_k(gate, topk)
        k_sel = kb[bi, hi, idx]
        v_sel = vb[bi, hi, idx]
        s_sel = jnp.einsum('bhqd,bhqnjd->bhqnj', q_c, k_sel).astype(f32) * scale
        s_sel = jnp.where((jnp.arange(topk) < own)[:, None], s_sel, -jnp.inf)
        s = jnp.concatenate([s_sel.reshape(b, h, qc, topk * bs), s_own], axis=-1)
        p = jax.nn.softmax(s, axis=-1).astype(v.dtype)
        p_sel = p[..., :topk * bs].reshape(b, h, qc, topk, bs)
        return (jnp.einsum('bhqnj,bhqnjd->bhqd', p_sel, v_sel)
                + jnp.einsum('bhqj,bhjd->bhqd', p[..., topk * bs:], v_own))

    o = lax.map(query_chunk, jnp.arange(lp // qc))
    o = o.transpose(1, 0, 3, 2, 4).reshape(b, lp, h, d)[:, :l]
    return o.reshape(b, l, h * d)

def mla_attention(c_q, c_kv, k_rope, q_norm_g, w_uq, kv_norm_g, w_ukv, cos, sin):
    f32 = jnp.float32
    b, l, _ = c_q.shape
    h = MLA_HEADS
    q = (rmsnorm(c_q, q_norm_g) @ w_uq).reshape(b, l, h, MLA_NOPE + MLA_ROPE)
    q_nope, q_rot = q[..., :MLA_NOPE], rope(q[..., MLA_NOPE:], cos[:, None, :], sin[:, None, :])
    kv = (rmsnorm(c_kv, kv_norm_g) @ w_ukv).reshape(b, l, h, MLA_NOPE + MLA_V)
    k_nope, v = kv[..., :MLA_NOPE], kv[..., MLA_NOPE:]
    k_rot = rope(k_rope, cos, sin)
    scale = (MLA_NOPE + MLA_ROPE) ** -0.5
    kpos = jnp.arange(l)

    def q_block(i):
        start = i * MLA_QBLOCK
        qn = lax.dynamic_slice_in_dim(q_nope, start, MLA_QBLOCK, axis=1)
        qr = lax.dynamic_slice_in_dim(q_rot, start, MLA_QBLOCK, axis=1)
        s = (jnp.einsum('bqhd,bkhd->bhqk', qn, k_nope)
             + jnp.einsum('bqhd,bkd->bhqk', qr, k_rot)).astype(f32) * scale
        qpos = start + jnp.arange(MLA_QBLOCK)
        s = jnp.where(kpos[None, :] <= qpos[:, None], s, -jnp.inf)
        p = jax.nn.softmax(s, axis=-1).astype(v.dtype)
        return jnp.einsum('bhqk,bkhd->bqhd', p, v)

    o = lax.map(q_block, jnp.arange(l // MLA_QBLOCK))
    return o.transpose(1, 0, 2, 3, 4).reshape(b, l, h * MLA_V)

def s5_ssm(u, lam_re, lam_im, b_re, b_im, c_re, c_im, d, log_dt, glu_w, glu_b):
    f32 = jnp.float32
    bsz, l, _ = u.shape
    uf = u.astype(f32).reshape(bsz, l, S5_GROUPS, S5_GROUP)
    lr = jnp.minimum(lam_re.astype(f32), -1e-4)
    li = lam_im.astype(f32)
    dt = jnp.exp(log_dt.astype(f32))[:, None]
    mag = jnp.exp(lr * dt)
    ar, ai = mag * jnp.cos(li * dt), mag * jnp.sin(li * dt)
    den = lr * lr + li * li
    cr = ((ar - 1.0) * lr + ai * li) / den
    ci = (ai * lr - (ar - 1.0) * li) / den
    br, bim = b_re.astype(f32), b_im.astype(f32)
    bbr = cr[..., None] * br - ci[..., None] * bim
    bbi = cr[..., None] * bim + ci[..., None] * br
    bur = jnp.einsum('blgc,gpc->blgp', uf, bbr)
    bui = jnp.einsum('blgc,gpc->blgp', uf, bbi)
    a_r = jnp.broadcast_to(ar, (1, l, S5_GROUPS, S5_STATE))
    a_i = jnp.broadcast_to(ai, (1, l, S5_GROUPS, S5_STATE))

    def combine(e1, e2):
        a1r, a1i, b1r, b1i = e1
        a2r, a2i, b2r, b2i = e2
        return (a2r * a1r - a2i * a1i, a2r * a1i + a2i * a1r,
                a2r * b1r - a2i * b1i + b2r, a2r * b1i + a2i * b1r + b2i)

    _, _, xr, xi = lax.associative_scan(combine, (a_r, a_i, bur, bui), axis=1)
    y = (jnp.einsum('blgp,gcp->blgc', xr, c_re.astype(f32))
         - jnp.einsum('blgp,gcp->blgc', xi, c_im.astype(f32))
         + d.astype(f32) * uf)
    y = jax.nn.gelu(y.reshape(bsz, l, S5_WIDTH))
    y = y * jax.nn.sigmoid(y @ glu_w.astype(f32) + glu_b.astype(f32))
    return y.astype(u.dtype)

def hybrid_layer(x, cos, sin, norm1_g, w_in, gdn_conv_w, gdn_a_log, gdn_dt_bias, gdn_norm_g,
                 mla_q_norm_g, mla_w_uq, mla_kv_norm_g, mla_w_ukv,
                 s5_lam_re, s5_lam_im, s5_b_re, s5_b_im, s5_c_re, s5_c_im, s5_d, s5_log_dt,
                 s5_glu_w, s5_glu_b, w_out, norm2_g, ffn_w_up, ffn_conv_w, ffn_w_down):
    b, l, _ = x.shape
    h = rmsnorm(x, norm1_g)
    proj = h @ w_in
    offs = np.cumsum(SPLITS)[:-1].tolist()
    (a_q, a_k, a_v, a_z, a_a, a_b, m_q, m_k, m_v, c_q, c_kv, c_kr, s_u) = jnp.split(proj, offs, axis=-1)
    o_a = gated_deltanet(a_q, a_k, a_v, a_z, a_a, a_b, gdn_conv_w, gdn_a_log, gdn_dt_bias, gdn_norm_g)
    o_b = moba_attention(m_q.reshape(b, l, MOBA_HEADS, MOBA_HD), m_k.reshape(b, l, MOBA_HEADS, MOBA_HD),
                         m_v.reshape(b, l, MOBA_HEADS, MOBA_HD))
    o_c = mla_attention(c_q, c_kv, c_kr, mla_q_norm_g, mla_w_uq, mla_kv_norm_g, mla_w_ukv, cos, sin)
    o_d = s5_ssm(s_u, s5_lam_re, s5_lam_im, s5_b_re, s5_b_im, s5_c_re, s5_c_im, s5_d, s5_log_dt,
                 s5_glu_w, s5_glu_b)
    x = x + jnp.concatenate([o_a, o_b, o_c, o_d], axis=-1) @ w_out
    h = rmsnorm(x, norm2_g)
    gate, val = jnp.split(causal_dwconv(h @ ffn_w_up, ffn_conv_w), 2, axis=-1)
    return x + (jax.nn.silu(gate) * val) @ ffn_w_down

def setup_inputs(seed: int = 0) -> dict:
    key = jax.random.key(seed)
    ks = jax.random.split(key, 32)
    f32 = jnp.float32

    def nrm(i, shape, scale):
        return scale * jax.random.normal(ks[i], shape, f32)

    def gain(i, shape):
        return 1.0 + nrm(i, shape, 0.02)

    dt_gdn = jnp.exp(jax.random.uniform(ks[4], (DEPTH, GDN_HEADS), f32, math.log(1e-3), math.log(1e-1)))
    return {
        'x': nrm(0, (BATCH, SEQ, D_MODEL), 1.0),
        'norm1_g': gain(1, (DEPTH, D_MODEL)),
        'w_in': nrm(2, (DEPTH, D_MODEL, N_IN), D_MODEL ** -0.5),
        'gdn_conv_w': nrm(3, (DEPTH, GDN_CONV, 3 * GDN_W), GDN_CONV ** -0.5),
        'gdn_a_log': jnp.log(jax.random.uniform(ks[5], (DEPTH, GDN_HEADS), f32, 1.0, 16.0)),
        'gdn_dt_bias': dt_gdn + jnp.log(-jnp.expm1(-dt_gdn)),
        'gdn_norm_g': gain(6, (DEPTH, GDN_DV)),
        'mla_q_norm_g': gain(7, (DEPTH, MLA_Q_LORA)),
        'mla_w_uq': nrm(8, (DEPTH, MLA_Q_LORA, MLA_HEADS * (MLA_NOPE + MLA_ROPE)), MLA_Q_LORA ** -0.5),
        'mla_kv_norm_g': gain(9, (DEPTH, MLA_KV_LORA)),
        'mla_w_ukv': nrm(10, (DEPTH, MLA_KV_LORA, MLA_HEADS * (MLA_NOPE + MLA_V)), MLA_KV_LORA ** -0.5),
        's5_lam_re': -0.5 + nrm(11, (DEPTH, S5_GROUPS, S5_STATE), 0.01),
        's5_lam_im': jnp.pi * jnp.arange(S5_STATE, dtype=f32) + nrm(12, (DEPTH, S5_GROUPS, S5_STATE), 0.01),
        's5_b_re': nrm(13, (DEPTH, S5_GROUPS, S5_STATE, S5_GROUP), (2 * S5_GROUP) ** -0.5),
        's5_b_im': nrm(14, (DEPTH, S5_GROUPS, S5_STATE, S5_GROUP), (2 * S5_GROUP) ** -0.5),
        's5_c_re': nrm(15, (DEPTH, S5_GROUPS, S5_GROUP, S5_STATE), S5_STATE ** -0.5),
        's5_c_im': nrm(16, (DEPTH, S5_GROUPS, S5_GROUP, S5_STATE), S5_STATE ** -0.5),
        's5_d': nrm(17, (DEPTH, S5_GROUPS, S5_GROUP), 1.0),
        's5_log_dt': jax.random.uniform(ks[18], (DEPTH, S5_GROUPS), f32, math.log(1e-3), math.log(1e-1)),
        's5_glu_w': nrm(19, (DEPTH, S5_WIDTH, S5_WIDTH), S5_WIDTH ** -0.5),
        's5_glu_b': nrm(20, (DEPTH, S5_WIDTH), 0.01),
        'w_out': nrm(21, (DEPTH, D_MIX, D_MODEL), D_MIX ** -0.5),
        'norm2_g': gain(22, (DEPTH, D_MODEL)),
        'ffn_w_up': nrm(23, (DEPTH, D_MODEL, 2 * D_FF), D_MODEL ** -0.5),
        'ffn_conv_w': nrm(24, (DEPTH, FFN_CONV, 2 * D_FF), FFN_CONV ** -0.5),
        'ffn_w_down': nrm(25, (DEPTH, D_FF, D_MODEL), D_FF ** -0.5),
        'final_norm_g': gain(26, (D_MODEL,)),
    }

def reference(x, norm1_g, w_in, gdn_conv_w, gdn_a_log, gdn_dt_bias, gdn_norm_g,
              mla_q_norm_g, mla_w_uq, mla_kv_norm_g, mla_w_ukv,
              s5_lam_re, s5_lam_im, s5_b_re, s5_b_im, s5_c_re, s5_c_im, s5_d, s5_log_dt,
              s5_glu_w, s5_glu_b, w_out, norm2_g, ffn_w_up, ffn_conv_w, ffn_w_down, final_norm_g):
    l = x.shape[1]
    inv_freq = ROPE_THETA ** (-jnp.arange(0, MLA_ROPE, 2, dtype=jnp.float32) / MLA_ROPE)
    ang = jnp.arange(l, dtype=jnp.float32)[:, None] * inv_freq[None, :]
    cos = jnp.cos(ang).astype(x.dtype)
    sin = jnp.sin(ang).astype(x.dtype)
    for i in range(DEPTH):
        x = hybrid_layer(x, cos, sin, norm1_g[i], w_in[i], gdn_conv_w[i], gdn_a_log[i], gdn_dt_bias[i],
                         gdn_norm_g[i], mla_q_norm_g[i], mla_w_uq[i], mla_kv_norm_g[i], mla_w_ukv[i],
                         s5_lam_re[i], s5_lam_im[i], s5_b_re[i], s5_b_im[i], s5_c_re[i], s5_c_im[i],
                         s5_d[i], s5_log_dt[i], s5_glu_w[i], s5_glu_b[i], w_out[i], norm2_g[i],
                         ffn_w_up[i], ffn_conv_w[i], ffn_w_down[i])
    return rmsnorm(x, final_norm_g)


_drawn_inputs = setup_inputs


def setup_inputs(seed=0):
    import zlib

    import numpy as np

    out = dict(_drawn_inputs(seed))
    spreads = {}
    factors = {'norm1_g': 4.096,
     'gdn_norm_g': 8.0,
     'mla_q_norm_g': 8.0,
     'mla_kv_norm_g': 8.0,
     's5_lam_re': 64.0,
     's5_lam_im': 25.424,
     's5_b_re': 35.528,
     's5_b_im': 36.936,
     's5_c_re': 35.232,
     's5_c_im': 35.416,
     's5_log_dt': 26.928,
     's5_glu_b': 200.0,
     'norm2_g': 11.487,
     'final_norm_g': 21.93}
    for name, (base, spread) in spreads.items():
        noise = np.random.default_rng([zlib.crc32(name.encode()), seed]).standard_normal(out[name].shape)
        drawn = base * np.exp(spread * noise) if base else spread * noise
        out[name] = jnp.asarray(drawn.astype(out[name].dtype))
    for name, factor in factors.items():
        out[name] = (out[name] * factor).astype(out[name].dtype)
    return out
```

```python
import math
from contextlib import ExitStack

import numpy as np

import concourse.bass as bass
from concourse import mybir

F32 = mybir.dt.float32
F32R = mybir.dt.float32r
BF16 = mybir.dt.bfloat16
ALU = mybir.AluOpType
ACT = mybir.ActivationFunctionType
AX = mybir.AxisListType

P = 128
L = 512
TT = L // P
D = 1024
KD = D // P
H = 4
HD = 64
PAIRS = H // 2
CH = 64
NCH = L // CH
QLORA, KVLORA, ROPE, MLA_QK = 192, 128, 32, 96
G, GW, NS = 16, 16, 64
ST = G * NS // P
HALF = L // 2
DFF = 2816
JF = DFF // P
EPS = 1e-6
BIG = 1e30
ROUND = 1.5 * 2.0 ** 23
TWO_PI = (6.28125, 1.9350051879882812e-3, 3.0199159819567529e-7)

A_Q, A_K, A_V, A_Z, A_A, A_B, M_Q, M_K, M_V, C_Q, C_KV, C_KR, S_U = (
    0, 256, 512, 768, 1024, 1028, 1032, 1288, 1544, 1800, 1992, 2120, 2152)

PROJ = [
    ("q0", [(0, A_Q, 128)]), ("k0", [(0, A_K, 128)]), ("v0", [(0, A_V, 128)]),
    ("misc", [(0, C_KR, 32), (32, C_KR + 16, 16), (48, C_KR, 16), (64, A_A, 32), (96, A_B, 32)]),
    ("u0", [(0, S_U, 128)]), ("u1", [(0, S_U + 128, 128)]),
    ("q1", [(0, A_Q + 128, 128)]), ("k1", [(0, A_K + 128, 128)]), ("v1", [(0, A_V + 128, 128)]),
    ("z0", [(0, A_Z, 128)]), ("z1", [(0, A_Z + 128, 128)]),
    ("cq0", [(0, C_Q, 128)]), ("cq1", [(0, C_Q + 128, 64)]), ("ckv", [(0, C_KV, 128)]),
    ("mq0", [(0, M_Q, 128)]), ("mk0", [(0, M_K, 128)]), ("mv0", [(0, M_V, 128)]),
    ("mq1", [(0, M_Q + 128, 128)]), ("mk1", [(0, M_K + 128, 128)]), ("mv1", [(0, M_V + 128, 128)]),
]
PN = {name: n for n, (name, _) in enumerate(PROJ)}
NPROJ = len(PROJ)
N_OUT0 = NPROJ
N_UP0 = N_OUT0 + KD
N_DOWN0 = N_UP0 + 2 * JF
RING = 4
RAW = 2

V_N1, V_N2, V_CONV, V_QN, V_KVN, V_GLUB, V_SD, V_GN, V_LRE, V_LIM, V_LDT, V_DTB, V_ALOG, V_ROWS = (
    0, 8, 16, 40, 42, 43, 45, 47, 48, 56, 64, 72, 73, 74)

_CONSTS = [("ident", 128), ("istack", 64), ("blockones", 128), ("ones", 128), ("dmask", 64),
           ("level", 6 * 64), ("selbc", 2 * 128), ("seltok", 2 * 8), ("scanmask", L), ("ropec", L),
           ("ropes", L), ("bmask", 2), ("cmask", 2), ("causal", 128)]
CO, _at = {}, 0
for _n, _w in _CONSTS:
    CO[_n] = _at
    _at += _w
CONST_COLS = _at


def constants():
    c = np.zeros((P, CONST_COLS), np.float32)

    def put(name, a):
        c[:a.shape[0], CO[name]:CO[name] + a.shape[1]] = a

    r = np.arange(P)
    j, i = r[:, None] % CH, np.arange(CH)[None, :]
    put("ident", np.eye(P, dtype=np.float32))
    put("istack", (j == i).astype(np.float32))
    put("blockones", (r[:, None] // HD == r[None, :] // HD).astype(np.float32))
    put("ones", np.ones((P, P), np.float32))
    put("dmask", np.where(i >= j, 0.0, -BIG).astype(np.float32))
    for l in range(6):
        s = 1 << l
        m = (i > j) & (i // (2 * s) == j // (2 * s)) & (i // s != j // s)
        c[:, CO["level"] + 64 * l:CO["level"] + 64 * (l + 1)] = m
    for p in range(PAIRS):
        for a in range(2):
            h = 2 * p + a
            for base in (0, 32):
                c[base + h, CO["selbc"] + 128 * p + 64 * a:CO["selbc"] + 128 * p + 64 * (a + 1)] = 1.0
            for q in range(4):
                c[32 * q + h, CO["seltok"] + 8 * a + 2 * q + p] = 1.0
    put("scanmask", np.broadcast_to((np.arange(L) % CH != 0).astype(np.float32), (P, L)))
    freq = np.float32(10000.0) ** (-np.arange(0, ROPE, 2, dtype=np.float32) / np.float32(ROPE))
    ang = np.arange(L, dtype=np.float32)[None, :] * freq.astype(np.float32)[:, None]
    cos, sin = np.cos(ang).astype(np.float32), np.sin(ang).astype(np.float32)
    put("ropec", np.tile(np.concatenate([cos, cos]), (4, 1)))
    put("ropes", np.tile(np.concatenate([-sin, sin]), (4, 1)))
    gg = np.arange(2)[None, :]
    put("bmask", (r[:, None] // NS == gg).astype(np.float32))
    put("cmask", ((r[:, None] // GW) % 2 == gg).astype(np.float32))
    put("causal", np.where(r[None, :] <= r[:, None], 0.0, -BIG).astype(np.float32))
    return c


def hybrid_trunk(nc, a):
    ctx = ExitStack()
    with ctx:
        def sb(name, shape, dt=F32):
            return ctx.enter_context(nc.sbuf_tensor(name, shape, dt))

        def sem(name):
            return ctx.enter_context(nc.semaphore(name))

        x_sb = sb("x_sb", [P, TT, D])
        hT_hi = sb("hT_hi", [P, KD, L], F32R)
        hT_lo = sb("hT_lo", [P, KD, L], F32R)
        w_raw = sb("w_raw", [P, RAW, D])
        w_hi = sb("w_hi", [P, RING, D], F32R)
        w_lo = sb("w_lo", [P, RING, D], F32R)
        const = sb("const", [P, CONST_COLS])
        ident16 = sb("ident16", [P, P], BF16)
        causal16 = sb("causal16", [P, P], BF16)
        vrows = sb("vrows", [P, P])
        ldt = sb("ldt", [P, 2])
        vec = sb("vec", [P, V_ROWS])
        taps_rows = sb("taps_rows", [P, 2, P])
        taps = sb("taps", [P, 3, 2 * JF, 1])
        fixed = sb("fixed", [P, 4])
        small = sb("small", [P, 8])

        FREE = nc.sbuf_bytes_remaining // 4 - 64
        arena = sb("arena", [P, FREE])
        top = [0]
        spans = {}

        def take(name, n, at=None):
            start = top[0] if at is None else at
            if at is None:
                top[0] += n
            assert start + n <= FREE, (name, start + n, FREE)
            spans[name] = (start, n)
            return arena[:, start:start + n]

        gq = [take(f"gq{p}", L) for p in range(PAIRS)]
        gk = [take(f"gk{p}", L) for p in range(PAIRS)]
        gv = [take(f"gv{p}", L) for p in range(PAIRS)]
        gz = [take(f"gz{p}", L) for p in range(PAIRS)]
        misc = take("misc", L)
        G0 = top[0]
        bd_names = ["KN", "QD", "ATT", "CM", "Y", "KW", "KD"]
        BD = {n: take("bd" + n, 2 * L).rearrange("p (c a i) -> p c a i", c=NCH, a=2) for n in bd_names}
        cp_names = ["DT", "LT", "X", "M1", "VP"]
        CP = {n: take("cp" + n, L).rearrange("p (c i) -> p c i", c=NCH) for n in cp_names}
        rows = take("rows", L)
        tok = take("tok", NCH * 8).rearrange("p (c q r) -> p c q r", c=NCH, q=4)
        glast = take("glast", NCH)
        state = take("state", 2 * HD).rearrange("p (b v) -> p b v", b=2)
        vnew = take("vnew", 2 * HD).rearrange("p (b v) -> p b v", b=2)
        onorm = take("onorm", 2 * NCH).rearrange("p (b c) -> p b c", b=2)
        G1 = top[0]
        su = [take(f"su{f}", L) for f in range(2)]
        work = [take(f"work{n}", L).rearrange("p (h t) -> p h t", h=2) for n in range(8)]
        bt = take("bt", 4 * P).rearrange("p (r f n) -> p r f n", r=2, f=2)
        ct = take("ct", 2 * ST * 32).rearrange("p (r s n) -> p r s n", r=2, s=ST)
        s5p = take("s5p", 24 * ST).rearrange("p (k s) -> p k s", s=ST)
        s5c = take("s5c", 4)
        gluw = take("gluw", 512).rearrange("p (k n) -> p k n", k=2)
        moq = [take(f"moq{p}", L) for p in range(PAIRS)]
        mok = [take(f"mok{p}", L) for p in range(PAIRS)]
        mov = take("mov", TT * 256).rearrange("p (t n) -> p t n", t=TT)
        cq = [take(f"cq{f}", L) for f in range(2)]
        ckv = take("ckv", L)

        b_nat = work[0].rearrange("p h t -> p (h t)")[:, 0:2 * P].rearrange("p (r s c) -> p r s c", r=2, s=ST)
        bbar = work[1].rearrange("p h t -> p (h t)")[:, 0:2 * P].rearrange("p (r s c) -> p r s c", r=2, s=ST)
        btmp = work[2].rearrange("p h t -> p (h t)")[:, 0:P].rearrange("p (s c) -> p s c", s=ST)
        bbd = work[3].rearrange("p h t -> p (h t)").rearrange("p (r s g c) -> p r s g c", r=2, s=ST, g=2)
        c_nat = work[4].rearrange("p h t -> p (h t)")[:, 0:4 * NS].rearrange("p (r f n) -> p r f n", r=2, f=2)
        cbd = work[5].rearrange("p h t -> p (h t)").rearrange("p (r f g n) -> p r f g n", r=2, f=2, g=2)

        xw = x_sb[:].rearrange("p t d -> p (t d)")
        cosT = xw[:, 0:ST * HALF].rearrange("p (s t) -> p s t", s=ST)
        sinT = xw[:, ST * HALF:2 * ST * HALF].rearrange("p (s t) -> p s t", s=ST)

        at = G0
        def over(name, n):
            nonlocal at
            v = take(name, n, at=at)
            at += n
            assert at <= G1, name
            return v
        q96 = over("q96", H * L).rearrange("p (h t) -> p h t", h=H)
        k96 = over("k96", H * L).rearrange("p (h t) -> p h t", h=H)
        mlav = over("mlav", TT * 256).rearrange("p (t n) -> p t n", t=TT)
        wuq = over("wuq", 2 * 512).rearrange("p (k n) -> p k n", k=2)
        wukv = over("wukv", 512)
        rope1, rope2, mrs = gq[0], gk[0], [gq[1], gk[1]]
        prob = [over(f"prob{b}", L) for b in range(2)]
        probT = [over(f"probT{b}", L).rearrange("p (k q) -> p k q", k=TT) for b in range(2)]
        smx = over("smx", 4 * 32).rearrange("p (k u) -> p k u", k=4)

        g_sb = take("g_sb", JF * L, at=0).rearrange("p (j t) -> p j t", j=JF)
        F0 = JF * L
        conv = [take(f"conv{b}", L, at=F0 + b * L) for b in range(4)]
        fing = take("fing", D, at=F0 + 4 * L)
        norm2 = take("norm2", TT * D, at=0).rearrange("p (t d) -> p t d", t=TT)
        junk = take("junk", D, at=F0 + 4 * L + D)
        stat = take("stat", 32, at=F0 + 4 * L + 2 * D)

        ps = ctx.enter_context(nc.psum_tensor("ps", [P, 8 * L], F32))

        def bank(b, n=L):
            return ps[:, b * L:b * L + n]

        s_x = [sem(f"x_loaded{t}") for t in range(TT)]
        s_const = sem("const_loaded")
        s_vrows = sem("vrows_loaded")
        s_taps = sem("taps_loaded")
        s_s5in = sem("s5_params_loaded")
        s_glu = sem("glu_w_loaded")
        s_mlaw = sem("mla_w_loaded")
        s_xre = sem("x_reloaded")
        s_fing = sem("final_gain_loaded")
        s_store = sem("stored")
        w_loaded = [sem(f"w_loaded{s}") for s in range(RING)]
        w_h = sem("w_high_ready")
        w_l = sem("w_low_ready")
        w_used = sem("w_used")
        act_step = sem("scalar_step")
        dve_step = sem("vector_step")
        pool_step = sem("pool_step")
        cleared = sem("tiles_cleared")
        vclear = sem("vrows_cleared")
        masks16 = sem("bf16_masks_ready")
        vec_t = sem("vec_transposed")
        vec_r = sem("vec_ready")
        xsq = sem("x_squares")
        xn = sem("x_normed")
        hT_t = sem("h_transposed")
        hT_h = sem("h_high_ready")
        hT_l = sem("h_low_ready")
        proj_done = sem("proj_done")
        proj_free = [sem(f"proj_bank_free{b}") for b in range(2)]
        conv0 = sem("conv_first_tap")
        conv_done = sem("conv_done")
        silu_done = sem("silu_done")
        gsq = sem("gdn_squares")
        gss = sem("gdn_square_sums")
        grn = sem("gdn_norm_factors")
        misc_ev = sem("misc_evacuated")
        row_act = sem("rows_by_scalar")
        row_dve = sem("rows_by_vector")
        rows_ready = sem("rows_ready")
        gbc = sem("gate_broadcast")
        tok_ps = sem("token_scalars_in_psum")
        tok_ready = sem("token_scalars_ready")
        egam = sem("exp_gamma_ready")
        gpre = sem("gdn_operands_ready")
        knbd = sem("kn_blocks_ready")
        vbd_ready = sem("v_blocks_ready")
        dt_arg = sem("decay_argument")
        dt_ready = sem("decay_ready")
        gkk = sem("gdn_kk_kq_ktok")
        gvt = sem("gdn_vtok")
        cm_ready = sem("level_mask_ready")
        cm_used = sem("level_mask_used")
        m1_ps = sem("m1_in_psum")
        m1_ready = sem("m1_ready")
        m2_ps = sem("m2_in_psum")
        x_ready = sem("inverse_ready")
        yt_ps = sem("inverse_transposed")
        y_act = sem("y_half0_ready")
        y_dve = sem("y_half1_ready")
        uw_ps = sem("u_w_in_psum")
        u_ready = sem("u_ready")
        wt_ready = sem("wt_ready")
        ws_ps = sem("w_state_in_psum")
        vnew_ready = sem("v_new_ready")
        kv_ps = sem("k_v_in_psum")
        state_ready = sem("state_ready")
        o_ps = sem("gdn_o_in_psum")
        o_sq = sem("gdn_o_squared")
        o_sum = sem("gdn_o_sums")
        o_fac = sem("gdn_o_factor")
        o_norm = sem("gdn_o_normed")
        oT_ps = sem("gdn_o_transposed")
        mix_h = sem("mix_high_ready")
        mix_tmp = sem("mix_value_ready")
        mix_l = sem("mix_low_ready")
        s5_act = sem("s5_scalar_steps")
        s5_dve = sem("s5_vector_steps")
        bbd_ready = sem("s5_b_blocks_ready")
        cbd_ready = sem("s5_c_blocks_ready")
        bc_t = sem("s5_bc_transposed")
        bc_ready = sem("s5_bc_ready")
        tab_c = sem("table_cos_part")
        tab_s = sem("table_sin_part")
        bu_ps = sem("s5_bu_in_psum")
        rot_prod = sem("s5_rotated_products")
        rot_sum = sem("s5_rotated_sums")
        unrot_prod = sem("s5_unrotated_products")
        xs_ready = sem("s5_states_ready")
        y_ps = sem("s5_y_in_psum")
        yd_ready = sem("s5_y_plus_d")
        gelu_ready = sem("s5_gelu_ready")
        glu_ps = sem("glu_in_psum")
        glu_sig = sem("glu_sigmoid_ready")
        mla_sq = sem("mla_squares")
        mla_ss = sem("mla_square_sums")
        mla_rn = sem("mla_norm_factors")
        mla_n = sem("mla_normed")
        mla_ps = sem("mla_product_in_psum")
        mla_ev = sem("mla_product_used")
        krot = sem("rope_key_ready")
        kcopy = sem("rope_key_copied")
        sc_ps = sem("scores_in_psum")
        sc_max = sem("scores_max")
        p_exp = sem("prob_exp")
        p_norm = sem("prob_normed")
        pT_ps = sem("prob_transposed")
        pT_ready = sem("probT_ready")
        pv_done = sem("pv_done")
        out_done = sem("out_product_done")
        x2_ready = sem("x2_ready")
        x2_sq = sem("x2_squares")
        n2_ready = sem("norm2_ready")
        h2_t = sem("h2_transposed")
        h2_h = sem("h2_high_ready")
        h2_l = sem("h2_low_ready")
        up_done = sem("up_done")
        up_tap = sem("up_first_tap")
        up_conv = sem("up_conv_done")
        up_silu = sem("up_silu_done")
        g_ready = sem("g_ready")
        g_h = sem("g_high_ready")
        g_l = sem("g_low_ready")
        down_done = sem("down_done")
        x3_ready = sem("x3_ready")
        x3_sq = sem("x3_squares")
        y_ready = sem("out_ready")

        def C(name, w=None, lo=0, hi=P, off=0):
            w = w or dict(_CONSTS)[name]
            return const[lo:hi, CO[name] + off:CO[name] + off + w]

        ident = C("ident")
        istack = C("istack")

        w_in_v = a["w_in"][0].rearrange("(k p) n -> p k n", p=P)
        w_up_v = a["ffn_w_up"][0].rearrange("(k p) n -> p k n", p=P)
        w_out_v = a["w_out"][0].rearrange("(k p) n -> k p n", p=P)
        w_dn_v = a["ffn_w_down"][0].rearrange("(k p) n -> k p n", p=P)
        x_v = a["x"][0].rearrange("(t p) d -> t p d", p=P)
        y_v = a["out"][0].rearrange("(t p) d -> t p d", p=P)

        def wk(t, slot, w=P):
            return t[:, slot, :].rearrange("p (k n) -> p k n", k=KD)[:, :, 0:w]

        def flat4(t):
            return t.rearrange("p c i -> p (c i)")[0:4, :]

        proj_copied = sem("proj_copied")
        bd_cleared = sem("blocks_cleared")
        gkk_used = sem("gdn_kk_kq_ktok_used")
        gnormed = sem("gdn_qk_normed")
        wswap = sem("rope_columns_swapped")
        z_ready = sem("z_silu_ready")
        gout_done = sem("gdn_output_ready")
        vp_ready = sem("beta_v_ready")
        HT_BANKS = [4, 5, 2, 3, 4, 5, 2, 3]
        YT = ps[:, 2 * L:3 * L].rearrange("p (c n) -> p c n", c=NCH)
        rA, rB, rC, rD = flat4(CP["X"]), flat4(CP["M1"]), flat4(CP["VP"]), moq[0][0:4, :]

        def arrived(n):
            extra = 16 * (len(PROJ[PN["misc"]][1]) - 1) if n % RAW == PN["misc"] % RAW and n >= PN["misc"] else 0
            return w_loaded[n % RAW], 16 * (n // RAW + 1) + extra

        EXTRA = [16 * (len(PROJ[PN["misc"]][1]) - 1) if r == PN["misc"] % RAW else 0 for r in range(RAW)]

        CONV_TILES = [PN[f"{t}{p}"] for p in range(PAIRS) for t in "qkv"]
        freed_by = {}
        for n in range(NPROJ):
            if n in CONV_TILES:
                freed_by[n] = (conv_done, sum(c <= n for c in CONV_TILES))
            else:
                freed_by[n] = (proj_copied, sum(m <= n and m not in CONV_TILES for m in range(NPROJ)))

        def blocks(t, c):
            return t[:, c].rearrange("p a i -> p (a i)")

        def flat(t):
            return t.rearrange("p c i -> p (c i)")

        ORDER = [("proj", PN["q0"]), ("proj", PN["k0"]), ("table", 0), ("proj", PN["v0"]), ("proj", PN["misc"]),
                 ("silu", 0), ("gnorm", 0), ("rows", 0), ("proj", PN["u0"]), ("gates", 0), ("table", 1),
                 ("proj", PN["u1"]), ("gkk", 0), ("table", 2), ("bu", 0)]
        late = list(range(PN["q1"], NPROJ))
        steps = []
        for p in range(PAIRS):
            if p:
                steps += [("silu", 1), ("gnorm", 1), ("gates", 1), ("gkk", 1)]
            steps += [("ginv", (p, l)) for l in range(6)] + [("guw", p)]
            steps += [("grec", (p, c)) for c in range(NCH)] + [("gout", p)]
        s5_steps = [("scan", 0)] + [step for s in range(1, ST) for step in (("bu", s), ("scan", s))]
        n_s5 = 0
        for m, step in enumerate(steps):
            ORDER.append(step)
            if m % 2 == 0 and late:
                ORDER.append(("proj", late.pop(0)))
            if m % 2 == 1 and n_s5 < len(s5_steps):
                ORDER.append(s5_steps[n_s5])
                n_s5 += 1
        ORDER += [("proj", n) for n in late] + s5_steps[n_s5:]
        ORDER = [s for s in ORDER if s[0] != "gout"]
        at0 = ORDER.index(("gnorm", 1))
        ORDER.insert(at0, ("gout", 0))
        ORDER += [("gout", 1), ("glu", 0), ("gmix", 0), ("mla", 0), ("attend", 0)]

        MLA_BANKS = [5, 6, 7, 2, 3, 4, 5, 6]

        def head_of(u):
            return u // 16, (u // 4) % 4, u % 4

        UNITS = 32
        SCALE = (HD ** -0.5, MLA_QK ** -0.5)

        def mix_bank(u):
            return [4, 0][(u // 8) % 2]

        s_ldt = sem("log_dt_loaded")
        ldt_rows = sem("log_dt_rows_ready")
        up_mid = sem("up_second_tap")
        VROW_DMAS = 17
        wtmp = arena[:, spans["work0"][0]:spans["work0"][0] + 4 * L]

        block = ctx.enter_context(nc.Block())

        @block.sync
        def _(sp):
            for t in range(TT):
                sp.dma_start(x_sb[:, t, :], x_v[t]).then_inc(s_x[t], 16)

            def load(n, r, dst, src):
                if n is not None and not (isinstance(n, int) and n < RAW):
                    sp.wait_ge(w_l, n - RAW + 1)
                sp.dma_start(dst, src).then_inc(w_loaded[r], 16)

            def load_proj(n):
                r = n % RAW
                for m, (at, col, width) in enumerate(PROJ[n][1]):
                    load(n if m == 0 else None, r, wk(w_raw, r)[:, :, at:at + width],
                         w_in_v[:, :, col:col + width])

            def load_out(k):
                load(N_OUT0 + k, (N_OUT0 + k) % RAW, w_raw[:, (N_OUT0 + k) % RAW, :], w_out_v[k])

            def load_up(i, b, e):
                load(N_UP0 + 4 * i + 2 * b + e, e, wk(w_raw, e),
                     w_up_v[:, :, bass.ds((2 * i + b) * P + e * DFF, P)])

            def load_down(k, r):
                load(N_DOWN0 + k, r, w_raw[:, r, :], w_dn_v[k])

            for n in range(2):
                load_proj(n)
            sp.wait_ge(vclear, 2)
            for n in range(2, NPROJ):
                load_proj(n)
                if n == PN["u0"]:
                    sp.dma_start(gluw, a["s5_glu_w"][0].rearrange("(k p) n -> p k n", p=P)).then_inc(s_glu, 16)
            for k in range(4):
                load_out(k)
            sp.wait_ge(unrot_prod, ST)
            for t in range(TT):
                sp.dma_start(x_sb[:, t, :], x_v[t]).then_inc(s_xre, 16)
            sp.wait_ge(oT_ps, PAIRS)
            uq_v = a["mla_w_uq"][0].rearrange("r (h n) -> r h n", h=H)
            for k, r0, r1 in ((0, 0, P), (1, P, QLORA)):
                for c0, c1 in ((0, HD), (HD, MLA_QK)):
                    sp.dma_start(wuq[0:r1 - r0, k, H * c0:H * c1].rearrange("p (h n) -> p h n", h=H),
                                 uq_v[r0:r1, :, c0:c1]).then_inc(s_mlaw, 16)
            ukv_v = a["mla_w_ukv"][0].rearrange("r (h n) -> r h n", h=H)
            for c in range(2):
                sp.dma_start(wukv[:, 256 * c:256 * c + 256].rearrange("p (h n) -> p h n", h=H),
                             ukv_v[:, :, HD * c:HD * c + HD]).then_inc(s_mlaw, 16)
            for k in range(4, KD):
                load_out(k)
            for b in range(2):
                for e in range(2):
                    load_up(0, b, e)
            sp.wait_ge(w_used, N_UP0)
            sp.dma_start(fing, a["final_norm_g"].rearrange("(a n) -> a n", a=1).broadcast_to([P, D])).then_inc(s_fing, 16)
            with sp.Fori(1, JF // 2) as i:
                for b in range(2):
                    for e in range(2):
                        load_up(i, b, e)
            with sp.Fori(0, 5) as i:
                for b in range(4):
                    load_down(4 * i + b, b % 2)
            for k in range(20, JF):
                load_down(k, k % 2)
            for t in range(TT):
                sp.wait_ge(y_ready, t + 1)
                sp.dma_start(y_v[t], x_sb[:, t, :]).then_inc(s_store, 16)
            sp.wait_ge(s_store, 16 * TT)

        def rotated_sum(pool, s):
            pool.wait_ge(rot_prod, s + 1)
            if s:
                pool.wait_ge(y_ps, s)
            pool.tensor_tensor(work[4], work[0], work[1], ALU.add).then_inc(rot_sum, 1)
            pool.tensor_tensor(work[5], work[2], work[3], ALU.subtract).then_inc(rot_sum, 1)

        @block.gpsimd
        def _(pool):
            pool.memset(vrows[:], 0.0).then_inc(vclear, 1)
            pool.memset(taps_rows[:], 0.0).then_inc(vclear, 1)
            pool.memset(rows, 0.0).then_inc(cleared, 1)
            pool.memset(fixed[:, 0:1], EPS).then_inc(cleared, 1)
            pool.memset(fixed[:, 1:2], math.log(HD ** -0.5)).then_inc(cleared, 1)
            pool.memset(fixed[:, 2:3], 1.0).then_inc(cleared, 1)

            def low(n, r, s):
                pool.wait_ge(w_h, n + 1)
                pool.tensor_tensor(w_lo[:, s, :], w_raw[:, r, :], w_hi[:, s, :].bitcast(F32),
                                   ALU.subtract).then_inc(w_l, 1)

            def low_at(n):
                low(n, n % RAW, n % RING)

            pool.wait_ge(cleared, 4)
            pool.wait_ge(s_ldt, 16)
            pool.tensor_scalar(vrows[V_LDT:V_LDT + 8, :].rearrange("s (g n) -> s g n", g=2),
                               ldt[V_LDT:V_LDT + 8, :].unsqueeze(2).broadcast_to([ST, 2, NS]), 1.0, 0.0,
                               ALU.mult, ALU.add).then_inc(ldt_rows, 1)
            pool.wait_ge(ldt_rows, 1)
            for n in range(3):
                low_at(n)
            nxt = 3

            def v_blocks(p):
                pool.wait_ge(silu_done, 3 * (p + 1))
                if p:
                    pool.wait_ge(uw_ps, p)
                vv = gv[p].rearrange("p (c i) -> p c i", c=NCH)
                pool.wait_ge(bd_cleared, 1)
                for e in range(2):
                    pool.tensor_scalar(BD["Y"][64 * e:64 * e + 64, :, e, :], vv[64 * e:64 * e + 64], 1.0, 0.0,
                                       ALU.mult, ALU.add).then_inc(vbd_ready, 1)
                    pool.wait_ge(vbd_ready, 2 * p + e + 1)

            for step, arg in ORDER:
                if step == "proj":
                    if nxt < N_OUT0 + 4:
                        low_at(nxt)
                        nxt += 1
                elif step == "gates":
                    v_blocks(arg)
                elif step == "ginv":
                    p, l = arg
                    m = 6 * p + l
                    pool.wait_ge(gkk_used, 4 * p + 2)
                    if m:
                        pool.wait_ge(m1_ps, m)
                    mask = C("level", 64, off=64 * l)
                    for e in range(2):
                        pool.tensor_tensor(BD["CM"][64 * e:64 * e + 64, :, e, :], CP["LT"][64 * e:64 * e + 64],
                                           mask[64 * e:64 * e + 64].unsqueeze(1).broadcast_to([64, NCH, CH]),
                                           ALU.mult).then_inc(cm_ready, 1)
                        pool.wait_ge(cm_ready, 2 * m + e + 1)
                elif step == "bu":
                    rotated_sum(pool, arg)
                elif step == "scan":
                    s = arg
                    pool.wait_ge(unrot_prod, s + 1)
                    pool.tensor_tensor(work[4], work[0], work[1], ALU.subtract).then_inc(xs_ready, 1)
                    pool.tensor_tensor(work[5], work[2], work[3], ALU.add).then_inc(xs_ready, 1)
            for n in range(nxt, N_UP0):
                low_at(n)
            with pool.Fori(0, JF // 2) as i:
                for b in range(2):
                    for e in range(2):
                        low(N_UP0 + 4 * i + 2 * b + e, e, 2 * b + e)
            with pool.Fori(0, 5) as i:
                for b in range(4):
                    low(N_DOWN0 + 4 * i + b, b % 2, b)
            for k in range(20, JF):
                low(N_DOWN0 + k, k % 2, k % 4)

        @block.scalar
        def _(act):
            chain = [0]

            def link(ins):
                chain[0] += 1
                ins.then_inc(act_step, 1)
                act.wait_ge(act_step, chain[0])

            act.dma_start(const[:], a["constants"]).then_inc(s_const, 16)
            act.wait_ge(vclear, 1)

            def row(r0, rows_n, src, c0=0, w=P):
                act.dma_start(vrows[r0:r0 + rows_n, c0:c0 + w], src).then_inc(s_vrows, 16)

            row(V_N1, 8, a["norm1_g"][0].rearrange("(k p) -> k p", p=P))
            row(V_N2, 8, a["norm2_g"][0].rearrange("(k p) -> k p", p=P))
            for t in range(4):
                row(V_CONV + 6 * t, 6, a["gdn_conv_w"][0, t].rearrange("(k p) -> k p", p=P))
            row(V_QN, 1, a["mla_q_norm_g"][:, 0:P])
            row(V_QN + 1, 1, a["mla_q_norm_g"][:, P:QLORA], w=QLORA - P)
            row(V_KVN, 1, a["mla_kv_norm_g"])
            row(V_GLUB, 2, a["s5_glu_b"][0].rearrange("(k p) -> k p", p=P))
            row(V_SD, 2, a["s5_d"][0].rearrange("(k g) c -> k (g c)", k=2))
            row(V_GN, 1, a["gdn_norm_g"], w=HD)
            row(V_GN, 1, a["gdn_norm_g"], c0=HD, w=HD)
            row(V_LRE, 8, a["s5_lam_re"][0].rearrange("(s g) n -> s (g n)", s=ST))
            row(V_LIM, 8, a["s5_lam_im"][0].rearrange("(s g) n -> s (g n)", s=ST))
            act.dma_start(ldt[V_LDT:V_LDT + 8, :], a["s5_log_dt"][0].rearrange("(s g) -> s g", s=ST)).then_inc(s_ldt, 16)
            row(V_DTB, 1, a["gdn_dt_bias"], c0=64, w=H)
            row(V_ALOG, 1, a["gdn_a_log"], w=H)
            act.wait_ge(vclear, 2)
            act.dma_start(taps_rows[0:88, 0, :], a["ffn_conv_w"][0, 0:2].rearrange("t (k p) -> (t k) p", p=P)).then_inc(s_taps, 16)
            act.dma_start(taps_rows[0:44, 1, :], a["ffn_conv_w"][0, 2].rearrange("(k p) -> k p", p=P)).then_inc(s_taps, 16)
            for r, name in enumerate(("s5_b_re", "s5_b_im")):
                act.dma_start(b_nat[:, r], a[name][0].rearrange("(s g) n c -> (g n) s c", s=ST)).then_inc(s_s5in, 16)
            for r, name in enumerate(("s5_c_re", "s5_c_im")):
                act.dma_start(c_nat[:, r], a[name][0].rearrange("(f g) c n -> (g c) f n", f=2)).then_inc(s_s5in, 16)

            act.wait_ge(s_const, 16)
            for t in range(TT):
                act.wait_ge(s_x[t], 16)
                link(act.activation(ps[:, 0:D], x_sb[:, t, :], ACT.Square, accum_out=small[:, t:t + 1]))
            act.wait_ge(cleared, 4)
            link(act.activation(small[:, 4:8], small[:, 0:4], ACT.Ln, scale=1.0 / D, bias=fixed[:, 0:1]))
            act.activation(small[:, 4:8], small[:, 4:8], ACT.Exp, scale=-0.5).then_inc(xsq, 1)

            def high(n, r, s, where=None):
                sem_, val = where or arrived(n)
                act.wait_ge(sem_, val)
                if not (isinstance(n, int) and n < RING):
                    act.wait_ge(w_used, n - RING + 1)
                act.activation(w_hi[:, s, :], w_raw[:, r, :], ACT.Copy).then_inc(w_h, 1)

            def high_at(n):
                high(n, n % RAW, n % RING)

            high_at(0)
            high_at(1)
            act.activation(ident16[:], ident, ACT.Copy).then_inc(masks16, 1)
            act.activation(causal16[:], C("causal"), ACT.Copy).then_inc(masks16, 1)
            act.wait_ge(vec_r, 1)
            for k in range(KD):
                act.wait_ge(hT_t, k + 1)
                act.activation(hT_hi[:, k, :], bank(HT_BANKS[k]), ACT.Copy,
                               scale=vec[:, V_N1 + k:V_N1 + k + 1]).then_inc(hT_h, 1)
            high_at(2)
            S = lambda k: s5p[:, k, :]
            act.activation(S(2), vec[:, V_LDT:V_LDT + 8], ACT.Exp).then_inc(s5_act, 1)
            act.wait_ge(s5_dve, 1)
            act.activation(S(9), S(3), ACT.Exp).then_inc(s5_act, 1)
            act.wait_ge(s5_dve, 2)
            act.activation(S(7), S(6), ACT.Sin).then_inc(s5_act, 1)
            act.activation(S(8), S(16), ACT.Sin).then_inc(s5_act, 1)
            def mix_high(pr):
                act.wait_ge(pv_done, 8 * (pr + 1))
                act.activation(hT_hi[:, 2 + pr, :], bank([4, 0][pr % 2]), ACT.Copy).then_inc(mix_h, 1)

            nxt = 3
            COPY_TO = {"u0": su[0], "u1": su[1], "z0": gz[0], "z1": gz[1], "cq0": cq[0], "cq1": cq[1], "ckv": ckv,
                       "mq0": moq[0], "mq1": moq[1], "mk0": mok[0], "mk1": mok[1], "misc": misc}
            n_conv = 0
            for step, arg in ORDER:
                if step == "proj":
                    n = arg
                    name = PROJ[n][0]
                    act.wait_ge(w_used, n + 1)
                    if n in CONV_TILES:
                        p, j = int(name[1]), "qkv".index(name[0])
                        dst = (gq, gk, gv)[j][p]
                        col = V_CONV + 6 * 3 + 2 * j + p
                        act.activation(dst, bank(n % 2), ACT.Copy, scale=vec[:, col:col + 1]).then_inc(conv0, 1)
                    elif name.startswith("mv"):
                        p = int(name[2])
                        act.activation(mov[:, :, P * p:P * p + P], bank(n % 2).rearrange("p (t n) -> p t n", t=TT),
                                       ACT.Copy).then_inc(proj_copied, 1)
                    else:
                        act.activation(COPY_TO[name], bank(n % 2), ACT.Copy).then_inc(proj_copied, 1)
                    if nxt < N_OUT0 + 4:
                        high_at(nxt)
                        nxt += 1
                elif step == "table" and arg == 0:
                    act.wait_ge(bc_t, 1)
                    act.activation(bt.rearrange("p r f n -> p (r f n)"), bank(6), ACT.Copy).then_inc(bc_ready, 1)
                    act.wait_ge(bc_t, 2)
                    act.activation(ct[:, 0].rearrange("p s n -> p (s n)"), bank(7, 256), ACT.Copy).then_inc(bc_ready, 1)
                    act.activation(ct[:, 1].rearrange("p s n -> p (s n)"), ps[:, 7 * L + 256:8 * L], ACT.Copy,
                                   scale=-1.0).then_inc(bc_ready, 1)
                elif step == "silu":
                    p = arg
                    for j, t in enumerate((gq[p], gk[p], gv[p])):
                        act.wait_ge(conv_done, 3 * p + j + 1)
                        act.activation(t, t, ACT.Silu).then_inc(silu_done, 1)
                elif step == "gnorm":
                    p = arg
                    act.wait_ge(silu_done, 3 * (p + 1))
                    if p:
                        act.wait_ge(x_ready, 6 * p)
                        act.wait_ge(cm_ready, 12 * p)
                    act.activation(flat(CP["DT"]), gq[p], ACT.Square).then_inc(gsq, 1)
                    act.activation(flat(CP["LT"]), gk[p], ACT.Square).then_inc(gsq, 1)
                    act.wait_ge(gss, 2 * p + 1)
                    link(act.activation(flat(CP["DT"]), bank(2), ACT.Ln, bias=fixed[:, 0:1]))
                    act.wait_ge(gss, 2 * p + 2)
                    link(act.activation(flat(CP["LT"]), bank(3), ACT.Ln, bias=fixed[:, 0:1]))
                    act.activation(flat(CP["DT"]), flat(CP["DT"]), ACT.Exp, scale=-0.5,
                                   bias=fixed[:, 1:2]).then_inc(grn, 1)
                    act.activation(flat(CP["LT"]), flat(CP["LT"]), ACT.Exp, scale=-0.5).then_inc(grn, 1)
                elif step == "rows":
                    act.wait_ge(proj_copied, freed_by[PN["misc"]][1])
                    act.activation(rA, misc[64:68, :], ACT.Identity, bias=vec[64:68, V_DTB:V_DTB + 1]).then_inc(row_act, 1)
                    act.activation(rC, misc[96:100, :], ACT.Tanh, scale=0.5).then_inc(row_act, 1)
                    act.activation(small[0:4, 0:1], vec[0:4, V_ALOG:V_ALOG + 1], ACT.Exp).then_inc(row_act, 1)
                    act.wait_ge(row_act, 1)
                    link(act.activation(rB, rA, ACT.Abs))
                    link(act.activation(rB, rB, ACT.Exp, scale=-1.0))
                    act.activation(rB, rB, ACT.Ln, bias=fixed[0:4, 2:3]).then_inc(row_act, 1)
                    act.wait_ge(row_dve, 2)
                    act.activation(rB, rows[0:4, :], ACT.Exp).then_inc(row_act, 1)
                    act.activation(rows[96:100, :], rD, ACT.Exp).then_inc(row_act, 1)
                elif step == "gates":
                    p = arg
                    act.wait_ge(gbc, 2 * p + 1)
                    act.activation(flat(CP["M1"]), bank(2), ACT.Exp).then_inc(egam, 1)
                    act.activation(glast, bank(2).rearrange("p (c i) -> p c i", c=NCH)[:, :, CH - 1], ACT.Exp).then_inc(egam, 1)
                    act.wait_ge(gnormed, 2 * p + 2)
                    kk = gk[p].rearrange("p (c i) -> p c i", c=NCH)
                    act.wait_ge(bd_cleared, 1)
                    if p:
                        act.wait_ge(o_ps, NCH * p)
                    for e in range(2):
                        act.activation(BD["KN"][64 * e:64 * e + 64, :, e, :], kk[64 * e:64 * e + 64], ACT.Copy).then_inc(knbd, 1)
                    act.wait_ge(dt_arg, p + 1)
                    act.activation(flat(CP["DT"]), flat(CP["DT"]), ACT.Exp).then_inc(dt_ready, 1)
                elif step == "ginv":
                    p, l = arg
                    m = 6 * p + l
                    if l:
                        act.wait_ge(m1_ps, m + 1)
                        act.activation(flat(CP["M1"]), bank(4), ACT.Copy).then_inc(m1_ready, 1)
                    act.wait_ge(yt_ps, m + 1)
                    act.activation(BD["Y"][0:64, :, 0, :], YT[0:64], ACT.Copy).then_inc(y_act, 1)
                elif step == "guw":
                    p = arg
                    act.wait_ge(uw_ps, p + 1)
                    act.activation(flat(CP["VP"]), bank(4), ACT.Copy).then_inc(u_ready, 1)
                    act.activation(BD["KN"].rearrange("p c a i -> p (c a i)"), ps[:, 2 * L:4 * L], ACT.Copy).then_inc(wt_ready, 1)
                elif step == "gout":
                    p = arg
                    if p == 0:
                        for z in range(PAIRS):
                            act.wait_ge(proj_copied, freed_by[PN[f"z{z}"]][1])
                            act.activation(gz[z], gz[z], ACT.Silu).then_inc(z_ready, 1)
                    act.wait_ge(o_ps, NCH * (p + 1))
                    act.activation(flat(CP["M1"]), bank(2), ACT.Square).then_inc(o_sq, 1)
                    act.wait_ge(o_sum, p + 1)
                    link(act.activation(onorm[:, 1], onorm[:, 0], ACT.Ln, scale=1.0 / HD, bias=fixed[:, 0:1]))
                    act.activation(onorm[:, 1], onorm[:, 1], ACT.Exp, scale=-0.5).then_inc(o_fac, 1)
                elif step == "glu":
                    for f in range(2):
                        act.wait_ge(yd_ready, f + 1)
                        act.activation(su[f], su[f], ACT.Gelu_apprx_tanh).then_inc(gelu_ready, 1)
                    for f in range(2):
                        act.wait_ge(glu_ps, f + 1)
                        act.activation(work[f].rearrange("p h t -> p (h t)"), bank(5 + f), ACT.Sigmoid,
                                       bias=vec[:, V_GLUB + f:V_GLUB + f + 1]).then_inc(glu_sig, 1)
                    act.wait_ge(w_used, NPROJ)
                    for f in range(2):
                        act.wait_ge(mix_tmp, f + 1)
                        act.activation(hT_hi[:, 6 + f, :], su[f], ACT.Copy).then_inc(mix_h, 1)
                elif step == "gmix":
                    for p in range(PAIRS):
                        act.wait_ge(gout_done, p + 1)
                        act.activation(hT_hi[:, p, :], gz[p], ACT.Copy).then_inc(mix_h, 1)
                elif step == "mla":
                    act.wait_ge(oT_ps, PAIRS)
                    act.activation(mrs[0], cq[0], ACT.Square).then_inc(mla_sq, 1)
                    act.activation(mrs[1][0:64], cq[1][0:64], ACT.Square).then_inc(mla_sq, 1)
                    act.activation(rope1, ckv, ACT.Square).then_inc(mla_sq, 1)
                    act.wait_ge(mla_ss, 1)
                    link(act.activation(mrs[0], bank(5), ACT.Ln, scale=1.0 / QLORA, bias=fixed[:, 0:1]))
                    act.wait_ge(mla_ss, 2)
                    link(act.activation(mrs[1], bank(6), ACT.Ln, scale=1.0 / KVLORA, bias=fixed[:, 0:1]))
                    act.activation(mrs[0], mrs[0], ACT.Exp, scale=-0.5).then_inc(mla_rn, 1)
                    act.activation(mrs[1], mrs[1], ACT.Exp, scale=-0.5).then_inc(mla_rn, 1)
                    act.wait_ge(s_mlaw, 96)
                    for k, kr in ((0, P), (1, 64)):
                        w4 = wuq[0:kr, k, H * HD:H * MLA_QK].rearrange("p (h n) -> p h n", h=H)
                        sw = wuq[0:kr, k, H * MLA_QK:].rearrange("p (h n) -> p h n", h=H)
                        act.activation(sw[:, :, 0:16], w4[:, :, 16:32], ACT.Copy).then_inc(wswap, 1)
                        act.activation(sw[:, :, 16:32], w4[:, :, 0:16], ACT.Copy).then_inc(wswap, 1)
                    for m, (dst, pair) in enumerate(((q96, 0), (q96, 1), (k96, 0), (k96, 1))):
                        act.wait_ge(mla_ps, (1, 2, 5, 6)[m])
                        b = MLA_BANKS[(0, 1, 4, 5)[m]]
                        act.activation(dst[0:64, 2 * pair, :], bank(b)[0:64], ACT.Copy).then_inc(mla_ev, 1)
                        act.activation(dst[0:64, 2 * pair + 1, :], bank(b)[64:128], ACT.Copy).then_inc(mla_ev, 1)
                    for m in range(2):
                        act.wait_ge(mla_ps, 7 + m)
                        act.activation(mlav[:, 2 * m:2 * m + 2, :].rearrange("p t n -> p (t n)"), bank(MLA_BANKS[6 + m]),
                                       ACT.Copy).then_inc(mla_ev, 1)
                    act.wait_ge(krot, 1)
                    for h in range(1, H):
                        act.activation(k96[64:96, h, :], k96[64:96, 0, :], ACT.Copy).then_inc(kcopy, 1)
                elif step == "attend":
                    def expo(u):
                        m, h, t = head_of(u)
                        act.wait_ge(sc_max, u + 1)
                        if u >= 2:
                            act.wait_ge(pT_ps, u - 1)
                        act.activation(prob[u % 2][:, 0:P * (t + 1)], bank(5 + u % 3, P * (t + 1)), ACT.Exp,
                                       bias=smx[:, 1, u:u + 1], scale=SCALE[m],
                                       accum_out=smx[:, 2, u:u + 1]).then_inc(p_exp, 1)

                    expo(0)
                    for u in range(UNITS):
                        if u + 1 < UNITS:
                            expo(u + 1)
                        m, h, t = head_of(u)
                        act.wait_ge(pT_ps, u + 1)
                        if u >= 2:
                            act.wait_ge(pv_done, u - 1)
                        act.activation(probT[u % 2][:, 0:t + 1, :].rearrange("p k q -> p (k q)"),
                                       bank(2 + u % 2, P * (t + 1)), ACT.Copy).then_inc(pT_ready, 1)
                        if u % 8 == 0 and u:
                            mix_high(u // 8 - 1)
                    mix_high(3)

            for n in range(nxt, N_UP0):
                high_at(n)

            def up_split(i, b):
                for e in range(2):
                    n = N_UP0 + 4 * i + 2 * b + e
                    high(n, e, 2 * b + e, (w_loaded[e], 16 * (N_UP0 // 2 + 2 * i + b + 1) + EXTRA[e]))

            up_split(0, 0)
            for t in range(TT):
                act.wait_ge(x2_ready, t + 1)
                act.activation(junk, x_sb[:, t, :], ACT.Square, accum_out=stat[:, t:t + 1]).then_inc(x2_sq, 1)
                act.wait_ge(x2_sq, t + 1)
            link(act.activation(stat[:, 4:8], stat[:, 0:4], ACT.Ln, scale=1.0 / D, bias=fixed[:, 0:1]))
            act.activation(stat[:, 4:8], stat[:, 4:8], ACT.Exp, scale=-0.5).then_inc(x2_sq, 1)
            for k in range(KD):
                act.wait_ge(h2_t, k + 1)
                act.activation(hT_hi[:, k, :], bank(k), ACT.Copy, scale=vec[:, V_N2 + k:V_N2 + k + 1]).then_inc(h2_h, 1)

            def up_evac(i, b):
                j = 2 * i + b
                act.wait_ge(w_used, N_UP0 + 2 * j + 2)
                if not (isinstance(j, int) and j < 2):
                    act.wait_ge(g_ready, j - 1)
                for e in range(2):
                    act.activation(conv[2 * b + e], bank(2 * b + e), ACT.Copy,
                                   scale=taps[:, 2, e * JF + j, :]).then_inc(up_tap, 1)
                act.wait_ge(up_conv, 2 * j + 1)
                act.activation(conv[2 * b], conv[2 * b], ACT.Silu).then_inc(up_silu, 1)

            act.preload_act_table(ACT.Silu)
            up_split(0, 1)
            up_evac(0, 0)
            up_split(1, 0)
            up_evac(0, 1)
            up_split(1, 1)
            up_evac(1, 0)
            with act.Fori(2, JF // 2) as i:
                up_split(i, 0)
                up_evac(i - 1, 1)
                up_split(i, 1)
                up_evac(i, 0)

            def g_high(k, s):
                act.activation(hT_hi[:, s, :], g_sb[:, k, :], ACT.Copy).then_inc(g_h, 1)

            for k in range(2):
                high(N_DOWN0 + k, k, k, (w_loaded[k], 16 * (N_DOWN0 // 2 + 1) + EXTRA[k]))
            up_evac(JF // 2 - 1, 1)
            act.wait_ge(w_used, N_DOWN0)
            for k in range(4):
                if k == 0:
                    act.wait_ge(g_ready, JF)
                g_high(k, k)
                if k >= 2:
                    high(N_DOWN0 + k, k % 2, k, (w_loaded[k % 2], 16 * (N_DOWN0 // 2 + k // 2 + 1) + EXTRA[k % 2]))
            with act.Fori(1, 5) as i:
                for b in range(4):
                    act.wait_ge(w_used, N_DOWN0 + 4 * i + b - RING + 1)
                    g_high(4 * i + b, b)
                    high(N_DOWN0 + 4 * i + b, b % 2, b,
                         (w_loaded[b % 2], 16 * (N_DOWN0 // 2 + 2 * i + b // 2 + 1) + EXTRA[b % 2]))
            for k in range(20, JF):
                act.wait_ge(w_used, N_DOWN0 + k - RING + 1)
                g_high(k, k % 4)
                high(N_DOWN0 + k, k % 2, k % 4, (w_loaded[k % 2], 16 * (N_DOWN0 // 2 + k // 2 + 1) + EXTRA[k % 2]))
            for t in range(TT):
                act.wait_ge(x3_ready, t + 1)
                act.activation(junk, x_sb[:, t, :], ACT.Square, accum_out=stat[:, 8 + t:9 + t]).then_inc(x3_sq, 1)
                act.wait_ge(x3_sq, 2 * t + 1)
                link(act.activation(stat[:, 12 + t:13 + t], stat[:, 8 + t:9 + t], ACT.Ln, scale=1.0 / D, bias=fixed[:, 0:1]))
                act.activation(stat[:, 12 + t:13 + t], stat[:, 12 + t:13 + t], ACT.Exp, scale=-0.5).then_inc(x3_sq, 1)

        @block.vector
        def _(dve):
            chain = [0]

            def link(ins):
                chain[0] += 1
                ins.then_inc(dve_step, 1)
                dve.wait_ge(dve_step, chain[0])

            S = lambda k: s5p[:, k, :]
            for m, n in enumerate(bd_names):
                ins = dve.memset(BD[n].rearrange("p c a i -> p (c a i)"), 0.0)
            ins.then_inc(bd_cleared, 1)

            dve.wait_ge(vec_t, 1)
            dve.tensor_copy(vec[:], bank(2, V_ROWS)).then_inc(vec_r, 1)
            dve.wait_ge(vec_t, 3)
            dve.tensor_copy(taps[:].rearrange("p t j a -> p (t j a)"), bank(3, 6 * JF)).then_inc(vec_r, 1)
            dve.wait_ge(xsq, 1)
            for t in range(TT):
                dve.tensor_scalar(x_sb[:, t, :], x_sb[:, t, :], small[:, 4 + t:5 + t], None, ALU.mult).then_inc(xn, 1)
            dve.wait_ge(vec_r, 1)

            for k in range(KD):
                dve.wait_ge(hT_h, k + 1)
                dve.scalar_tensor_tensor(hT_lo[:, k, :], bank(HT_BANKS[k]), vec[:, V_N1 + k:V_N1 + k + 1],
                                         hT_hi[:, k, :].bitcast(F32), ALU.mult, ALU.subtract).then_inc(hT_l, 1)

            dve.tensor_scalar(S(0), vec[:, V_LRE:V_LRE + 8], -1e-4, None, ALU.min)
            link(dve.tensor_copy(S(1), vec[:, V_LIM:V_LIM + 8]))
            dve.wait_ge(s5_act, 1)
            dve.tensor_tensor(S(3), S(0), S(2), ALU.mult).then_inc(s5_dve, 1)
            link(dve.tensor_tensor(S(4), S(1), S(2), ALU.mult))
            link(dve.tensor_scalar(S(5), S(4), 1.0 / (2.0 * math.pi), ROUND, ALU.mult, ALU.add))
            link(dve.tensor_scalar(S(5), S(5), ROUND, None, ALU.subtract))
            src = S(4)
            for part in TWO_PI:
                link(dve.scalar_tensor_tensor(S(6), S(5), -part, src, ALU.mult, ALU.add))
                src = S(6)
            link(dve.tensor_scalar(S(6), S(6), math.pi, -math.pi, ALU.min, ALU.max))
            link(dve.scalar_tensor_tensor(S(16), S(6), -1.0, S(6), ALU.mult, ALU.max))
            dve.tensor_scalar(S(16), S(16), -1.0, math.pi / 2, ALU.mult, ALU.add).then_inc(s5_dve, 1)
            link(dve.tensor_tensor(S(12), S(0), S(0), ALU.mult))
            link(dve.tensor_tensor(S(13), S(1), S(1), ALU.mult))
            link(dve.tensor_tensor(S(12), S(12), S(13), ALU.add))
            link(dve.reciprocal(S(13), S(12)))
            dve.wait_ge(s5_act, 4)
            link(dve.tensor_tensor(S(10), S(9), S(8), ALU.mult))
            link(dve.tensor_tensor(S(11), S(9), S(7), ALU.mult))
            link(dve.tensor_scalar(S(10), S(10), 1.0, None, ALU.subtract))
            dve.tensor_tensor(S(14), S(10), S(0), ALU.mult)
            dve.tensor_tensor(S(17), S(11), S(1), ALU.mult)
            dve.tensor_tensor(S(15), S(11), S(0), ALU.mult)
            link(dve.tensor_tensor(S(18), S(10), S(1), ALU.mult))
            dve.tensor_tensor(S(14), S(14), S(17), ALU.add)
            link(dve.tensor_tensor(S(15), S(15), S(18), ALU.subtract))
            dve.tensor_tensor(S(14), S(14), S(13), ALU.mult)
            link(dve.tensor_tensor(S(15), S(15), S(13), ALU.mult))
            cr = S(14).unsqueeze(2).broadcast_to([P, ST, GW])
            ci = S(15).unsqueeze(2).broadcast_to([P, ST, GW])
            dve.wait_ge(s_s5in, 64)
            dve.tensor_tensor(bbar[:, 0], b_nat[:, 0], cr, ALU.mult)
            link(dve.tensor_tensor(btmp, b_nat[:, 1], ci, ALU.mult))
            link(dve.tensor_tensor(bbar[:, 0], bbar[:, 0], btmp, ALU.subtract))
            dve.tensor_tensor(bbar[:, 1], b_nat[:, 1], cr, ALU.mult)
            link(dve.tensor_tensor(btmp, b_nat[:, 0], ci, ALU.mult))
            link(dve.tensor_tensor(bbar[:, 1], bbar[:, 1], btmp, ALU.add))
            for r in range(2):
                for g in range(2):
                    dve.tensor_scalar(bbd[:, r, :, g, :], bbar[:, r], C("bmask", 1, off=g), None,
                                      ALU.mult).then_inc(bbd_ready, 1)
            for g in range(2):
                for r in range(2):
                    dve.tensor_scalar(cbd[:, r, :, g, :], c_nat[:, r], C("cmask", 1, off=g), None,
                                      ALU.mult).then_inc(cbd_ready, 1)

            def table_level(n):
                lo = slice(0, n)
                up = slice(n, 2 * n)
                cb = cosT[:, :, n - 1:n].broadcast_to([P, ST, n])
                sb_ = sinT[:, :, n - 1:n].broadcast_to([P, ST, n])
                t1 = wtmp[:, 0:ST * n].rearrange("p (s t) -> p s t", s=ST)
                t2 = wtmp[:, ST * n:2 * ST * n].rearrange("p (s t) -> p s t", s=ST)
                dve.tensor_tensor(cosT[:, :, up], cosT[:, :, lo], cb, ALU.mult)
                dve.tensor_tensor(t1, sinT[:, :, lo], sb_, ALU.mult)
                dve.tensor_tensor(sinT[:, :, up], sinT[:, :, lo], cb, ALU.mult)
                link(dve.tensor_tensor(t2, cosT[:, :, lo], sb_, ALU.mult))
                dve.tensor_tensor(cosT[:, :, up], cosT[:, :, up], t1, ALU.subtract)
                link(dve.tensor_tensor(sinT[:, :, up], sinT[:, :, up], t2, ALU.add))

            def conv_taps(p, j, m, n):
                dst = (gq, gk, gv)[j][p]
                dve.wait_ge(conv0, m + 1)
                for tap, back in ((2, 1), (1, 2), (0, 3)):
                    col = V_CONV + 6 * tap + 2 * j + p
                    ins = dve.scalar_tensor_tensor(dst[:, back:], bank(n % 2)[:, 0:L - back], vec[:, col:col + 1],
                                                   dst[:, back:], ALU.mult, ALU.add)
                    if back < 3:
                        link(ins)
                ins.then_inc(conv_done, 1)

            def y_plus_d(f):
                dve.wait_ge(y_ps, 4 * f + 4)
                dve.scalar_tensor_tensor(su[f], su[f], vec[:, V_SD + f:V_SD + f + 1], bank(7), ALU.mult,
                                         ALU.add).then_inc(yd_ready, 1)

            def mix_low(pr):
                dve.wait_ge(mix_h, 5 + pr)
                dve.tensor_tensor(hT_lo[:, 2 + pr, :], bank([4, 0][pr % 2]), hT_hi[:, 2 + pr, :].bitcast(F32),
                                  ALU.subtract).then_inc(mix_l, 1)

            def tokc(q, p, e=None):
                v = tok if e is None else tok[64 * e:64 * e + 64]
                return v[:, :, q, p:p + 1].broadcast_to([P if e is None else 64, NCH, CH])

            def half(t, e):
                return t[64 * e:64 * e + 64]

            def ps3(b):
                return bank(b).rearrange("p (c i) -> p c i", c=NCH)

            n_conv = 0
            n_state = 0
            for step, arg in ORDER:
                if step == "proj":
                    n = arg
                    name = PROJ[n][0]
                    if n in CONV_TILES:
                        conv_taps(int(name[1]), "qkv".index(name[0]), n_conv, n)
                        n_conv += 1
                elif step == "table":
                    if arg == 0:
                        dve.wait_ge(hT_t, KD)
                        dve.wait_ge(bc_t, 2)
                        dve.tensor_copy(cosT[:, :, 0], S(8))
                        link(dve.tensor_copy(sinT[:, :, 0], S(7)))
                        for l in range(6):
                            table_level(1 << l)
                    else:
                        table_level(1 << (5 + arg))
                elif step == "rows":
                    dve.wait_ge(row_act, 4)
                    dve.wait_ge(cleared, 1)
                    link(dve.scalar_tensor_tensor(rA, rA, 0.0, rB, ALU.max, ALU.add))
                    link(dve.tensor_scalar(rA, rA, small[0:4, 0:1], -1.0, ALU.mult, ALU.mult))
                    dve.tensor_scalar(rC, rC, 0.5, 0.5, ALU.mult, ALU.add).then_inc(dve_step, 1)
                    chain[0] += 1
                    dve.tensor_tensor_scan(rows[0:4, :], C("scanmask", lo=0, hi=4), rA, 0.0, ALU.mult, ALU.add).then_inc(row_dve, 1)
                    dve.wait_ge(dve_step, chain[0])
                    dve.tensor_copy(rows[32:36, :], rC)
                    dve.wait_ge(row_dve, 1)
                    gam = rows[0:4, :].rearrange("p (c i) -> p c i", c=NCH)
                    dve.tensor_tensor(rD.rearrange("p (c i) -> p c i", c=NCH), gam[:, :, CH - 1:CH].broadcast_to([4, NCH, CH]),
                                      gam, ALU.subtract).then_inc(row_dve, 1)
                    dve.wait_ge(row_act, 5)
                    dve.tensor_tensor(rows[64:68, :], rC, rB, ALU.mult).then_inc(row_dve, 1)
                elif step == "gates":
                    p = arg
                    dve.wait_ge(grn, 2 * p + 1)
                    dve.tensor_tensor(gq[p], gq[p], flat(CP["DT"]), ALU.mult).then_inc(gnormed, 1)
                    dve.wait_ge(grn, 2 * p + 2)
                    dve.tensor_tensor(gk[p], gk[p], flat(CP["LT"]), ALU.mult).then_inc(gnormed, 1)
                    if p == 0:
                        dve.wait_ge(tok_ps, 1)
                        dve.tensor_copy(tok.rearrange("p c q r -> p (c q r)"), bank(4, 8 * NCH)).then_inc(tok_ready, 1)
                        dve.wait_ge(tok_ready, 1)
                    dve.wait_ge(egam, 2 * p + 2)
                    dve.wait_ge(gnormed, 2 * p + 2)
                    link(dve.tensor_tensor(CP["DT"], ps3(2), tokc(0, p), ALU.subtract))
                    dve.scalar_tensor_tensor(CP["DT"], CP["DT"], 0.0, C("dmask").unsqueeze(1).broadcast_to([P, NCH, CH]),
                                             ALU.min, ALU.add).then_inc(dt_arg, 1)
                    for e in range(2):
                        dve.tensor_tensor(half(BD["QD"], e)[:, :, e, :], half(gq[p], e).rearrange("p (c i) -> p c i", c=NCH),
                                          half(CP["M1"], e), ALU.mult).then_inc(dve_step, 1)
                        chain[0] += 1
                    dve.wait_ge(dve_step, chain[0])
                    dve.wait_ge(gbc, 2 * p + 2)
                    dve.tensor_tensor(flat(CP["M1"]), gk[p], bank(3), ALU.mult).then_inc(gpre, 1)
                elif step == "gkk":
                    p = arg
                    dve.wait_ge(gkk, 3 * p + 2)
                    dve.wait_ge(dt_ready, p + 1)
                    for e in range(2):
                        ins = dve.tensor_tensor(half(BD["ATT"], e)[:, :, e, :], half(ps3(3), e), half(CP["DT"], e), ALU.mult)
                    ins.then_inc(gkk_used, 1)
                    dve.tensor_tensor(CP["LT"], ps3(2), CP["DT"], ALU.mult).then_inc(gkk_used, 1)
                    dve.wait_ge(gkk, 3 * p + 3)
                    for q, n in ((2, "KW"), (3, "KD")):
                        for e in range(2):
                            ins = dve.tensor_tensor(half(BD[n], e)[:, :, e, :], half(ps3(4), e), tokc(q, p, e), ALU.mult)
                        ins.then_inc(gkk_used, 1)
                    dve.wait_ge(gvt, p + 1)
                    dve.tensor_tensor(CP["VP"], ps3(2), tokc(1, p), ALU.mult).then_inc(vp_ready, 1)
                elif step == "ginv":
                    p, l = arg
                    m = 6 * p + l
                    if l == 0:
                        dve.wait_ge(m1_ps, m + 1)
                        dve.tensor_tensor(CP["X"], istack.unsqueeze(1).broadcast_to([P, NCH, CH]), ps3(4),
                                          ALU.subtract).then_inc(x_ready, 1)
                    else:
                        dve.wait_ge(m2_ps, 5 * p + l)
                        dve.tensor_tensor(CP["X"], CP["X"], ps3(4), ALU.subtract).then_inc(x_ready, 1)
                    dve.wait_ge(yt_ps, m + 1)
                    dve.tensor_copy(BD["Y"][64:128, :, 1, :], YT[64:128]).then_inc(y_dve, 1)
                elif step == "grec":
                    p, c = arg
                    if c:
                        dve.wait_ge(ws_ps, 7 * p + c)
                        dve.wait_ge(u_ready, p + 1)
                        dve.tensor_tensor(vnew[:, c % 2, :], CP["VP"][:, c, :], bank(4, HD), ALU.subtract).then_inc(vnew_ready, 1)
                    if c < NCH - 1:
                        dve.wait_ge(kv_ps, 7 * p + c + 1)
                        kv = ps[:, 3 * L + HD * (c % 2):3 * L + HD * (c % 2) + HD]
                        if c == 0:
                            if p:
                                dve.wait_ge(o_ps, NCH * p)
                            dve.tensor_copy(state[:, 0, :], kv).then_inc(state_ready, 1)
                        else:
                            dve.wait_ge(o_ps, NCH * p + c)
                            dve.scalar_tensor_tensor(state[:, c % 2, :], state[:, 1 - c % 2, :], glast[:, c:c + 1], kv,
                                                     ALU.mult, ALU.add).then_inc(state_ready, 1)
                        n_state += 1
                        dve.wait_ge(state_ready, n_state)
                elif step == "gout":
                    p = arg
                    dve.wait_ge(o_sq, p + 1)
                    dve.reduce_sum(onorm[:, 0], CP["M1"], axis=AX.X).then_inc(o_sum, 1)
                    dve.wait_ge(o_fac, p + 1)
                    for e in range(2):
                        dve.tensor_tensor(half(BD["QD"], e)[:, :, e, :], half(ps3(2), e),
                                          half(onorm, e)[:, 1, :].unsqueeze(2).broadcast_to([64, NCH, HD]),
                                          ALU.mult).then_inc(o_norm, 1)
                    dve.wait_ge(oT_ps, p + 1)
                    dve.wait_ge(z_ready, p + 1)
                    dve.scalar_tensor_tensor(gz[p], bank(4), vec[:, V_GN:V_GN + 1], gz[p], ALU.mult,
                                             ALU.mult).then_inc(gout_done, 1)
                elif step == "bu":
                    s = arg
                    dve.wait_ge(bu_ps, s + 1)
                    if s:
                        dve.wait_ge(xs_ready, 2 * s)
                    c2 = cosT[:, s:s + 1, :].broadcast_to([P, 2, HALF])
                    s2 = sinT[:, s:s + 1, :].broadcast_to([P, 2, HALF])
                    bur = bank(5).rearrange("p (h t) -> p h t", h=2)
                    bui = bank(6).rearrange("p (h t) -> p h t", h=2)
                    dve.tensor_tensor(work[0], bur, c2, ALU.mult)
                    dve.tensor_tensor(work[1], bui, s2, ALU.mult)
                    dve.tensor_tensor(work[2], bui, c2, ALU.mult)
                    dve.tensor_tensor(work[3], bur, s2, ALU.mult).then_inc(rot_prod, 1)
                elif step == "scan":
                    s = arg
                    mag = S(9)[:, s:s + 1].broadcast_to([P, HALF])
                    for e in range(2):
                        dve.wait_ge(rot_sum, 2 * s + 1 + e)
                        dve.tensor_tensor_scan(work[6 + e][:, 0, :], mag, work[4 + e][:, 0, :], 0.0, ALU.mult, ALU.add).then_inc(dve_step, 1)
                        chain[0] += 1
                    dve.wait_ge(dve_step, chain[0])
                    ce, se = cosT[:, s, HALF - 1:HALF], sinT[:, s, HALF - 1:HALF]
                    wr, wi = work[6][:, 0, HALF - 1:HALF], work[7][:, 0, HALF - 1:HALF]
                    dve.tensor_tensor(s5c[:, 0:1], wi, se, ALU.mult)
                    link(dve.tensor_tensor(s5c[:, 1:2], wi, ce, ALU.mult))
                    dve.scalar_tensor_tensor(s5c[:, 2:3], wr, ce, s5c[:, 0:1], ALU.mult, ALU.subtract)
                    link(dve.scalar_tensor_tensor(s5c[:, 3:4], wr, se, s5c[:, 1:2], ALU.mult, ALU.add))
                    for e in range(2):
                        ins = dve.tensor_tensor_scan(work[6 + e][:, 1, :], mag, work[4 + e][:, 1, :], s5c[:, 2 + e:3 + e],
                                                     ALU.mult, ALU.add)
                    link(ins)
                    c2 = cosT[:, s:s + 1, :].broadcast_to([P, 2, HALF])
                    s2 = sinT[:, s:s + 1, :].broadcast_to([P, 2, HALF])
                    dve.tensor_tensor(work[0], work[6], c2, ALU.mult)
                    dve.tensor_tensor(work[1], work[7], s2, ALU.mult)
                    dve.tensor_tensor(work[2], work[6], s2, ALU.mult)
                    dve.tensor_tensor(work[3], work[7], c2, ALU.mult).then_inc(unrot_prod, 1)
                    if s == ST // 2:
                        y_plus_d(0)
                elif step == "glu":
                    y_plus_d(1)
                    dve.wait_ge(w_used, NPROJ)
                    dve.wait_ge(glu_ps, 2)
                    for f in range(2):
                        dve.wait_ge(glu_sig, f + 1)
                        dve.tensor_tensor(su[f], su[f], work[f].rearrange("p h t -> p (h t)"), ALU.mult).then_inc(mix_tmp, 1)
                    for f in range(2):
                        dve.wait_ge(mix_tmp, f + 1)
                        dve.wait_ge(mix_h, f + 1)
                        dve.tensor_tensor(hT_lo[:, 6 + f, :], su[f], hT_hi[:, 6 + f, :].bitcast(F32), ALU.subtract).then_inc(mix_l, 1)
                elif step == "gmix":
                    for p in range(PAIRS):
                        dve.wait_ge(gout_done, p + 1)
                        dve.wait_ge(mix_h, 3 + p)
                        dve.tensor_tensor(hT_lo[:, p, :], gz[p], hT_hi[:, p, :].bitcast(F32), ALU.subtract).then_inc(mix_l, 1)
                elif step == "mla":
                    for m, (t, g, f) in enumerate(((cq[0], V_QN, mrs[0]), (cq[1][0:64], V_QN + 1, mrs[0][0:64]), (ckv, V_KVN, mrs[1]))):
                        dve.wait_ge(mla_rn, 1 if m < 2 else 2)
                        n_ = t.shape[0]
                        dve.scalar_tensor_tensor(t, t, vec[0:n_, g:g + 1], f, ALU.mult, ALU.mult).then_inc(mla_n, 1)
                    dve.wait_ge(mla_ps, 3)
                    dve.tensor_tensor(rope1, bank(MLA_BANKS[2]), C("ropec"), ALU.mult)
                    dve.wait_ge(mla_ps, 4)
                    link(dve.tensor_tensor(rope2, bank(MLA_BANKS[3]), C("ropes"), ALU.mult))
                    for h in range(H):
                        ins = dve.tensor_tensor(q96[64:96, h, :], rope1[32 * h:32 * h + 32], rope2[32 * h:32 * h + 32], ALU.add)
                    link(ins)
                    dve.tensor_tensor(rope1[0:32], misc[0:32], C("ropec", lo=0, hi=32), ALU.mult)
                    link(dve.tensor_tensor(rope2[0:32], misc[32:64], C("ropes", lo=32, hi=64), ALU.mult))
                    dve.tensor_tensor(k96[64:96, 0, :], rope1[0:32], rope2[0:32], ALU.add).then_inc(krot, 1)
                elif step == "attend":
                    def maxi(u):
                        m, h, t = head_of(u)
                        dve.wait_ge(sc_ps, u + 1)
                        link(dve.reduce_max(smx[:, 0, u:u + 1], bank(5 + u % 3, P * (t + 1)), axis=AX.X))
                        dve.tensor_scalar(smx[:, 1, u:u + 1], smx[:, 0, u:u + 1], -SCALE[m], None, ALU.mult).then_inc(sc_max, 1)

                    maxi(0)
                    for u in range(UNITS):
                        if u + 1 < UNITS:
                            maxi(u + 1)
                        m, h, t = head_of(u)
                        dve.wait_ge(p_exp, u + 1)
                        link(dve.reciprocal(smx[:, 3, u:u + 1], smx[:, 2, u:u + 1]))
                        pr = prob[u % 2][:, 0:P * (t + 1)]
                        dve.tensor_scalar(pr, pr, smx[:, 3, u:u + 1], None, ALU.mult).then_inc(p_norm, 1)
                        if u % 8 == 0 and u:
                            mix_low(u // 8 - 1)
                    mix_low(3)

            dve.wait_ge(w_used, N_UP0)
            for t in range(TT):
                dve.wait_ge(s_xre, 16 * TT)
                for hf in range(2):
                    xs = x_sb[:, t, L * hf:L * hf + L]
                    ins = dve.tensor_tensor(xs, xs, bank(2 * t + hf), ALU.add)
                ins.then_inc(x2_ready, 1)
            dve.wait_ge(x2_sq, TT + 1)
            dve.wait_ge(x2_ready, TT)
            for t in range(TT):
                dve.tensor_scalar(norm2[:, t, :], x_sb[:, t, :], stat[:, 4 + t:5 + t], None, ALU.mult).then_inc(n2_ready, 1)
            for k in range(KD):
                dve.wait_ge(h2_h, k + 1)
                dve.scalar_tensor_tensor(hT_lo[:, k, :], bank(k), vec[:, V_N2 + k:V_N2 + k + 1],
                                         hT_hi[:, k, :].bitcast(F32), ALU.mult, ALU.subtract).then_inc(h2_l, 1)

            def up(i, b):
                j = 2 * i + b
                for e in range(2):
                    t = conv[2 * b + e]
                    dve.wait_ge(up_tap, 2 * j + e + 1)
                    dve.scalar_tensor_tensor(t[:, 1:], bank(2 * b + e)[:, 0:L - 1], taps[:, 1, e * JF + j, :], t[:, 1:],
                                             ALU.mult, ALU.add).then_inc(up_mid, 1)
                    dve.wait_ge(up_mid, 2 * j + e + 1)
                    dve.scalar_tensor_tensor(t[:, 2:], bank(2 * b + e)[:, 0:L - 2], taps[:, 0, e * JF + j, :], t[:, 2:],
                                             ALU.mult, ALU.add).then_inc(up_conv, 1)
                dve.wait_ge(up_conv, 2 * j + 2)
                dve.wait_ge(up_silu, j + 1)
                dve.tensor_tensor(g_sb[:, j, :], conv[2 * b], conv[2 * b + 1], ALU.mult).then_inc(g_ready, 1)

            with dve.Fori(0, JF // 2) as i:
                for b in range(2):
                    up(i, b)

            def g_low(k, s):
                dve.wait_ge(g_h, k + 1)
                dve.tensor_tensor(hT_lo[:, s, :], g_sb[:, k, :], hT_hi[:, s, :].bitcast(F32), ALU.subtract).then_inc(g_l, 1)

            dve.wait_ge(g_ready, JF)
            with dve.Fori(0, 5) as i:
                for b in range(4):
                    g_low(4 * i + b, b)
            for k in range(20, JF):
                g_low(k, k % 4)
            dve.wait_ge(w_used, N_DOWN0 + JF)
            dve.wait_ge(s_fing, 16)
            for t in range(TT):
                for hf in range(2):
                    xs = x_sb[:, t, L * hf:L * hf + L]
                    ins = dve.tensor_tensor(xs, xs, bank(2 * t + hf), ALU.add)
                ins.then_inc(x3_ready, 1)
            for t in range(TT):
                dve.wait_ge(x3_sq, 2 * t + 2)
                dve.scalar_tensor_tensor(x_sb[:, t, :], x_sb[:, t, :], stat[:, 12 + t:13 + t], fing, ALU.mult,
                                         ALU.mult).then_inc(y_ready, 1)

        @block.tensor
        def _(pe):
            def mm(out, lhsT, rhs, start=True, stop=True):
                return pe.matmul(out, lhsT, rhs, start=start, stop=stop)

            pe.wait_ge(s_const, 16)
            pe.wait_ge(s_vrows, 16 * VROW_DMAS)
            pe.wait_ge(ldt_rows, 1)
            pe.transpose(bank(2, V_ROWS), vrows[0:V_ROWS, :], C("ident", V_ROWS, hi=V_ROWS)).then_inc(vec_t, 1)
            pe.wait_ge(s_taps, 32)
            pe.transpose(bank(3, 88), taps_rows[0:88, 0, :], C("ident", 88, hi=88)).then_inc(vec_t, 1)
            pe.transpose(ps[:, 3 * L + 88:3 * L + 132], taps_rows[0:44, 1, :], C("ident", 44, hi=44)).then_inc(vec_t, 1)
            pe.wait_ge(xn, TT)
            for k in range(KD):
                b = HT_BANKS[k]
                if b in (2, 3) and k < 4:
                    pe.wait_ge(vec_r, b - 1)
                if k >= 4:
                    pe.wait_ge(hT_l, k - 3)
                for t in range(TT):
                    ins = pe.transpose(ps[:, b * L + P * t:b * L + P * t + P], x_sb[:, t, P * k:P * k + P], ident)
                ins.then_inc(hT_t, 1)
            def split_products(out, lhs, rhs, first, last):
                ins = None
                for m, (l_, r_) in enumerate(((0, 0), (1, 0), (0, 1))):
                    ins = mm(out, lhs[l_], rhs[r_], start=first and m == 0, stop=last and m == 2)
                return ins

            def weights(s, cols=slice(0, D)):
                return w_hi[:, s, cols], w_lo[:, s, cols]

            def proj(n):
                s = n % RING
                pe.wait_ge(w_l, n + 1)
                if n == 0:
                    pe.wait_ge(hT_l, KD)
                if n >= 2:
                    pe.wait_ge(*freed_by[n - 2])
                if PROJ[n][0].startswith("mv"):
                    for t in range(TT):
                        for k in range(KD):
                            tk = slice(P * t, P * t + P)
                            ins = split_products(bank(n % 2)[:, tk], (hT_hi[:, k, tk], hT_lo[:, k, tk]),
                                                 weights(s, slice(P * k, P * k + P)), k == 0, k == KD - 1)
                else:
                    for k in range(KD):
                        ins = split_products(bank(n % 2), weights(s, slice(P * k, P * k + P)),
                                             (hT_hi[:, k, :], hT_lo[:, k, :]), k == 0, k == KD - 1)
                ins.then_inc(w_used, 1)

            def col(b, c, w=CH):
                return ps[:, b * L + w * c:b * L + w * c + w]

            def s5_y(s):
                pe.wait_ge(xs_ready, 2 * s + 2)
                if s == 4:
                    pe.wait_ge(yd_ready, 1)
                if s == 0:
                    pe.wait_ge(bc_ready, 3)
                q = 32 * (s % 4)
                out = ps[q:q + 32, 7 * L:8 * L]
                mm(out, ct[:, 0, s, :], work[4].rearrange("p h t -> p (h t)"), True, False)
                mm(out, ct[:, 1, s, :], work[5].rearrange("p h t -> p (h t)"), False, True).then_inc(y_ps, 1)

            n_ws = n_kv = 0
            for step, arg in ORDER:
                if step == "proj":
                    proj(arg)
                elif step == "table" and arg == 0:
                    pe.wait_ge(bbd_ready, 4)
                    for r in range(2):
                        for f in range(2):
                            at = 6 * L + P * (2 * r + f)
                            ins = pe.transpose(ps[:, at:at + P], bbd[:, r, 4 * f:4 * f + 4].rearrange("p s g c -> p (s g c)"), ident)
                    ins.then_inc(bc_t, 1)
                    pe.wait_ge(cbd_ready, 4)
                    for r in range(2):
                        for f in range(2):
                            at = 7 * L + P * (2 * r + f)
                            ins = pe.transpose(ps[:, at:at + P], cbd[:, r, f].rearrange("p g n -> p (g n)"), ident)
                    ins.then_inc(bc_t, 1)
                elif step == "gnorm":
                    p = arg
                    if p:
                        pe.wait_ge(o_norm, 2 * p)
                    for m, t in enumerate(("DT", "LT")):
                        pe.wait_ge(gsq, 2 * p + m + 1)
                        mm(bank(2 + m), C("blockones"), flat(CP[t])).then_inc(gss, 1)
                elif step == "gates":
                    p = arg
                    pe.wait_ge(row_act, 6)
                    pe.wait_ge(row_dve, 3)
                    pe.wait_ge(grn, 2 * p + 2)
                    mm(bank(2), C("selbc", P, lo=0, hi=4, off=P * p), rows[0:4, :]).then_inc(gbc, 1)
                    mm(bank(3), C("selbc", P, lo=32, hi=36, off=P * p), rows[32:36, :]).then_inc(gbc, 1)
                    if p == 0:
                        for c in range(NCH):
                            for e in range(2):
                                ins = mm(ps[64 * e:64 * e + 64, 4 * L + 8 * c:4 * L + 8 * c + 8],
                                         rows[0:100, CH * c:CH * c + CH], C("seltok", 8, lo=0, hi=100, off=8 * e))
                        ins.then_inc(tok_ps, 1)
                elif step == "gkk":
                    p = arg
                    pe.wait_ge(knbd, 2 * (p + 1))
                    pe.wait_ge(gpre, p + 1)
                    pe.wait_ge(egam, 2 * (p + 1))
                    pe.wait_ge(tok_ready, 1)
                    if p:
                        pe.wait_ge(gout_done, p)
                    for c in range(NCH):
                        ins = mm(col(2, c), blocks(BD["KN"], c), CP["M1"][:, c])
                    ins.then_inc(gkk, 1)
                    for c in range(NCH):
                        ins = mm(col(3, c), blocks(BD["KN"], c), gq[p][:, CH * c:CH * c + CH])
                    ins.then_inc(gkk, 1)
                    for c in range(NCH):
                        ins = mm(col(4, c), blocks(BD["KN"], c), istack)
                    ins.then_inc(gkk, 1)
                    pe.wait_ge(vbd_ready, 2 * (p + 1))
                    pe.wait_ge(gkk_used, 4 * p + 2)
                    for c in range(NCH):
                        ins = mm(col(2, c), blocks(BD["Y"], c), istack)
                    ins.then_inc(gvt, 1)
                elif step == "ginv":
                    p, l = arg
                    m = 6 * p + l
                    pe.wait_ge(cm_ready, 2 * (m + 1))
                    if l == 0:
                        pe.wait_ge(gkk_used, 4 * (p + 1))
                    else:
                        pe.wait_ge(x_ready, m)
                    for c in range(NCH):
                        ins = mm(col(4, c), blocks(BD["CM"], c), istack if l == 0 else CP["X"][:, c])
                    ins.then_inc(m1_ps, 1)
                    if l:
                        pe.wait_ge(m1_ready, 5 * p + l)
                        pe.wait_ge(y_act, m)
                        pe.wait_ge(y_dve, m)
                        for c in range(NCH):
                            ins = mm(col(4, c), blocks(BD["Y"], c), CP["M1"][:, c])
                        ins.then_inc(m2_ps, 1)
                    pe.wait_ge(x_ready, m + 1)
                    if l == 0:
                        pe.wait_ge(vp_ready, p + 1)
                    for c in range(NCH):
                        for e in range(2):
                            r = slice(64 * e, 64 * e + 64)
                            ins = mm(YT[r, c, :], CP["X"][r, c], ident[r, 64 * e:64 * e + 64])
                    ins.then_inc(yt_ps, 1)
                elif step == "guw":
                    p = arg
                    m = 6 * p + 6
                    pe.wait_ge(y_act, m)
                    pe.wait_ge(y_dve, m)
                    for c in range(NCH):
                        mm(col(4, c), blocks(BD["Y"], c), CP["VP"][:, c])
                    for c in range(NCH):
                        ins = mm(ps[:, 2 * L + P * c:2 * L + P * c + P], blocks(BD["KW"], c), blocks(BD["Y"], c))
                    ins.then_inc(uw_ps, 1)
                elif step == "grec":
                    p, c = arg
                    if c == 0:
                        pe.wait_ge(u_ready, p + 1)
                        pe.wait_ge(wt_ready, p + 1)
                        mm(col(3, 0), blocks(BD["KD"], 0), CP["VP"][:, 0]).then_inc(kv_ps, 1)
                        mm(col(2, 0), blocks(BD["ATT"], 0), CP["VP"][:, 0]).then_inc(o_ps, 1)
                    else:
                        pe.wait_ge(state_ready, 7 * p + c)
                        former = state[:, 1 - c % 2, :]
                        mm(col(4, 0), blocks(BD["KN"], c), former).then_inc(ws_ps, 1)
                        mm(col(2, c), blocks(BD["QD"], c), former, True, False)
                        pe.wait_ge(vnew_ready, 7 * p + c)
                        vn = vnew[:, c % 2, :]
                        if c < NCH - 1:
                            mm(col(3, c % 2), blocks(BD["KD"], c), vn).then_inc(kv_ps, 1)
                        mm(col(2, c), blocks(BD["ATT"], c), vn, False, True).then_inc(o_ps, 1)
                elif step == "gout":
                    p = arg
                    pe.wait_ge(o_norm, 2 * (p + 1))
                    for c in range(NCH):
                        ins = mm(col(4, c), blocks(BD["QD"], c), istack)
                    ins.then_inc(oT_ps, 1)
                elif step == "bu":
                    s = arg
                    f, q = s // 4, 32 * (s % 4)
                    pe.wait_ge(proj_copied, freed_by[PN[f"u{f}"]][1])
                    pe.wait_ge(bc_ready, 3)
                    if s:
                        pe.wait_ge(rot_prod, s)
                    for r in range(2):
                        ins = mm(bank(5 + r), bt[q:q + 32, r, f, :], su[f][q:q + 32, :])
                    ins.then_inc(bu_ps, 1)
                    if s:
                        s5_y(s - 1)
                elif step == "glu":
                    s5_y(ST - 1)
                    pe.wait_ge(gelu_ready, 2)
                    pe.wait_ge(s_glu, 16)
                    pe.wait_ge(rot_prod, ST)
                    for f in range(2):
                        mm(bank(5 + f), gluw[:, 0, P * f:P * f + P], su[0], True, False)
                        mm(bank(5 + f), gluw[:, 1, P * f:P * f + P], su[1], False, True).then_inc(glu_ps, 1)
                elif step == "mla":
                    pe.wait_ge(glu_sig, 2)
                    pe.wait_ge(mla_sq, 2)
                    mm(bank(5), C("ones"), mrs[0], True, False)
                    mm(bank(5), C("ones", hi=64), mrs[1][0:64], False, True).then_inc(mla_ss, 1)
                    pe.wait_ge(mla_sq, 3)
                    mm(bank(6), C("ones"), rope1).then_inc(mla_ss, 1)
                    pe.wait_ge(mla_n, 3)
                    pe.wait_ge(wswap, 4)
                    pe.wait_ge(yd_ready, 2)
                    pe.wait_ge(gout_done, PAIRS)

                    for m in range(4):
                        b, cols = MLA_BANKS[m], slice(P * m, P * m + P)
                        mm(bank(b), wuq[:, 0, cols], cq[0], True, False)
                        mm(bank(b), wuq[0:64, 1, cols], cq[1][0:64], False, True).then_inc(mla_ps, 1)
                    for m in range(2):
                        mm(bank(MLA_BANKS[4 + m]), wukv[:, P * m:P * m + P], ckv).then_inc(mla_ps, 1)
                    for m in range(2):
                        pe.wait_ge(mla_ev, 2 * (m + 1))
                        for t in range(2):
                            b = MLA_BANKS[6 + m]
                            tk = P * (2 * m + t)
                            ins = mm(ps[:, b * L + 256 * t:b * L + 256 * t + 256], ckv[:, tk:tk + P], wukv[:, 256:512])
                        ins.then_inc(mla_ps, 1)
                elif step == "attend":
                    pe.wait_ge(*freed_by[NPROJ - 2])
                    pe.wait_ge(*freed_by[NPROJ - 1])
                    pe.wait_ge(mla_ev, 10)
                    pe.wait_ge(krot, 1)
                    pe.wait_ge(kcopy, 3)
                    pe.wait_ge(masks16, 2)

                    def score(u):
                        m, h, t = head_of(u)
                        if u >= 3:
                            pe.wait_ge(p_exp, u - 2)
                        b = 5 + u % 3
                        qs = slice(P * t, P * t + P)
                        if m == 0:
                            r = slice(64 * (h % 2), 64 * (h % 2) + 64)
                            q_, k_ = moq[h // 2][r, qs], mok[h // 2][r]
                        else:
                            q_, k_ = q96[0:96, h, qs], k96[0:96, h]
                        if t:
                            mm(bank(b, P * t), q_, k_[:, 0:P * t])
                        diag = ps[:, b * L + P * t:b * L + P * t + P]
                        mm(diag, q_, k_[:, qs], True, False)
                        mm(diag, ident16[:], causal16[:], False, True).then_inc(sc_ps, 1)

                    def pv(u):
                        m, h, t = head_of(u)
                        pe.wait_ge(pT_ready, u + 1)
                        if u % 8 == 0 and u >= 16:
                            pe.wait_ge(mix_l, 4 + u // 8 - 1)
                        e = h % 2
                        v_ = mov if m == 0 else mlav
                        out = ps[64 * e:64 * e + 64, mix_bank(u) * L + P * t:mix_bank(u) * L + P * t + P]
                        for k in range(t + 1):
                            ins = mm(out, v_[:, k, HD * h:HD * h + HD], probT[u % 2][:, k, :], k == 0, k == t)
                        ins.then_inc(pv_done, 1)

                    score(0)
                    score(1)
                    for u in range(UNITS):
                        if u + 2 < UNITS:
                            score(u + 2)
                        m, h, t = head_of(u)
                        pe.wait_ge(p_norm, u + 1)
                        if u >= 2:
                            pe.wait_ge(pT_ready, u - 1)
                        for k in range(t + 1):
                            ins = pe.transpose(ps[:, (2 + u % 2) * L + P * k:(2 + u % 2) * L + P * k + P],
                                               prob[u % 2][:, P * k:P * k + P], ident)
                        ins.then_inc(pT_ps, 1)
                        if u:
                            pv(u - 1)
                    pv(UNITS - 1)

            def tokens_out(k, s, left, first, last):
                for t in range(TT):
                    tk = slice(P * t, P * t + P)
                    for hf in range(2):
                        ins = split_products(bank(2 * t + hf), (hT_hi[:, left, tk], hT_lo[:, left, tk]),
                                             weights(s, slice(L * hf, L * hf + L)), first, last)
                ins.then_inc(w_used, 1)

            pe.wait_ge(mix_l, KD)
            for k in range(KD):
                pe.wait_ge(w_l, N_OUT0 + k + 1)
                tokens_out(k, (N_OUT0 + k) % RING, k, k == 0, k == KD - 1)
            pe.wait_ge(x2_ready, TT)
            pe.wait_ge(n2_ready, TT)
            for k in range(KD):
                for t in range(TT):
                    ins = pe.transpose(ps[:, k * L + P * t:k * L + P * t + P], norm2[:, t, P * k:P * k + P], ident)
                ins.then_inc(h2_t, 1)
            pe.wait_ge(h2_l, KD)

            def up(i, b):
                for e in range(2):
                    n = N_UP0 + 4 * i + 2 * b + e
                    pe.wait_ge(w_l, n + 1)
                    if not isinstance(i, int):
                        pe.wait_ge(up_conv, 4 * i + 2 * b + e - 3)
                    for k in range(KD):
                        ins = split_products(bank(2 * b + e), weights(2 * b + e, slice(P * k, P * k + P)),
                                             (hT_hi[:, k, :], hT_lo[:, k, :]), k == 0, k == KD - 1)
                    ins.then_inc(w_used, 1)

            for b in range(2):
                up(0, b)
            with pe.Fori(1, JF // 2) as i:
                for b in range(2):
                    up(i, b)

            def down(k, s):
                pe.wait_ge(w_l, N_DOWN0 + k + 1)
                pe.wait_ge(g_l, k + 1)
                tokens_out(k, s, s, isinstance(k, int) and k == 0, isinstance(k, int) and k == JF - 1)

            for k in range(4):
                down(k, k)
            with pe.Fori(1, 5) as i:
                for b in range(4):
                    down(4 * i + b, b)
            for k in range(20, JF):
                down(k, k % 4)


_INS = ["x", "norm1_g", "w_in", "gdn_conv_w", "gdn_a_log", "gdn_dt_bias", "gdn_norm_g", "mla_q_norm_g",
        "mla_w_uq", "mla_kv_norm_g", "mla_w_ukv", "s5_lam_re", "s5_lam_im", "s5_b_re", "s5_b_im",
        "s5_c_re", "s5_c_im", "s5_d", "s5_log_dt", "s5_glu_w", "s5_glu_b", "w_out", "norm2_g",
        "ffn_w_up", "ffn_conv_w", "ffn_w_down", "final_norm_g"]


def kernel(**inputs):
    import numpy as _np
    import concourse.bacc as _bacc
    from concourse import mybir as _mybir
    from concourse.bass_utils import run_bass_kernel_spmd as _run

    nc = _bacc.Bacc("TRN2", target_bir_lowering=False, num_devices=1)
    arrays, aps = {}, {}
    for name in _INS:
        arr = _np.ascontiguousarray(inputs[name])
        arrays[f"in_{name}"] = arr
        aps[name] = nc.dram_tensor(f"in_{name}", arr.shape, _mybir.dt.from_np(arr.dtype), kind="ExternalInput").ap()
    arrays["constants"] = constants()
    aps["constants"] = nc.dram_tensor("constants", (P, CONST_COLS), F32, kind="ExternalInput").ap()
    aps["out"] = nc.dram_tensor("out", (1, L, D), F32, kind="ExternalOutput").ap()
    hybrid_trunk(nc, aps)
    r = _run(nc, [arrays], core_ids=[0])
    return r.results[0]["out"]
```

```python
import math
from contextlib import ExitStack

import numpy as np

import concourse.bass as bass
from concourse import mybir

F32 = mybir.dt.float32
F32R = mybir.dt.float32r
BF16 = mybir.dt.bfloat16
ALU = mybir.AluOpType
ACT = mybir.ActivationFunctionType
AX = mybir.AxisListType

P = 128
L = 512
TT = L // P
D = 1024
KD = D // P
H = 4
HD = 64
PAIRS = H // 2
CH = 64
NCH = L // CH
QLORA, KVLORA, ROPE, MLA_QK = 192, 128, 32, 96
G, GW, NS = 16, 16, 64
ST = G * NS // P
HALF = L // 2
DFF = 2816
JF = DFF // P
EPS = 1e-6
BIG = 1e30
ROUND = 1.5 * 2.0 ** 23
TWO_PI = (6.28125, 1.9350051879882812e-3, 3.0199159819567529e-7)

A_Q, A_K, A_V, A_Z, A_A, A_B, M_Q, M_K, M_V, C_Q, C_KV, C_KR, S_U = (
    0, 256, 512, 768, 1024, 1028, 1032, 1288, 1544, 1800, 1992, 2120, 2152)

PROJ = [
    ("q0", [(0, A_Q, 128)]), ("k0", [(0, A_K, 128)]), ("v0", [(0, A_V, 128)]),
    ("misc", [(0, C_KR, 32), (32, C_KR + 16, 16), (48, C_KR, 16), (64, A_A, 32), (96, A_B, 32)]),
    ("u0", [(0, S_U, 128)]), ("u1", [(0, S_U + 128, 128)]),
    ("q1", [(0, A_Q + 128, 128)]), ("k1", [(0, A_K + 128, 128)]), ("v1", [(0, A_V + 128, 128)]),
    ("z0", [(0, A_Z, 128)]), ("z1", [(0, A_Z + 128, 128)]),
    ("cq0", [(0, C_Q, 128)]), ("cq1", [(0, C_Q + 128, 64)]), ("ckv", [(0, C_KV, 128)]),
    ("mq0", [(0, M_Q, 128)]), ("mk0", [(0, M_K, 128)]), ("mv0", [(0, M_V, 128)]),
    ("mq1", [(0, M_Q + 128, 128)]), ("mk1", [(0, M_K + 128, 128)]), ("mv1", [(0, M_V + 128, 128)]),
]
LEVELS = 6
UNITS = 2 * H * TT
PN = {name: n for n, (name, _) in enumerate(PROJ)}
NPROJ = len(PROJ)
N_OUT0 = NPROJ
N_UP0 = N_OUT0 + KD
N_DOWN0 = N_UP0 + 2 * JF
RING = 4
RAW = 2

V_N1, V_N2, V_CONV, V_QN, V_KVN, V_GLUB, V_SD, V_GN, V_LRE, V_LIM, V_LDT, V_DTB, V_ALOG, V_ROWS = (
    0, 8, 16, 40, 42, 43, 45, 47, 48, 56, 64, 72, 73, 74)

_CONSTS = [("ident", 128), ("istack", 64), ("blockones", 128), ("ones", 128), ("dmask", 64),
           ("level", 6 * 64), ("selbc", 2 * 128), ("seltok", 2 * 8), ("scanmask", L), ("ropec", L),
           ("ropes", L), ("bmask", 2), ("cmask", 2), ("causal", 128)]
CO, _at = {}, 0
for _n, _w in _CONSTS:
    CO[_n] = _at
    _at += _w
CONST_COLS = _at


def constants():
    c = np.zeros((P, CONST_COLS), np.float32)

    def put(name, a):
        c[:a.shape[0], CO[name]:CO[name] + a.shape[1]] = a

    r = np.arange(P)
    j, i = r[:, None] % CH, np.arange(CH)[None, :]
    put("ident", np.eye(P, dtype=np.float32))
    put("istack", (j == i).astype(np.float32))
    put("blockones", (r[:, None] // HD == r[None, :] // HD).astype(np.float32))
    put("ones", np.ones((P, P), np.float32))
    put("dmask", np.where(i >= j, 0.0, -BIG).astype(np.float32))
    for l in range(6):
        s = 1 << l
        m = (j > i) & (i // (2 * s) == j // (2 * s)) & (i // s != j // s)
        c[:, CO["level"] + 64 * l:CO["level"] + 64 * (l + 1)] = m
    for p in range(PAIRS):
        for a in range(2):
            h = 2 * p + a
            for base in (0, 32):
                c[base + h, CO["selbc"] + 128 * p + 64 * a:CO["selbc"] + 128 * p + 64 * (a + 1)] = 1.0
            for q in range(4):
                c[32 * q + h, CO["seltok"] + 8 * a + 2 * q + p] = 1.0
    put("scanmask", np.broadcast_to((np.arange(L) % CH != 0).astype(np.float32), (P, L)))
    freq = np.float32(10000.0) ** (-np.arange(0, ROPE, 2, dtype=np.float32) / np.float32(ROPE))
    ang = np.arange(L, dtype=np.float32)[None, :] * freq.astype(np.float32)[:, None]
    cos, sin = np.cos(ang).astype(np.float32), np.sin(ang).astype(np.float32)
    put("ropec", np.tile(np.concatenate([cos, cos]), (4, 1)))
    put("ropes", np.tile(np.concatenate([-sin, sin]), (4, 1)))
    gg = np.arange(2)[None, :]
    put("bmask", (r[:, None] // NS == gg).astype(np.float32))
    put("cmask", ((r[:, None] // GW) % 2 == gg).astype(np.float32))
    put("causal", np.where(r[None, :] <= r[:, None], 0.0, -BIG).astype(np.float32))
    return c


def hybrid_trunk(nc, a):
    ctx = ExitStack()
    with ctx:
        def sb(name, shape, dt=F32):
            return ctx.enter_context(nc.sbuf_tensor(name, shape, dt))

        def sem(name):
            return ctx.enter_context(nc.semaphore(name))

        x_sb = sb("x_sb", [P, TT, D])
        hT_hi = sb("hT_hi", [P, KD, L], F32R)
        hT_lo = sb("hT_lo", [P, KD, L], F32R)
        w_raw = sb("w_raw", [P, RAW, D])
        w_hi = sb("w_hi", [P, RING, D], F32R)
        w_lo = sb("w_lo", [P, RING, D], F32R)
        const = sb("const", [P, CONST_COLS])
        ident16 = sb("ident16", [P, P], BF16)
        causal16 = sb("causal16", [P, P], BF16)
        vrows = sb("vrows", [P, P])
        ldt = sb("ldt", [P, 2])
        vec = sb("vec", [P, V_ROWS])
        taps_rows = sb("taps_rows", [P, 2, P])
        taps = sb("taps", [P, 3, 2 * JF, 1])
        fixed = sb("fixed", [P, 4])
        small = sb("small", [P, 8])

        FREE = nc.sbuf_bytes_remaining // 4 - 64
        arena = sb("arena", [P, FREE])
        top = [0]
        spans = {}

        def take(name, n, at=None):
            start = top[0] if at is None else at
            if at is None:
                top[0] += n
            assert start + n <= FREE, (name, start + n, FREE)
            spans[name] = (start, n)
            return arena[:, start:start + n]

        gq = [take(f"gq{p}", L) for p in range(PAIRS)]
        gk = [take(f"gk{p}", L) for p in range(PAIRS)]
        gv = [take(f"gv{p}", L) for p in range(PAIRS)]
        gz = [take(f"gz{p}", L) for p in range(PAIRS)]
        misc = take("misc", L)
        G0 = top[0]
        bd_names = ["KN", "QD", "ATT", "LT", "Y", "KW", "KD"]
        BD = {n: take("bd" + n, 2 * L).rearrange("p (c a i) -> p c a i", c=NCH, a=2) for n in bd_names}
        cp_names = ["DT", "X", "M1", "VP"]
        CP = {n: take("cp" + n, L).rearrange("p (c i) -> p c i", c=NCH) for n in cp_names}
        rows = take("rows", L)
        tok = take("tok", NCH * 8).rearrange("p (c q r) -> p c q r", c=NCH, q=4)
        glast = take("glast", NCH)
        state = take("state", 2 * HD).rearrange("p (b v) -> p b v", b=2)
        vnew = take("vnew", 2 * HD).rearrange("p (b v) -> p b v", b=2)
        onorm = take("onorm", 2 * NCH).rearrange("p (b c) -> p b c", b=2)
        G1 = top[0]
        su = [take(f"su{f}", L) for f in range(2)]
        work = [take(f"work{n}", L).rearrange("p (h t) -> p h t", h=2) for n in range(8)]
        bt = take("bt", 4 * P).rearrange("p (r f n) -> p r f n", r=2, f=2)
        ct = take("ct", 2 * ST * 32).rearrange("p (r s n) -> p r s n", r=2, s=ST)
        s5p = take("s5p", 24 * ST).rearrange("p (k s) -> p k s", s=ST)
        s5c = take("s5c", 4)
        gluw = take("gluw", 512).rearrange("p (k n) -> p k n", k=2)
        moq = [take(f"moq{p}", L) for p in range(PAIRS)]
        mok = [take(f"mok{p}", L) for p in range(PAIRS)]
        mov = take("mov", TT * 256).rearrange("p (t n) -> p t n", t=TT)
        cq = [take(f"cq{f}", L) for f in range(2)]
        ckv = take("ckv", L)
        smx = take("smx", 4 * 32).rearrange("p (k u) -> p k u", k=4)

        b_nat = work[0].rearrange("p h t -> p (h t)")[:, 0:2 * P].rearrange("p (r s c) -> p r s c", r=2, s=ST)
        bbar = work[1].rearrange("p h t -> p (h t)")[:, 0:2 * P].rearrange("p (r s c) -> p r s c", r=2, s=ST)
        btmp = work[2].rearrange("p h t -> p (h t)")[:, 0:P].rearrange("p (s c) -> p s c", s=ST)
        bbd = work[3].rearrange("p h t -> p (h t)").rearrange("p (r s g c) -> p r s g c", r=2, s=ST, g=2)
        c_nat = work[4].rearrange("p h t -> p (h t)")[:, 0:4 * NS].rearrange("p (r f n) -> p r f n", r=2, f=2)
        cbd = work[5].rearrange("p h t -> p (h t)").rearrange("p (r f g n) -> p r f g n", r=2, f=2, g=2)

        xw = x_sb[:].rearrange("p t d -> p (t d)")
        cosT = xw[:, 0:ST * HALF].rearrange("p (s t) -> p s t", s=ST)
        sinT = xw[:, ST * HALF:2 * ST * HALF].rearrange("p (s t) -> p s t", s=ST)

        q96 = xw[:, 0:H * L].rearrange("p (h t) -> p h t", h=H)
        k96 = xw[:, H * L:2 * H * L].rearrange("p (h t) -> p h t", h=H)
        def works(n, m):
            at = spans[f"work{n}"][0]
            return arena[:, at:at + m * L]

        mlav = works(0, 2).rearrange("p (t n) -> p t n", t=TT)
        wuq = works(2, 2).rearrange("p (k n) -> p k n", k=2)
        rope2, wukv, rope1, mrs = works(4, 1), works(6, 1), works(7, 1), su
        prob = [w_raw[:, 0, L * b:L * b + L] for b in range(2)]
        probT = [w_raw[:, 1, L * b:L * b + L].rearrange("p (k q) -> p k q", k=TT) for b in range(2)]

        g_sb = take("g_sb", JF * L, at=0).rearrange("p (j t) -> p j t", j=JF)
        F0 = JF * L
        conv = [take(f"conv{b}", L, at=F0 + b * L) for b in range(4)]
        fing = take("fing", D, at=F0 + 4 * L)
        norm2 = take("norm2", TT * D, at=0).rearrange("p (t d) -> p t d", t=TT)
        junk = take("junk", D, at=F0 + 4 * L + D)
        stat = take("stat", 32, at=F0 + 4 * L + 2 * D)

        ps = ctx.enter_context(nc.psum_tensor("ps", [P, 8 * L], F32))

        def bank(b, n=L):
            return ps[:, b * L:b * L + n]

        s_x = [sem(f"x_loaded{t}") for t in range(TT)]
        s_const = sem("const_loaded")
        s_vrows = sem("vrows_loaded")
        s_taps = sem("taps_loaded")
        s_s5in = sem("s5_params_loaded")
        s_glu = sem("glu_w_loaded")
        s_mlaw = sem("mla_w_loaded")
        s_xre = sem("x_reloaded")
        s_fing = sem("final_gain_loaded")
        s_store = sem("stored")
        w_loaded = [sem(f"w_loaded{s}") for s in range(RING)]
        w_h = sem("w_high_ready")
        w_l = sem("w_low_ready")
        w_used = sem("w_used")
        act_step = sem("scalar_step")
        dve_step = sem("vector_step")
        pool_step = sem("pool_step")
        cleared = sem("tiles_cleared")
        vclear = sem("vrows_cleared")
        masks16 = sem("bf16_masks_ready")
        vec_t = sem("vec_transposed")
        vec_r = sem("vec_ready")
        xsq = sem("x_squares")
        xn = sem("x_normed")
        hT_t = sem("h_transposed")
        hT_h = sem("h_high_ready")
        hT_l = sem("h_low_ready")
        proj_done = sem("proj_done")
        proj_free = [sem(f"proj_bank_free{b}") for b in range(2)]
        conv0 = sem("conv_first_tap")
        conv_done = sem("conv_done")
        silu_done = sem("silu_done")
        gsq = sem("gdn_squares")
        gss = sem("gdn_square_sums")
        grn = sem("gdn_norm_factors")
        misc_ev = sem("misc_evacuated")
        row_act = sem("rows_by_scalar")
        row_dve = sem("rows_by_vector")
        rows_ready = sem("rows_ready")
        gbc = sem("gate_broadcast")
        tok_ps = sem("token_scalars_in_psum")
        tok_ready = sem("token_scalars_ready")
        egam = sem("exp_gamma_ready")
        gpre = sem("gdn_operands_ready")
        knbd = sem("kn_blocks_ready")
        vbd_ready = sem("v_blocks_ready")
        dt_arg = sem("decay_argument")
        dt_ready = sem("decay_ready")
        gkk = sem("gdn_kk_kq_ktok")
        gvt = sem("gdn_vtok")
        cm_ready = sem("level_mask_ready")
        cm_used = sem("level_mask_used")
        m1_ps = sem("m1_in_psum")
        m1_ready = sem("m1_ready")
        m2_ps = sem("m2_in_psum")
        x_ready = sem("inverse_ready")
        yt_ps = sem("inverse_transposed")
        y_act = sem("y_half0_ready")
        y_dve = sem("y_half1_ready")
        uw_ps = sem("u_w_in_psum")
        u_ready = sem("u_ready")
        wt_ready = sem("wt_ready")
        ws_ps = sem("w_state_in_psum")
        vnew_ready = sem("v_new_ready")
        kv_ps = sem("k_v_in_psum")
        state_ready = sem("state_ready")
        o_ps = sem("gdn_o_in_psum")
        o_sq = sem("gdn_o_squared")
        o_sum = sem("gdn_o_sums")
        o_fac = sem("gdn_o_factor")
        o_norm = sem("gdn_o_normed")
        oT_ps = sem("gdn_o_transposed")
        mix_h = sem("mix_high_ready")
        mix_tmp = sem("mix_value_ready")
        mix_l = sem("mix_low_ready")
        s5_act = sem("s5_scalar_steps")
        s5_dve = sem("s5_vector_steps")
        bbd_ready = sem("s5_b_blocks_ready")
        cbd_ready = sem("s5_c_blocks_ready")
        bc_t = sem("s5_bc_transposed")
        bc_ready = sem("s5_bc_ready")
        tab_c = sem("table_cos_part")
        tab_s = sem("table_sin_part")
        bu_ps = sem("s5_bu_in_psum")
        rot_prod = sem("s5_rotated_products")
        rot_sum = sem("s5_rotated_sums")
        unrot_prod = sem("s5_unrotated_products")
        xs_ready = sem("s5_states_ready")
        y_ps = sem("s5_y_in_psum")
        yd_ready = sem("s5_y_plus_d")
        gelu_ready = sem("s5_gelu_ready")
        glu_ps = sem("glu_in_psum")
        glu_sig = sem("glu_sigmoid_ready")
        mla_sq = sem("mla_squares")
        mla_ss = sem("mla_square_sums")
        mla_rn = sem("mla_norm_factors")
        mla_n = sem("mla_normed")
        mla_ps = sem("mla_product_in_psum")
        mla_ev = sem("mla_product_used")
        krot = sem("rope_key_ready")
        kcopy = sem("rope_key_copied")
        sc_ps = sem("scores_in_psum")
        sc_max = sem("scores_max")
        p_exp = sem("prob_exp")
        p_norm = sem("prob_normed")
        pT_ps = sem("prob_transposed")
        pT_ready = sem("probT_ready")
        pv_done = sem("pv_done")
        out_done = sem("out_product_done")
        x2_ready = sem("x2_ready")
        x2_sq = sem("x2_squares")
        n2_ready = sem("norm2_ready")
        h2_t = sem("h2_transposed")
        h2_h = sem("h2_high_ready")
        h2_l = sem("h2_low_ready")
        up_done = sem("up_done")
        up_tap = sem("up_first_tap")
        up_conv = sem("up_conv_done")
        up_silu = sem("up_silu_done")
        g_ready = sem("g_ready")
        g_h = sem("g_high_ready")
        g_l = sem("g_low_ready")
        down_done = sem("down_done")
        x3_ready = sem("x3_ready")
        x3_sq = sem("x3_squares")
        y_ready = sem("out_ready")

        def C(name, w=None, lo=0, hi=P, off=0):
            w = w or dict(_CONSTS)[name]
            return const[lo:hi, CO[name] + off:CO[name] + off + w]

        ident = C("ident")
        istack = C("istack")

        w_in_v = a["w_in"][0].rearrange("(k p) n -> p k n", p=P)
        w_up_v = a["ffn_w_up"][0].rearrange("(k p) n -> p k n", p=P)
        w_out_v = a["w_out"][0].rearrange("(k p) n -> k p n", p=P)
        w_dn_v = a["ffn_w_down"][0].rearrange("(k p) n -> k p n", p=P)
        x_v = a["x"][0].rearrange("(t p) d -> t p d", p=P)
        y_v = a["out"][0].rearrange("(t p) d -> t p d", p=P)

        def wk(t, slot, w=P):
            return t[:, slot, :].rearrange("p (k n) -> p k n", k=KD)[:, :, 0:w]

        def flat4(t):
            return t.rearrange("p c i -> p (c i)")[0:4, :]

        proj_copied = sem("proj_copied")
        bd_cleared = sem("blocks_cleared")
        gkk_used = sem("gdn_kk_kq_ktok_used")
        gnormed = sem("gdn_qk_normed")
        wswap = sem("rope_columns_swapped")
        z_ready = sem("z_silu_ready")
        gout_done = sem("gdn_output_ready")
        vp_ready = sem("beta_v_ready")
        s5mix_h = sem("s5_mix_high")
        attmix_h = sem("attention_mix_high")
        gmix_h = sem("gdn_mix_high")
        s5mix_l = sem("s5_mix_low")
        attmix_l = sem("attention_mix_low")
        gmix_l = sem("gdn_mix_low")
        y_ready_inv = sem("inverse_transposed_ready")
        HT_BANKS = [4, 5, 2, 3, 4, 5, 2, 3]
        YT = ps[0:64, 2 * L:4 * L].rearrange("p (c n) -> p c n", c=NCH)
        rA, rB, rC, rD = flat4(CP["X"]), flat4(CP["M1"]), moq[1][0:4, :], moq[0][0:4, :]

        def slot(n):
            return n % RING

        def arrived(n):
            extra = 16 * (len(PROJ[PN["misc"]][1]) - 1) if n % RAW == PN["misc"] % RAW and n >= PN["misc"] else 0
            return w_loaded[n % RAW], 16 * (n // RAW + 1) + extra

        EXTRA = [16 * (len(PROJ[PN["misc"]][1]) - 1) if r == PN["misc"] % RAW else 0 for r in range(RAW)]

        CONV_TILES = [PN[f"{t}{p}"] for p in range(PAIRS) for t in "qkv"]
        freed_by = {}
        for n in range(NPROJ):
            if n in CONV_TILES:
                freed_by[n] = (conv_done, sum(c <= n for c in CONV_TILES))
            else:
                freed_by[n] = (proj_copied, sum(m <= n and m not in CONV_TILES for m in range(NPROJ)))

        def blocks(t, c):
            return t[:, c].rearrange("p a i -> p (a i)")

        def flat(t):
            return t.rearrange("p c i -> p (c i)")

        def delta_chain(p):
            chain = [("gates", p), ("gkk", p), ("m1", (p, 0))]
            for l in range(1, LEVELS):
                chain += [("m1", (p, l)), ("m2", (p, l))]
            return chain + [("yt", p), ("guw", p)] + [("grec", (p, c)) for c in range(NCH)] + [("gout", p)]

        def woven(chain, fill):
            out, done = [], 0
            for m, step in enumerate(chain):
                out.append(step)
                upto = len(fill) * (m + 1) // len(chain)
                for f in fill[done:upto]:
                    out += f
                done = upto
            return out

        later = [("proj", n) for n in range(PN["q1"], NPROJ)]
        fill = [[later.pop(0), ("table", 2)]]
        for s in range(ST):
            fill += [[("bu", s)], [later.pop(0)], [("scan", s)] + ([later.pop(0)] if s < 5 else [])]
        fill += [[step] for step in later]
        ORDER = [("proj", PN["q0"]), ("proj", PN["k0"]), ("table", 0), ("proj", PN["v0"]), ("proj", PN["misc"]),
                 ("silu", 0), ("gnorm", 0), ("proj", PN["u0"]), ("rows", 0), ("proj", PN["u1"]), ("table", 1)]
        ORDER += woven(delta_chain(0), fill)
        ORDER += [("glu", 0), ("gouT", 0), ("silu", 1), ("gnorm", 1), ("glu", 1), ("gmix", 0)]
        fill = [[("mla", m)] for m in range(3)] + [[("att", u)] for u in range(-1, UNITS + 1)]
        ORDER += woven(delta_chain(1), fill) + [("gouT", 1), ("gmix", 1)]

        MLA_BANKS = [5, 6, 7, 0, 1, 5, 6, 7]

        def head_of(u):
            return u // 16, (u // 4) % 4, u % 4

        SCALE = (HD ** -0.5, MLA_QK ** -0.5)

        MIX_BANK = 0

        def transposed_bank(u):
            return (7, 1)[u % 2]

        s_ldt = sem("log_dt_loaded")
        ldt_rows = sem("log_dt_rows_ready")
        up_mid = sem("up_second_tap")
        VROW_DMAS = 17
        wtmp = arena[:, spans["work0"][0]:spans["work0"][0] + 4 * L]

        block = ctx.enter_context(nc.Block())

        @block.sync
        def _(sp):
            for t in range(TT):
                sp.dma_start(x_sb[:, t, :], x_v[t]).then_inc(s_x[t], 16)

            def load(n, r, dst, src):
                if n is not None and not (isinstance(n, int) and n < RAW):
                    sp.wait_ge(w_l, n - RAW + 1)
                sp.dma_start(dst, src).then_inc(w_loaded[r], 16)

            def load_proj(n):
                r = n % RAW
                for m, (at, col, width) in enumerate(PROJ[n][1]):
                    load(n if m == 0 else None, r, wk(w_raw, r)[:, :, at:at + width],
                         w_in_v[:, :, col:col + width])

            def load_out(k):
                load(N_OUT0 + k, (N_OUT0 + k) % RAW, w_raw[:, (N_OUT0 + k) % RAW, :], w_out_v[k])

            def load_up(i, b, e):
                load(N_UP0 + 4 * i + 2 * b + e, e, wk(w_raw, e),
                     w_up_v[:, :, bass.ds((2 * i + b) * P + e * DFF, P)])

            def load_down(k, r):
                load(N_DOWN0 + k, r, w_raw[:, r, :], w_dn_v[k])

            for n in range(2):
                load_proj(n)
            sp.wait_ge(vclear, 2)
            for n in range(2, NPROJ):
                load_proj(n)
                if n == PN["u0"]:
                    sp.dma_start(gluw, a["s5_glu_w"][0].rearrange("(k p) n -> p k n", p=P)).then_inc(s_glu, 16)
            for k in range(4):
                load_out(k)
            sp.wait_ge(xs_ready, 2 * ST)
            uq_v = a["mla_w_uq"][0].rearrange("r (h n) -> r h n", h=H)
            for k, r0, r1 in ((0, 0, P), (1, P, QLORA)):
                for c0, c1 in ((0, HD), (HD, MLA_QK)):
                    sp.dma_start(wuq[0:r1 - r0, k, H * c0:H * c1].rearrange("p (h n) -> p h n", h=H),
                                 uq_v[r0:r1, :, c0:c1]).then_inc(s_mlaw, 16)
            ukv_v = a["mla_w_ukv"][0].rearrange("r (h n) -> r h n", h=H)
            for c in range(2):
                sp.dma_start(wukv[:, 256 * c:256 * c + 256].rearrange("p (h n) -> p h n", h=H),
                             ukv_v[:, :, HD * c:HD * c + HD]).then_inc(s_mlaw, 16)
            sp.wait_ge(pv_done, UNITS)
            for k in range(4, KD):
                load_out(k)
                if k == 5:
                    for t in range(TT):
                        sp.dma_start(x_sb[:, t, :], x_v[t]).then_inc(s_xre, 16)
            for b in range(2):
                for e in range(2):
                    load_up(0, b, e)
            sp.wait_ge(w_used, N_UP0)
            sp.dma_start(fing, a["final_norm_g"].rearrange("(a n) -> a n", a=1).broadcast_to([P, D])).then_inc(s_fing, 16)
            with sp.Fori(1, JF // 2) as i:
                for b in range(2):
                    for e in range(2):
                        load_up(i, b, e)
            with sp.Fori(0, 5) as i:
                for b in range(4):
                    load_down(4 * i + b, b % 2)
            for k in range(20, JF):
                load_down(k, k % 2)
            for t in range(TT):
                sp.wait_ge(y_ready, t + 1)
                sp.dma_start(y_v[t], x_sb[:, t, :]).then_inc(s_store, 16)
            sp.wait_ge(s_store, 16 * TT)

        def rotated_sum(pool, s):
            pool.wait_ge(rot_prod, s + 1)
            if s:
                pool.wait_ge(y_ps, s)
            pool.tensor_tensor(work[4], work[0], work[1], ALU.add).then_inc(rot_sum, 1)
            pool.tensor_tensor(work[5], work[2], work[3], ALU.subtract).then_inc(rot_sum, 1)

        @block.gpsimd
        def _(pool):
            pool.memset(vrows[:], 0.0).then_inc(vclear, 1)
            pool.memset(taps_rows[:], 0.0).then_inc(vclear, 1)
            pool.memset(rows, 0.0).then_inc(cleared, 1)
            pool.memset(fixed[:, 0:1], EPS).then_inc(cleared, 1)
            pool.memset(fixed[:, 1:2], math.log(HD ** -0.5)).then_inc(cleared, 1)
            pool.memset(fixed[:, 2:3], 1.0).then_inc(cleared, 1)

            def low(n, r, s):
                pool.wait_ge(w_h, n + 1)
                pool.tensor_tensor(w_lo[:, s, :], w_raw[:, r, :], w_hi[:, s, :].bitcast(F32),
                                   ALU.subtract).then_inc(w_l, 1)

            def low_at(n):
                low(n, n % RAW, slot(n))

            pool.wait_ge(cleared, 4)
            pool.wait_ge(s_ldt, 16)
            pool.tensor_scalar(vrows[V_LDT:V_LDT + 8, :].rearrange("s (g n) -> s g n", g=2),
                               ldt[V_LDT:V_LDT + 8, :].unsqueeze(2).broadcast_to([ST, 2, NS]), 1.0, 0.0,
                               ALU.mult, ALU.add).then_inc(ldt_rows, 1)
            pool.wait_ge(ldt_rows, 1)
            for n in range(3):
                low_at(n)
            nxt = 3

            def v_blocks(p):
                pool.wait_ge(silu_done, 3 * (p + 1))
                if p:
                    pool.wait_ge(uw_ps, p)
                vv = gv[p].rearrange("p (c i) -> p c i", c=NCH)
                pool.wait_ge(bd_cleared, 1)
                for e in range(2):
                    pool.tensor_scalar(BD["Y"][64 * e:64 * e + 64, :, e, :], vv[64 * e:64 * e + 64], 1.0, 0.0,
                                       ALU.mult, ALU.add).then_inc(vbd_ready, 1)
                    pool.wait_ge(vbd_ready, 2 * p + e + 1)

            for step, arg in ORDER:
                if step == "proj":
                    while nxt <= arg + RING:
                        low_at(nxt)
                        nxt += 1
                elif step == "gates":
                    v_blocks(arg)
                elif step == "bu":
                    rotated_sum(pool, arg)
                elif step == "scan":
                    s = arg
                    pool.wait_ge(unrot_prod, s + 1)
                    pool.tensor_tensor(work[4], work[0], work[1], ALU.subtract).then_inc(xs_ready, 1)
                    pool.tensor_tensor(work[5], work[2], work[3], ALU.add).then_inc(xs_ready, 1)
            for n in range(nxt, N_UP0):
                low_at(n)
            with pool.Fori(0, JF // 2) as i:
                for b in range(2):
                    for e in range(2):
                        low(N_UP0 + 4 * i + 2 * b + e, e, 2 * b + e)
            with pool.Fori(0, 5) as i:
                for b in range(4):
                    low(N_DOWN0 + 4 * i + b, b % 2, b)
            for k in range(20, JF):
                low(N_DOWN0 + k, k % 2, k % 4)

        @block.scalar
        def _(act):
            chain = [0]

            def link(ins):
                chain[0] += 1
                ins.then_inc(act_step, 1)
                act.wait_ge(act_step, chain[0])

            act.dma_start(const[:], a["constants"]).then_inc(s_const, 16)
            act.wait_ge(vclear, 1)

            def row(r0, rows_n, src, c0=0, w=P):
                act.dma_start(vrows[r0:r0 + rows_n, c0:c0 + w], src).then_inc(s_vrows, 16)

            row(V_N1, 8, a["norm1_g"][0].rearrange("(k p) -> k p", p=P))
            row(V_N2, 8, a["norm2_g"][0].rearrange("(k p) -> k p", p=P))
            for t in range(4):
                row(V_CONV + 6 * t, 6, a["gdn_conv_w"][0, t].rearrange("(k p) -> k p", p=P))
            row(V_QN, 1, a["mla_q_norm_g"][:, 0:P])
            row(V_QN + 1, 1, a["mla_q_norm_g"][:, P:QLORA], w=QLORA - P)
            row(V_KVN, 1, a["mla_kv_norm_g"])
            row(V_GLUB, 2, a["s5_glu_b"][0].rearrange("(k p) -> k p", p=P))
            row(V_SD, 2, a["s5_d"][0].rearrange("(k g) c -> k (g c)", k=2))
            row(V_GN, 1, a["gdn_norm_g"], w=HD)
            row(V_GN, 1, a["gdn_norm_g"], c0=HD, w=HD)
            row(V_LRE, 8, a["s5_lam_re"][0].rearrange("(s g) n -> s (g n)", s=ST))
            row(V_LIM, 8, a["s5_lam_im"][0].rearrange("(s g) n -> s (g n)", s=ST))
            act.dma_start(ldt[V_LDT:V_LDT + 8, :], a["s5_log_dt"][0].rearrange("(s g) -> s g", s=ST)).then_inc(s_ldt, 16)
            row(V_DTB, 1, a["gdn_dt_bias"], c0=64, w=H)
            row(V_ALOG, 1, a["gdn_a_log"], w=H)
            act.wait_ge(vclear, 2)
            act.dma_start(taps_rows[0:88, 0, :], a["ffn_conv_w"][0, 0:2].rearrange("t (k p) -> (t k) p", p=P)).then_inc(s_taps, 16)
            act.dma_start(taps_rows[0:44, 1, :], a["ffn_conv_w"][0, 2].rearrange("(k p) -> k p", p=P)).then_inc(s_taps, 16)
            for r, name in enumerate(("s5_b_re", "s5_b_im")):
                act.dma_start(b_nat[:, r], a[name][0].rearrange("(s g) n c -> (g n) s c", s=ST)).then_inc(s_s5in, 16)
            for r, name in enumerate(("s5_c_re", "s5_c_im")):
                act.dma_start(c_nat[:, r], a[name][0].rearrange("(f g) c n -> (g c) f n", f=2)).then_inc(s_s5in, 16)

            act.wait_ge(s_const, 16)
            for t in range(TT):
                act.wait_ge(s_x[t], 16)
                link(act.activation(ps[:, 0:D], x_sb[:, t, :], ACT.Square, accum_out=small[:, t:t + 1]))
            act.wait_ge(cleared, 4)
            link(act.activation(small[:, 4:8], small[:, 0:4], ACT.Ln, scale=1.0 / D, bias=fixed[:, 0:1]))
            act.activation(small[:, 4:8], small[:, 4:8], ACT.Exp, scale=-0.5).then_inc(xsq, 1)

            def high(n, r, s, where=None):
                sem_, val = where or arrived(n)
                act.wait_ge(sem_, val)
                if not (isinstance(n, int) and n < RING):
                    act.wait_ge(w_used, n - RING + 1)
                act.activation(w_hi[:, s, :], w_raw[:, r, :], ACT.Copy).then_inc(w_h, 1)

            def high_at(n):
                high(n, n % RAW, slot(n))

            high_at(0)
            high_at(1)
            act.activation(ident16[:], ident, ACT.Copy).then_inc(masks16, 1)
            act.activation(causal16[:], C("causal"), ACT.Copy).then_inc(masks16, 1)
            act.wait_ge(vec_r, 1)
            for k in range(KD):
                act.wait_ge(hT_t, k + 1)
                act.activation(hT_hi[:, k, :], bank(HT_BANKS[k]), ACT.Copy,
                               scale=vec[:, V_N1 + k:V_N1 + k + 1]).then_inc(hT_h, 1)
            high_at(2)
            S = lambda k: s5p[:, k, :]
            act.activation(S(2), vec[:, V_LDT:V_LDT + 8], ACT.Exp).then_inc(s5_act, 1)
            act.wait_ge(s5_dve, 1)
            act.activation(S(9), S(3), ACT.Exp).then_inc(s5_act, 1)
            act.wait_ge(s5_dve, 2)
            act.activation(S(7), S(6), ACT.Sin).then_inc(s5_act, 1)
            act.activation(S(8), S(16), ACT.Sin).then_inc(s5_act, 1)
            def mix_high(pr):
                act.wait_ge(pv_done, 8 * (pr + 1))
                act.activation(hT_hi[:, 2 + pr, :], bank(MIX_BANK), ACT.Copy).then_inc(attmix_h, 1)

            nxt = 3
            COPY_TO = {"u0": su[0], "u1": su[1], "z0": gz[0], "z1": gz[1], "cq0": cq[0], "cq1": cq[1], "ckv": ckv,
                       "mq0": moq[0], "mq1": moq[1], "mk0": mok[0], "mk1": mok[1], "misc": misc}
            n_conv = 0
            for step, arg in ORDER:
                if step == "proj":
                    n = arg
                    name = PROJ[n][0]
                    act.wait_ge(w_used, n + 1)
                    if n in CONV_TILES:
                        p, j = int(name[1]), "qkv".index(name[0])
                        dst = (gq, gk, gv)[j][p]
                        col = V_CONV + 6 * 3 + 2 * j + p
                        act.activation(dst, bank(n % 2), ACT.Copy, scale=vec[:, col:col + 1]).then_inc(conv0, 1)
                    elif name.startswith("mv"):
                        p = int(name[2])
                        act.activation(mov[:, :, P * p:P * p + P], bank(n % 2).rearrange("p (t n) -> p t n", t=TT),
                                       ACT.Copy).then_inc(proj_copied, 1)
                    else:
                        act.activation(COPY_TO[name], bank(n % 2), ACT.Copy).then_inc(proj_copied, 1)
                    while nxt <= n + RING:
                        high_at(nxt)
                        nxt += 1
                elif step == "table" and arg == 0:
                    act.wait_ge(bc_t, 1)
                    act.activation(bt.rearrange("p r f n -> p (r f n)"), bank(6), ACT.Copy).then_inc(bc_ready, 1)
                    act.wait_ge(bc_t, 2)
                    act.activation(ct[:, 0].rearrange("p s n -> p (s n)"), bank(7, 256), ACT.Copy).then_inc(bc_ready, 1)
                    act.activation(ct[:, 1].rearrange("p s n -> p (s n)"), ps[:, 7 * L + 256:8 * L], ACT.Copy,
                                   scale=-1.0).then_inc(bc_ready, 1)
                elif step == "silu":
                    p = arg
                    for j, t in enumerate((gq[p], gk[p], gv[p])):
                        act.wait_ge(conv_done, 3 * p + j + 1)
                        act.activation(t, t, ACT.Silu).then_inc(silu_done, 1)
                elif step == "gnorm":
                    p = arg
                    act.wait_ge(silu_done, 3 * (p + 1))
                    if p:
                        act.wait_ge(gkk_used, 4 * p)
                        act.wait_ge(o_ps, NCH * p)
                    act.activation(flat(CP["DT"]), gq[p], ACT.Square).then_inc(gsq, 1)
                    act.activation(flat(CP["VP"]), gk[p], ACT.Square).then_inc(gsq, 1)
                    act.wait_ge(gss, 2 * p + 1)
                    link(act.activation(flat(CP["DT"]), bank(2), ACT.Ln, bias=fixed[:, 0:1]))
                    act.wait_ge(gss, 2 * p + 2)
                    link(act.activation(flat(CP["VP"]), bank(3), ACT.Ln, bias=fixed[:, 0:1]))
                    act.activation(flat(CP["DT"]), flat(CP["DT"]), ACT.Exp, scale=-0.5,
                                   bias=fixed[:, 1:2]).then_inc(grn, 1)
                    act.activation(flat(CP["VP"]), flat(CP["VP"]), ACT.Exp, scale=-0.5).then_inc(grn, 1)
                elif step == "rows":
                    act.wait_ge(proj_copied, freed_by[PN["misc"]][1])
                    act.activation(rA, misc[64:68, :], ACT.Identity, bias=vec[64:68, V_DTB:V_DTB + 1]).then_inc(row_act, 1)
                    act.activation(rC, misc[96:100, :], ACT.Tanh, scale=0.5).then_inc(row_act, 1)
                    act.activation(small[0:4, 0:1], vec[0:4, V_ALOG:V_ALOG + 1], ACT.Exp).then_inc(row_act, 1)
                    act.wait_ge(row_act, 1)
                    link(act.activation(rB, rA, ACT.Abs))
                    link(act.activation(rB, rB, ACT.Exp, scale=-1.0))
                    act.activation(rB, rB, ACT.Ln, bias=fixed[0:4, 2:3]).then_inc(row_act, 1)
                    act.wait_ge(row_dve, 2)
                    act.activation(rB, rows[0:4, :], ACT.Exp).then_inc(row_act, 1)
                    act.activation(rows[96:100, :], rD, ACT.Exp).then_inc(row_act, 1)
                elif step == "gates":
                    p = arg
                    act.wait_ge(gbc, 2 * p + 1)
                    act.activation(flat(CP["M1"]), bank(2), ACT.Exp).then_inc(egam, 1)
                    act.activation(glast, bank(2).rearrange("p (c i) -> p c i", c=NCH)[:, :, CH - 1], ACT.Exp).then_inc(egam, 1)
                    act.wait_ge(gnormed, 2 * p + 2)
                    kk = gk[p].rearrange("p (c i) -> p c i", c=NCH)
                    act.wait_ge(bd_cleared, 1)
                    if p:
                        act.wait_ge(o_ps, NCH * p)
                    for e in range(2):
                        act.activation(BD["KN"][64 * e:64 * e + 64, :, e, :], kk[64 * e:64 * e + 64], ACT.Copy).then_inc(knbd, 1)
                    act.wait_ge(dt_arg, p + 1)
                    act.activation(flat(CP["DT"]), flat(CP["DT"]), ACT.Exp).then_inc(dt_ready, 1)
                elif step in ("m1", "yt"):
                    if step == "yt" or arg[1]:
                        act.wait_ge(yt_ps, LEVELS * (arg if step == "yt" else arg[0]) + (LEVELS if step == "yt" else arg[1]))
                        for e in range(2):
                            act.activation(BD["Y"][64 * e:64 * e + 64, :, e, :], YT[:, :, CH * e:CH * e + CH],
                                           ACT.Copy).then_inc(y_ready_inv, 1)
                elif step == "guw":
                    p = arg
                    act.wait_ge(uw_ps, p + 1)
                    act.activation(flat(CP["VP"]), bank(4), ACT.Copy).then_inc(u_ready, 1)
                    act.activation(BD["KN"].rearrange("p c a i -> p (c a i)"), ps[:, 2 * L:4 * L], ACT.Copy).then_inc(wt_ready, 1)
                elif step == "gout":
                    p = arg
                    if p == 0:
                        for z in range(PAIRS):
                            act.wait_ge(proj_copied, freed_by[PN[f"z{z}"]][1])
                            act.activation(gz[z], gz[z], ACT.Silu).then_inc(z_ready, 1)
                    act.wait_ge(o_ps, NCH * (p + 1))
                    act.activation(flat(CP["M1"]), bank(2), ACT.Square).then_inc(o_sq, 1)
                    act.wait_ge(o_sum, p + 1)
                    link(act.activation(onorm[:, 1], onorm[:, 0], ACT.Ln, scale=1.0 / HD, bias=fixed[:, 0:1]))
                    act.activation(onorm[:, 1], onorm[:, 1], ACT.Exp, scale=-0.5).then_inc(o_fac, 1)
                elif step == "glu" and arg == 0:
                    for f in range(2):
                        act.wait_ge(yd_ready, f + 1)
                        act.activation(su[f], su[f], ACT.Gelu_apprx_tanh).then_inc(gelu_ready, 1)
                elif step == "glu":
                    for f in range(2):
                        act.wait_ge(glu_ps, f + 1)
                        act.activation(work[f].rearrange("p h t -> p (h t)"), bank(5 + f), ACT.Sigmoid,
                                       bias=vec[:, V_GLUB + f:V_GLUB + f + 1]).then_inc(glu_sig, 1)
                    act.wait_ge(w_used, NPROJ)
                    for f in range(2):
                        act.wait_ge(mix_tmp, f + 1)
                        act.activation(hT_hi[:, 6 + f, :], su[f], ACT.Copy).then_inc(s5mix_h, 1)
                elif step == "gmix":
                    p = arg
                    act.wait_ge(gout_done, p + 1)
                    act.wait_ge(w_used, NPROJ)
                    act.activation(hT_hi[:, p, :], gz[p], ACT.Copy).then_inc(gmix_h, 1)
                elif step == "mla" and arg == 0:
                    act.wait_ge(s5mix_l, 2)
                    act.activation(mrs[0], cq[0], ACT.Square).then_inc(mla_sq, 1)
                    act.activation(mrs[1][0:64], cq[1][0:64], ACT.Square).then_inc(mla_sq, 1)
                    act.activation(rope1, ckv, ACT.Square).then_inc(mla_sq, 1)
                    act.wait_ge(s_mlaw, 96)
                    for k, kr in ((0, P), (1, 64)):
                        w4 = wuq[0:kr, k, H * HD:H * MLA_QK].rearrange("p (h n) -> p h n", h=H)
                        sw = wuq[0:kr, k, H * MLA_QK:].rearrange("p (h n) -> p h n", h=H)
                        act.activation(sw[:, :, 0:16], w4[:, :, 16:32], ACT.Copy).then_inc(wswap, 1)
                        act.activation(sw[:, :, 16:32], w4[:, :, 0:16], ACT.Copy).then_inc(wswap, 1)
                    act.wait_ge(mla_ss, 1)
                    link(act.activation(mrs[0], bank(5), ACT.Ln, scale=1.0 / QLORA, bias=fixed[:, 0:1]))
                    act.wait_ge(mla_ss, 2)
                    link(act.activation(mrs[1], bank(6), ACT.Ln, scale=1.0 / KVLORA, bias=fixed[:, 0:1]))
                    act.activation(mrs[0], mrs[0], ACT.Exp, scale=-0.5).then_inc(mla_rn, 1)
                    act.activation(mrs[1], mrs[1], ACT.Exp, scale=-0.5).then_inc(mla_rn, 1)
                elif step == "mla" and arg == 1:
                    for pair in range(2):
                        act.wait_ge(mla_ps, 1 + pair)
                        b = MLA_BANKS[pair]
                        act.activation(q96[0:64, 2 * pair, :], bank(b)[0:64], ACT.Copy).then_inc(mla_ev, 1)
                        act.activation(q96[0:64, 2 * pair + 1, :], bank(b)[64:128], ACT.Copy).then_inc(mla_ev, 1)
                elif step == "mla":
                    for pair in range(2):
                        act.wait_ge(mla_ps, 5 + pair)
                        b = MLA_BANKS[4 + pair]
                        act.activation(k96[0:64, 2 * pair, :], bank(b)[0:64], ACT.Copy).then_inc(mla_ev, 1)
                        act.activation(k96[0:64, 2 * pair + 1, :], bank(b)[64:128], ACT.Copy).then_inc(mla_ev, 1)
                    act.wait_ge(krot, 1)
                    for h in range(1, H):
                        act.activation(k96[64:96, h, :], k96[64:96, 0, :], ACT.Copy).then_inc(kcopy, 1)
                    for m in range(2):
                        act.wait_ge(mla_ps, 7 + m)
                        act.activation(mlav[:, 2 * m:2 * m + 2, :].rearrange("p t n -> p (t n)"), bank(MLA_BANKS[6 + m]),
                                       ACT.Copy).then_inc(mla_ev, 1)
                elif step == "att":
                    u = arg
                    if u < 0:
                        act.wait_ge(w_l, N_OUT0 + RAW + 2)
                    if u + 1 < UNITS:
                        m, h, t = head_of(u + 1)
                        act.wait_ge(sc_max, u + 2)
                        if u >= 1:
                            act.wait_ge(pT_ps, u)
                        act.activation(prob[(u + 1) % 2][:, 0:P * (t + 1)], bank(5 + (u + 1) % 2, P * (t + 1)), ACT.Exp,
                                       bias=smx[:, 1, u + 1:u + 2], scale=SCALE[m],
                                       accum_out=smx[:, 2, u + 1:u + 2]).then_inc(p_exp, 1)
                    if 0 <= u < UNITS:
                        m, h, t = head_of(u)
                        act.wait_ge(pT_ps, u + 1)
                        if u >= 2:
                            act.wait_ge(pv_done, u - 1)
                        act.activation(probT[u % 2][:, 0:t + 1, :].rearrange("p k q -> p (k q)"),
                                       bank(transposed_bank(u), P * (t + 1)), ACT.Copy).then_inc(pT_ready, 1)
                    if u % 8 == 0 and u > 0:
                        mix_high(u // 8 - 1)

            for n in range(nxt, N_UP0):
                high_at(n)

            def up_split(i, b):
                for e in range(2):
                    n = N_UP0 + 4 * i + 2 * b + e
                    high(n, e, 2 * b + e, (w_loaded[e], 16 * (N_UP0 // 2 + 2 * i + b + 1) + EXTRA[e]))

            up_split(0, 0)
            for t in range(TT):
                act.wait_ge(x2_ready, t + 1)
                act.activation(junk, x_sb[:, t, :], ACT.Square, accum_out=stat[:, t:t + 1]).then_inc(x2_sq, 1)
                act.wait_ge(x2_sq, t + 1)
            link(act.activation(stat[:, 4:8], stat[:, 0:4], ACT.Ln, scale=1.0 / D, bias=fixed[:, 0:1]))
            act.activation(stat[:, 4:8], stat[:, 4:8], ACT.Exp, scale=-0.5).then_inc(x2_sq, 1)
            for k in range(KD):
                act.wait_ge(h2_t, k + 1)
                act.activation(hT_hi[:, k, :], bank(k), ACT.Copy, scale=vec[:, V_N2 + k:V_N2 + k + 1]).then_inc(h2_h, 1)

            def up_evac(i, b):
                j = 2 * i + b
                act.wait_ge(w_used, N_UP0 + 2 * j + 2)
                if not (isinstance(j, int) and j < 2):
                    act.wait_ge(g_ready, j - 1)
                for e in range(2):
                    act.activation(conv[2 * b + e], bank(2 * b + e), ACT.Copy,
                                   scale=taps[:, 2, e * JF + j, :]).then_inc(up_tap, 1)
                act.wait_ge(up_conv, 2 * j + 1)
                act.activation(conv[2 * b], conv[2 * b], ACT.Silu).then_inc(up_silu, 1)

            act.preload_act_table(ACT.Silu)
            up_split(0, 1)
            up_evac(0, 0)
            up_split(1, 0)
            up_evac(0, 1)
            up_split(1, 1)
            up_evac(1, 0)
            with act.Fori(2, JF // 2) as i:
                up_split(i, 0)
                up_evac(i - 1, 1)
                up_split(i, 1)
                up_evac(i, 0)

            def g_high(k, s):
                act.activation(hT_hi[:, s, :], g_sb[:, k, :], ACT.Copy).then_inc(g_h, 1)

            for k in range(2):
                high(N_DOWN0 + k, k, k, (w_loaded[k], 16 * (N_DOWN0 // 2 + 1) + EXTRA[k]))
            up_evac(JF // 2 - 1, 1)
            act.wait_ge(w_used, N_DOWN0)
            for k in range(4):
                if k == 0:
                    act.wait_ge(g_ready, JF)
                g_high(k, k)
                if k >= 2:
                    high(N_DOWN0 + k, k % 2, k, (w_loaded[k % 2], 16 * (N_DOWN0 // 2 + k // 2 + 1) + EXTRA[k % 2]))
            with act.Fori(1, 5) as i:
                for b in range(4):
                    act.wait_ge(w_used, N_DOWN0 + 4 * i + b - RING + 1)
                    g_high(4 * i + b, b)
                    high(N_DOWN0 + 4 * i + b, b % 2, b,
                         (w_loaded[b % 2], 16 * (N_DOWN0 // 2 + 2 * i + b // 2 + 1) + EXTRA[b % 2]))
            for k in range(20, JF):
                act.wait_ge(w_used, N_DOWN0 + k - RING + 1)
                g_high(k, k % 4)
                high(N_DOWN0 + k, k % 2, k % 4, (w_loaded[k % 2], 16 * (N_DOWN0 // 2 + k // 2 + 1) + EXTRA[k % 2]))
            for t in range(TT):
                act.wait_ge(x3_ready, t + 1)
                act.activation(junk, x_sb[:, t, :], ACT.Square, accum_out=stat[:, 8 + t:9 + t]).then_inc(x3_sq, 1)
                act.wait_ge(x3_sq, 2 * t + 1)
                link(act.activation(stat[:, 12 + t:13 + t], stat[:, 8 + t:9 + t], ACT.Ln, scale=1.0 / D, bias=fixed[:, 0:1]))
                act.activation(stat[:, 12 + t:13 + t], stat[:, 12 + t:13 + t], ACT.Exp, scale=-0.5).then_inc(x3_sq, 1)

        @block.vector
        def _(dve):
            chain = [0]

            def link(ins):
                chain[0] += 1
                ins.then_inc(dve_step, 1)
                dve.wait_ge(dve_step, chain[0])

            S = lambda k: s5p[:, k, :]
            for m, n in enumerate(bd_names):
                ins = dve.memset(BD[n].rearrange("p c a i -> p (c a i)"), 0.0)
            ins.then_inc(bd_cleared, 1)

            dve.wait_ge(vec_t, 1)
            dve.tensor_copy(vec[:], bank(2, V_ROWS)).then_inc(vec_r, 1)
            dve.wait_ge(vec_t, 3)
            dve.tensor_copy(taps[:].rearrange("p t j a -> p (t j a)"), bank(3, 6 * JF)).then_inc(vec_r, 1)
            dve.wait_ge(xsq, 1)
            for t in range(TT):
                dve.tensor_scalar(x_sb[:, t, :], x_sb[:, t, :], small[:, 4 + t:5 + t], None, ALU.mult).then_inc(xn, 1)
            dve.wait_ge(vec_r, 1)

            for k in range(KD):
                dve.wait_ge(hT_h, k + 1)
                dve.scalar_tensor_tensor(hT_lo[:, k, :], bank(HT_BANKS[k]), vec[:, V_N1 + k:V_N1 + k + 1],
                                         hT_hi[:, k, :].bitcast(F32), ALU.mult, ALU.subtract).then_inc(hT_l, 1)

            dve.tensor_scalar(S(0), vec[:, V_LRE:V_LRE + 8], -1e-4, None, ALU.min)
            link(dve.tensor_copy(S(1), vec[:, V_LIM:V_LIM + 8]))
            dve.wait_ge(s5_act, 1)
            dve.tensor_tensor(S(3), S(0), S(2), ALU.mult).then_inc(s5_dve, 1)
            link(dve.tensor_tensor(S(4), S(1), S(2), ALU.mult))
            link(dve.tensor_scalar(S(5), S(4), 1.0 / (2.0 * math.pi), ROUND, ALU.mult, ALU.add))
            link(dve.tensor_scalar(S(5), S(5), ROUND, None, ALU.subtract))
            src = S(4)
            for part in TWO_PI:
                link(dve.scalar_tensor_tensor(S(6), S(5), -part, src, ALU.mult, ALU.add))
                src = S(6)
            link(dve.tensor_scalar(S(6), S(6), math.pi, -math.pi, ALU.min, ALU.max))
            link(dve.scalar_tensor_tensor(S(16), S(6), -1.0, S(6), ALU.mult, ALU.max))
            dve.tensor_scalar(S(16), S(16), -1.0, math.pi / 2, ALU.mult, ALU.add).then_inc(s5_dve, 1)
            link(dve.tensor_tensor(S(12), S(0), S(0), ALU.mult))
            link(dve.tensor_tensor(S(13), S(1), S(1), ALU.mult))
            link(dve.tensor_tensor(S(12), S(12), S(13), ALU.add))
            link(dve.reciprocal(S(13), S(12)))
            dve.wait_ge(s5_act, 4)
            link(dve.tensor_tensor(S(10), S(9), S(8), ALU.mult))
            link(dve.tensor_tensor(S(11), S(9), S(7), ALU.mult))
            link(dve.tensor_scalar(S(10), S(10), 1.0, None, ALU.subtract))
            dve.tensor_tensor(S(14), S(10), S(0), ALU.mult)
            dve.tensor_tensor(S(17), S(11), S(1), ALU.mult)
            dve.tensor_tensor(S(15), S(11), S(0), ALU.mult)
            link(dve.tensor_tensor(S(18), S(10), S(1), ALU.mult))
            dve.tensor_tensor(S(14), S(14), S(17), ALU.add)
            link(dve.tensor_tensor(S(15), S(15), S(18), ALU.subtract))
            dve.tensor_tensor(S(14), S(14), S(13), ALU.mult)
            link(dve.tensor_tensor(S(15), S(15), S(13), ALU.mult))
            cr = S(14).unsqueeze(2).broadcast_to([P, ST, GW])
            ci = S(15).unsqueeze(2).broadcast_to([P, ST, GW])
            dve.wait_ge(s_s5in, 64)
            dve.tensor_tensor(bbar[:, 0], b_nat[:, 0], cr, ALU.mult)
            link(dve.tensor_tensor(btmp, b_nat[:, 1], ci, ALU.mult))
            link(dve.tensor_tensor(bbar[:, 0], bbar[:, 0], btmp, ALU.subtract))
            dve.tensor_tensor(bbar[:, 1], b_nat[:, 1], cr, ALU.mult)
            link(dve.tensor_tensor(btmp, b_nat[:, 0], ci, ALU.mult))
            link(dve.tensor_tensor(bbar[:, 1], bbar[:, 1], btmp, ALU.add))
            for r in range(2):
                for g in range(2):
                    dve.tensor_scalar(bbd[:, r, :, g, :], bbar[:, r], C("bmask", 1, off=g), None,
                                      ALU.mult).then_inc(bbd_ready, 1)
            for g in range(2):
                for r in range(2):
                    dve.tensor_scalar(cbd[:, r, :, g, :], c_nat[:, r], C("cmask", 1, off=g), None,
                                      ALU.mult).then_inc(cbd_ready, 1)

            def table_level(n):
                lo = slice(0, n)
                up = slice(n, 2 * n)
                cb = cosT[:, :, n - 1:n].broadcast_to([P, ST, n])
                sb_ = sinT[:, :, n - 1:n].broadcast_to([P, ST, n])
                t1 = wtmp[:, 0:ST * n].rearrange("p (s t) -> p s t", s=ST)
                t2 = wtmp[:, ST * n:2 * ST * n].rearrange("p (s t) -> p s t", s=ST)
                dve.tensor_tensor(cosT[:, :, up], cosT[:, :, lo], cb, ALU.mult)
                dve.tensor_tensor(t1, sinT[:, :, lo], sb_, ALU.mult)
                dve.tensor_tensor(sinT[:, :, up], sinT[:, :, lo], cb, ALU.mult)
                link(dve.tensor_tensor(t2, cosT[:, :, lo], sb_, ALU.mult))
                dve.tensor_tensor(cosT[:, :, up], cosT[:, :, up], t1, ALU.subtract)
                link(dve.tensor_tensor(sinT[:, :, up], sinT[:, :, up], t2, ALU.add))

            def conv_taps(p, j, m, n):
                dst = (gq, gk, gv)[j][p]
                dve.wait_ge(conv0, m + 1)
                for tap, back in ((2, 1), (1, 2), (0, 3)):
                    col = V_CONV + 6 * tap + 2 * j + p
                    ins = dve.scalar_tensor_tensor(dst[:, back:], bank(n % 2)[:, 0:L - back], vec[:, col:col + 1],
                                                   dst[:, back:], ALU.mult, ALU.add)
                    if back < 3:
                        link(ins)
                ins.then_inc(conv_done, 1)

            def y_plus_d(f):
                dve.wait_ge(y_ps, 4 * f + 4)
                dve.scalar_tensor_tensor(su[f], su[f], vec[:, V_SD + f:V_SD + f + 1], bank(7), ALU.mult,
                                         ALU.add).then_inc(yd_ready, 1)

            def mix_low(pr):
                dve.wait_ge(attmix_h, 1 + pr)
                dve.tensor_tensor(hT_lo[:, 2 + pr, :], bank(MIX_BANK), hT_hi[:, 2 + pr, :].bitcast(F32),
                                  ALU.subtract).then_inc(attmix_l, 1)

            def tokc(q, p, e=None):
                v = tok if e is None else tok[64 * e:64 * e + 64]
                return v[:, :, q, p:p + 1].broadcast_to([P if e is None else 64, NCH, CH])

            def half(t, e):
                return t[64 * e:64 * e + 64]

            def ps3(b):
                return bank(b).rearrange("p (c i) -> p c i", c=NCH)

            n_conv = 0
            n_state = 0
            for step, arg in ORDER:
                if step == "proj":
                    n = arg
                    name = PROJ[n][0]
                    if n in CONV_TILES:
                        conv_taps(int(name[1]), "qkv".index(name[0]), n_conv, n)
                        n_conv += 1
                elif step == "table":
                    if arg == 0:
                        dve.wait_ge(hT_t, KD)
                        dve.wait_ge(bc_t, 2)
                        dve.tensor_copy(cosT[:, :, 0], S(8))
                        link(dve.tensor_copy(sinT[:, :, 0], S(7)))
                        for l in range(6):
                            table_level(1 << l)
                    else:
                        table_level(1 << (5 + arg))
                elif step == "rows":
                    dve.wait_ge(row_act, 4)
                    dve.wait_ge(cleared, 1)
                    link(dve.scalar_tensor_tensor(rA, rA, 0.0, rB, ALU.max, ALU.add))
                    link(dve.tensor_scalar(rA, rA, small[0:4, 0:1], -1.0, ALU.mult, ALU.mult))
                    dve.tensor_scalar(rC, rC, 0.5, 0.5, ALU.mult, ALU.add).then_inc(dve_step, 1)
                    chain[0] += 1
                    dve.tensor_tensor_scan(rows[0:4, :], C("scanmask", lo=0, hi=4), rA, 0.0, ALU.mult, ALU.add).then_inc(row_dve, 1)
                    dve.wait_ge(dve_step, chain[0])
                    dve.tensor_copy(rows[32:36, :], rC)
                    dve.wait_ge(row_dve, 1)
                    gam = rows[0:4, :].rearrange("p (c i) -> p c i", c=NCH)
                    dve.tensor_tensor(rD.rearrange("p (c i) -> p c i", c=NCH), gam[:, :, CH - 1:CH].broadcast_to([4, NCH, CH]),
                                      gam, ALU.subtract).then_inc(row_dve, 1)
                    dve.wait_ge(row_act, 5)
                    dve.tensor_tensor(rows[64:68, :], rC, rB, ALU.mult).then_inc(row_dve, 1)
                elif step == "gates":
                    p = arg
                    dve.wait_ge(grn, 2 * p + 1)
                    dve.tensor_tensor(gq[p], gq[p], flat(CP["DT"]), ALU.mult).then_inc(gnormed, 1)
                    dve.wait_ge(grn, 2 * p + 2)
                    dve.tensor_tensor(gk[p], gk[p], flat(CP["VP"]), ALU.mult).then_inc(gnormed, 1)
                    if p == 0:
                        dve.wait_ge(tok_ps, 1)
                        dve.tensor_copy(tok.rearrange("p c q r -> p (c q r)"), bank(4, 8 * NCH)).then_inc(tok_ready, 1)
                        dve.wait_ge(tok_ready, 1)
                    dve.wait_ge(egam, 2 * p + 2)
                    dve.wait_ge(gnormed, 2 * p + 2)
                    link(dve.tensor_tensor(CP["DT"], ps3(2), tokc(0, p), ALU.subtract))
                    dve.scalar_tensor_tensor(CP["DT"], CP["DT"], 0.0, C("dmask").unsqueeze(1).broadcast_to([P, NCH, CH]),
                                             ALU.min, ALU.add).then_inc(dt_arg, 1)
                    for e in range(2):
                        dve.tensor_tensor(half(BD["QD"], e)[:, :, e, :], half(gq[p], e).rearrange("p (c i) -> p c i", c=NCH),
                                          half(CP["M1"], e), ALU.mult).then_inc(dve_step, 1)
                        chain[0] += 1
                    dve.wait_ge(dve_step, chain[0])
                    dve.wait_ge(gbc, 2 * p + 2)
                    dve.tensor_tensor(flat(CP["M1"]), gk[p], bank(3), ALU.mult).then_inc(gpre, 1)
                elif step == "gkk":
                    p = arg
                    dve.wait_ge(gkk, 3 * p + 2)
                    dve.wait_ge(dt_ready, p + 1)
                    for e in range(2):
                        ins = dve.tensor_tensor(half(BD["ATT"], e)[:, :, e, :], half(ps3(3), e), half(CP["DT"], e), ALU.mult)
                    ins.then_inc(gkk_used, 1)
                    for e in range(2):
                        ins = dve.tensor_tensor(half(BD["LT"], e)[:, :, e, :], half(ps3(2), e), half(CP["DT"], e), ALU.mult)
                    ins.then_inc(gkk_used, 1)
                    dve.wait_ge(gkk, 3 * p + 3)
                    for q, n in ((2, "KW"), (3, "KD")):
                        for e in range(2):
                            ins = dve.tensor_tensor(half(BD[n], e)[:, :, e, :], half(ps3(4), e), tokc(q, p, e), ALU.mult)
                        ins.then_inc(gkk_used, 1)
                    dve.wait_ge(gvt, p + 1)
                    dve.tensor_tensor(CP["VP"], ps3(2), tokc(1, p), ALU.mult).then_inc(vp_ready, 1)
                elif step == "m1":
                    p, l = arg
                    dve.wait_ge(m1_ps, LEVELS * p + l + 1)
                    mask = C("level", 64, off=64 * l).unsqueeze(1).broadcast_to([P, NCH, CH])
                    dve.tensor_tensor(CP["M1"], ps3(4), mask, ALU.mult).then_inc(m1_ready, 1)
                    if l == 0:
                        dve.wait_ge(m1_ready, LEVELS * p + 1)
                        dve.tensor_tensor(CP["X"], istack.unsqueeze(1).broadcast_to([P, NCH, CH]), CP["M1"],
                                          ALU.subtract).then_inc(x_ready, 1)
                elif step == "m2":
                    p, l = arg
                    dve.wait_ge(m2_ps, (LEVELS - 1) * p + l)
                    dve.tensor_tensor(CP["X"], CP["X"], ps3(4), ALU.subtract).then_inc(x_ready, 1)
                elif step == "grec":
                    p, c = arg
                    if c:
                        dve.wait_ge(ws_ps, 7 * p + c)
                        dve.wait_ge(u_ready, p + 1)
                        dve.tensor_tensor(vnew[:, c % 2, :], CP["VP"][:, c, :], bank(4, HD), ALU.subtract).then_inc(vnew_ready, 1)
                    if c < NCH - 1:
                        dve.wait_ge(kv_ps, 7 * p + c + 1)
                        kv = ps[:, 3 * L + HD * (c % 2):3 * L + HD * (c % 2) + HD]
                        if c == 0:
                            if p:
                                dve.wait_ge(o_ps, NCH * p)
                            dve.tensor_copy(state[:, 0, :], kv).then_inc(state_ready, 1)
                        else:
                            dve.wait_ge(o_ps, NCH * p + c)
                            dve.scalar_tensor_tensor(state[:, c % 2, :], state[:, 1 - c % 2, :], glast[:, c:c + 1], kv,
                                                     ALU.mult, ALU.add).then_inc(state_ready, 1)
                        n_state += 1
                        dve.wait_ge(state_ready, n_state)
                elif step == "gout":
                    p = arg
                    dve.wait_ge(o_sq, p + 1)
                    dve.reduce_sum(onorm[:, 0], CP["M1"], axis=AX.X).then_inc(o_sum, 1)
                    dve.wait_ge(o_fac, p + 1)
                    for e in range(2):
                        dve.tensor_tensor(half(BD["QD"], e)[:, :, e, :], half(ps3(2), e),
                                          half(onorm, e)[:, 1, :].unsqueeze(2).broadcast_to([64, NCH, HD]),
                                          ALU.mult).then_inc(o_norm, 1)
                elif step == "gouT":
                    p = arg
                    dve.wait_ge(oT_ps, p + 1)
                    dve.wait_ge(z_ready, p + 1)
                    dve.scalar_tensor_tensor(gz[p], bank(4), vec[:, V_GN:V_GN + 1], gz[p], ALU.mult,
                                             ALU.mult).then_inc(gout_done, 1)
                elif step == "bu":
                    s = arg
                    dve.wait_ge(bu_ps, s + 1)
                    if s:
                        dve.wait_ge(xs_ready, 2 * s)
                    c2 = cosT[:, s:s + 1, :].broadcast_to([P, 2, HALF])
                    s2 = sinT[:, s:s + 1, :].broadcast_to([P, 2, HALF])
                    bur = bank(5).rearrange("p (h t) -> p h t", h=2)
                    bui = bank(6).rearrange("p (h t) -> p h t", h=2)
                    dve.tensor_tensor(work[0], bur, c2, ALU.mult)
                    dve.tensor_tensor(work[1], bui, s2, ALU.mult)
                    dve.tensor_tensor(work[2], bui, c2, ALU.mult)
                    dve.tensor_tensor(work[3], bur, s2, ALU.mult).then_inc(rot_prod, 1)
                elif step == "scan":
                    s = arg
                    mag = S(9)[:, s:s + 1].broadcast_to([P, HALF])
                    for e in range(2):
                        dve.wait_ge(rot_sum, 2 * s + 1 + e)
                        dve.tensor_tensor_scan(work[6 + e][:, 0, :], mag, work[4 + e][:, 0, :], 0.0, ALU.mult, ALU.add).then_inc(dve_step, 1)
                        chain[0] += 1
                    dve.wait_ge(dve_step, chain[0])
                    ce, se = cosT[:, s, HALF - 1:HALF], sinT[:, s, HALF - 1:HALF]
                    wr, wi = work[6][:, 0, HALF - 1:HALF], work[7][:, 0, HALF - 1:HALF]
                    dve.tensor_tensor(s5c[:, 0:1], wi, se, ALU.mult)
                    link(dve.tensor_tensor(s5c[:, 1:2], wi, ce, ALU.mult))
                    dve.scalar_tensor_tensor(s5c[:, 2:3], wr, ce, s5c[:, 0:1], ALU.mult, ALU.subtract)
                    link(dve.scalar_tensor_tensor(s5c[:, 3:4], wr, se, s5c[:, 1:2], ALU.mult, ALU.add))
                    for e in range(2):
                        ins = dve.tensor_tensor_scan(work[6 + e][:, 1, :], mag, work[4 + e][:, 1, :], s5c[:, 2 + e:3 + e],
                                                     ALU.mult, ALU.add)
                    link(ins)
                    c2 = cosT[:, s:s + 1, :].broadcast_to([P, 2, HALF])
                    s2 = sinT[:, s:s + 1, :].broadcast_to([P, 2, HALF])
                    dve.tensor_tensor(work[0], work[6], c2, ALU.mult)
                    dve.tensor_tensor(work[1], work[7], s2, ALU.mult)
                    dve.tensor_tensor(work[2], work[6], s2, ALU.mult)
                    dve.tensor_tensor(work[3], work[7], c2, ALU.mult).then_inc(unrot_prod, 1)
                    if s == ST // 2:
                        y_plus_d(0)
                elif step == "glu" and arg == 0:
                    y_plus_d(1)
                elif step == "glu":
                    dve.wait_ge(w_used, NPROJ)
                    dve.wait_ge(glu_ps, 2)
                    for f in range(2):
                        dve.wait_ge(glu_sig, f + 1)
                        dve.tensor_tensor(su[f], su[f], work[f].rearrange("p h t -> p (h t)"), ALU.mult).then_inc(mix_tmp, 1)
                    for f in range(2):
                        dve.wait_ge(mix_tmp, f + 1)
                        dve.wait_ge(s5mix_h, f + 1)
                        dve.tensor_tensor(hT_lo[:, 6 + f, :], su[f], hT_hi[:, 6 + f, :].bitcast(F32), ALU.subtract).then_inc(s5mix_l, 1)
                elif step == "gmix":
                    p = arg
                    dve.wait_ge(gout_done, p + 1)
                    dve.wait_ge(gmix_h, p + 1)
                    dve.tensor_tensor(hT_lo[:, p, :], gz[p], hT_hi[:, p, :].bitcast(F32), ALU.subtract).then_inc(gmix_l, 1)
                elif step == "mla" and arg == 0:
                    for m, (t, g, f) in enumerate(((cq[0], V_QN, mrs[0]), (cq[1][0:64], V_QN + 1, mrs[0][0:64]), (ckv, V_KVN, mrs[1]))):
                        dve.wait_ge(mla_rn, 1 if m < 2 else 2)
                        n_ = t.shape[0]
                        dve.scalar_tensor_tensor(t, t, vec[0:n_, g:g + 1], f, ALU.mult, ALU.mult).then_inc(mla_n, 1)
                elif step == "mla" and arg == 1:
                    dve.wait_ge(mla_ps, 3)
                    dve.tensor_tensor(rope1, bank(MLA_BANKS[2]), C("ropec"), ALU.mult)
                    dve.wait_ge(mla_ps, 4)
                    link(dve.tensor_tensor(rope2, bank(MLA_BANKS[3]), C("ropes"), ALU.mult))
                    for h in range(H):
                        ins = dve.tensor_tensor(q96[64:96, h, :], rope1[32 * h:32 * h + 32], rope2[32 * h:32 * h + 32], ALU.add)
                    link(ins)
                    dve.tensor_tensor(rope1[0:32], misc[0:32], C("ropec", lo=0, hi=32), ALU.mult)
                    link(dve.tensor_tensor(rope2[0:32], misc[32:64], C("ropes", lo=32, hi=64), ALU.mult))
                    dve.tensor_tensor(k96[64:96, 0, :], rope1[0:32], rope2[0:32], ALU.add).then_inc(krot, 1)
                elif step == "att":
                    u = arg
                    if u + 1 < UNITS:
                        m, h, t = head_of(u + 1)
                        dve.wait_ge(sc_ps, u + 2)
                        link(dve.reduce_max(smx[:, 0, u + 1:u + 2], bank(5 + (u + 1) % 2, P * (t + 1)), axis=AX.X))
                        dve.tensor_scalar(smx[:, 1, u + 1:u + 2], smx[:, 0, u + 1:u + 2], -SCALE[m], None,
                                          ALU.mult).then_inc(sc_max, 1)
                    if 0 <= u < UNITS:
                        m, h, t = head_of(u)
                        dve.wait_ge(p_exp, u + 1)
                        link(dve.reciprocal(smx[:, 3, u:u + 1], smx[:, 2, u:u + 1]))
                        pr = prob[u % 2][:, 0:P * (t + 1)]
                        dve.tensor_scalar(pr, pr, smx[:, 3, u:u + 1], None, ALU.mult).then_inc(p_norm, 1)
                    if u % 8 == 0 and u > 0:
                        mix_low(u // 8 - 1)

            dve.wait_ge(w_used, N_UP0)
            for t in range(TT):
                dve.wait_ge(s_xre, 16 * TT)
                for hf in range(2):
                    xs = x_sb[:, t, L * hf:L * hf + L]
                    ins = dve.tensor_tensor(xs, xs, bank(2 * t + hf), ALU.add)
                ins.then_inc(x2_ready, 1)
            dve.wait_ge(x2_sq, TT + 1)
            dve.wait_ge(x2_ready, TT)
            for t in range(TT):
                dve.tensor_scalar(norm2[:, t, :], x_sb[:, t, :], stat[:, 4 + t:5 + t], None, ALU.mult).then_inc(n2_ready, 1)
            for k in range(KD):
                dve.wait_ge(h2_h, k + 1)
                dve.scalar_tensor_tensor(hT_lo[:, k, :], bank(k), vec[:, V_N2 + k:V_N2 + k + 1],
                                         hT_hi[:, k, :].bitcast(F32), ALU.mult, ALU.subtract).then_inc(h2_l, 1)

            def up(i, b):
                j = 2 * i + b
                for e in range(2):
                    t = conv[2 * b + e]
                    dve.wait_ge(up_tap, 2 * j + e + 1)
                    dve.scalar_tensor_tensor(t[:, 1:], bank(2 * b + e)[:, 0:L - 1], taps[:, 1, e * JF + j, :], t[:, 1:],
                                             ALU.mult, ALU.add).then_inc(up_mid, 1)
                    dve.wait_ge(up_mid, 2 * j + e + 1)
                    dve.scalar_tensor_tensor(t[:, 2:], bank(2 * b + e)[:, 0:L - 2], taps[:, 0, e * JF + j, :], t[:, 2:],
                                             ALU.mult, ALU.add).then_inc(up_conv, 1)
                dve.wait_ge(up_conv, 2 * j + 2)
                dve.wait_ge(up_silu, j + 1)
                dve.tensor_tensor(g_sb[:, j, :], conv[2 * b], conv[2 * b + 1], ALU.mult).then_inc(g_ready, 1)

            with dve.Fori(0, JF // 2) as i:
                for b in range(2):
                    up(i, b)

            def g_low(k, s):
                dve.wait_ge(g_h, k + 1)
                dve.tensor_tensor(hT_lo[:, s, :], g_sb[:, k, :], hT_hi[:, s, :].bitcast(F32), ALU.subtract).then_inc(g_l, 1)

            dve.wait_ge(g_ready, JF)
            with dve.Fori(0, 5) as i:
                for b in range(4):
                    g_low(4 * i + b, b)
            for k in range(20, JF):
                g_low(k, k % 4)
            dve.wait_ge(w_used, N_DOWN0 + JF)
            dve.wait_ge(s_fing, 16)
            for t in range(TT):
                for hf in range(2):
                    xs = x_sb[:, t, L * hf:L * hf + L]
                    ins = dve.tensor_tensor(xs, xs, bank(2 * t + hf), ALU.add)
                ins.then_inc(x3_ready, 1)
            for t in range(TT):
                dve.wait_ge(x3_sq, 2 * t + 2)
                dve.scalar_tensor_tensor(x_sb[:, t, :], x_sb[:, t, :], stat[:, 12 + t:13 + t], fing, ALU.mult,
                                         ALU.mult).then_inc(y_ready, 1)

        @block.tensor
        def _(pe):
            def mm(out, lhsT, rhs, start=True, stop=True):
                return pe.matmul(out, lhsT, rhs, start=start, stop=stop)

            pe.wait_ge(s_const, 16)
            pe.wait_ge(s_vrows, 16 * VROW_DMAS)
            pe.wait_ge(ldt_rows, 1)
            pe.transpose(bank(2, V_ROWS), vrows[0:V_ROWS, :], C("ident", V_ROWS, hi=V_ROWS)).then_inc(vec_t, 1)
            pe.wait_ge(s_taps, 32)
            pe.transpose(bank(3, 88), taps_rows[0:88, 0, :], C("ident", 88, hi=88)).then_inc(vec_t, 1)
            pe.transpose(ps[:, 3 * L + 88:3 * L + 132], taps_rows[0:44, 1, :], C("ident", 44, hi=44)).then_inc(vec_t, 1)
            pe.wait_ge(xn, TT)
            for k in range(KD):
                b = HT_BANKS[k]
                if b in (2, 3) and k < 4:
                    pe.wait_ge(vec_r, b - 1)
                if k >= 4:
                    pe.wait_ge(hT_l, k - 3)
                for t in range(TT):
                    ins = pe.transpose(ps[:, b * L + P * t:b * L + P * t + P], x_sb[:, t, P * k:P * k + P], ident)
                ins.then_inc(hT_t, 1)
            def split_products(out, lhs, rhs, first, last):
                ins = None
                for m, (l_, r_) in enumerate(((0, 0), (1, 0), (0, 1))):
                    ins = mm(out, lhs[l_], rhs[r_], start=first and m == 0, stop=last and m == 2)
                return ins

            def weights(s, cols=slice(0, D)):
                return w_hi[:, s, cols], w_lo[:, s, cols]

            def proj(n):
                s = slot(n)
                pe.wait_ge(w_l, n + 1)
                if n == 0:
                    pe.wait_ge(hT_l, KD)
                if n >= 2:
                    pe.wait_ge(*freed_by[n - 2])
                if PROJ[n][0].startswith("mv"):
                    for t in range(TT):
                        for k in range(KD):
                            tk = slice(P * t, P * t + P)
                            ins = split_products(bank(n % 2)[:, tk], (hT_hi[:, k, tk], hT_lo[:, k, tk]),
                                                 weights(s, slice(P * k, P * k + P)), k == 0, k == KD - 1)
                else:
                    for k in range(KD):
                        ins = split_products(bank(n % 2), weights(s, slice(P * k, P * k + P)),
                                             (hT_hi[:, k, :], hT_lo[:, k, :]), k == 0, k == KD - 1)
                ins.then_inc(w_used, 1)

            def col(b, c, w=CH):
                return ps[:, b * L + w * c:b * L + w * c + w]

            def s5_y(s):
                pe.wait_ge(xs_ready, 2 * s + 2)
                if s == 4:
                    pe.wait_ge(yd_ready, 1)
                if s == 0:
                    pe.wait_ge(bc_ready, 3)
                q = 32 * (s % 4)
                out = ps[q:q + 32, 7 * L:8 * L]
                mm(out, ct[:, 0, s, :], work[4].rearrange("p h t -> p (h t)"), True, False)
                mm(out, ct[:, 1, s, :], work[5].rearrange("p h t -> p (h t)"), False, True).then_inc(y_ps, 1)

            def inverse_transposed(p, l):
                pe.wait_ge(x_ready, LEVELS * p + l + 1)
                if l == 0:
                    pe.wait_ge(vp_ready, p + 1)
                for c in range(NCH):
                    ins = pe.transpose(YT[:, c, :], CP["X"][:, c], ident)
                ins.then_inc(yt_ps, 1)

            for step, arg in ORDER:
                if step == "proj":
                    proj(arg)
                elif step == "table" and arg == 0:
                    pe.wait_ge(bbd_ready, 4)
                    for r in range(2):
                        for f in range(2):
                            at = 6 * L + P * (2 * r + f)
                            ins = pe.transpose(ps[:, at:at + P], bbd[:, r, 4 * f:4 * f + 4].rearrange("p s g c -> p (s g c)"), ident)
                    ins.then_inc(bc_t, 1)
                    pe.wait_ge(cbd_ready, 4)
                    for r in range(2):
                        for f in range(2):
                            at = 7 * L + P * (2 * r + f)
                            ins = pe.transpose(ps[:, at:at + P], cbd[:, r, f].rearrange("p g n -> p (g n)"), ident)
                    ins.then_inc(bc_t, 1)
                elif step == "gnorm":
                    p = arg
                    if p:
                        pe.wait_ge(o_norm, 2 * p)
                    for m, t in enumerate(("DT", "VP")):
                        pe.wait_ge(gsq, 2 * p + m + 1)
                        mm(bank(2 + m), C("blockones"), flat(CP[t])).then_inc(gss, 1)
                elif step == "gates":
                    p = arg
                    pe.wait_ge(row_act, 6)
                    pe.wait_ge(row_dve, 3)
                    pe.wait_ge(grn, 2 * p + 2)
                    mm(bank(2), C("selbc", P, lo=0, hi=4, off=P * p), rows[0:4, :]).then_inc(gbc, 1)
                    mm(bank(3), C("selbc", P, lo=32, hi=36, off=P * p), rows[32:36, :]).then_inc(gbc, 1)
                    if p == 0:
                        for c in range(NCH):
                            for e in range(2):
                                ins = mm(ps[64 * e:64 * e + 64, 4 * L + 8 * c:4 * L + 8 * c + 8],
                                         rows[0:100, CH * c:CH * c + CH], C("seltok", 8, lo=0, hi=100, off=8 * e))
                        ins.then_inc(tok_ps, 1)
                elif step == "gkk":
                    p = arg
                    pe.wait_ge(knbd, 2 * (p + 1))
                    pe.wait_ge(gpre, p + 1)
                    pe.wait_ge(egam, 2 * (p + 1))
                    pe.wait_ge(tok_ready, 1)
                    if p:
                        pe.wait_ge(gout_done, p)
                    for c in range(NCH):
                        ins = mm(col(2, c), blocks(BD["KN"], c), CP["M1"][:, c])
                    ins.then_inc(gkk, 1)
                    for c in range(NCH):
                        ins = mm(col(3, c), blocks(BD["KN"], c), gq[p][:, CH * c:CH * c + CH])
                    ins.then_inc(gkk, 1)
                    for c in range(NCH):
                        ins = mm(col(4, c), blocks(BD["KN"], c), istack)
                    ins.then_inc(gkk, 1)
                    pe.wait_ge(vbd_ready, 2 * (p + 1))
                    pe.wait_ge(gkk_used, 4 * p + 2)
                    for c in range(NCH):
                        ins = mm(col(2, c), blocks(BD["Y"], c), istack)
                    ins.then_inc(gvt, 1)
                elif step == "m1":
                    p, l = arg
                    m = LEVELS * p + l
                    if l == 0:
                        pe.wait_ge(gkk_used, 4 * (p + 1))
                    else:
                        pe.wait_ge(x_ready, m)
                    for c in range(NCH):
                        ins = mm(col(4, c), blocks(BD["LT"], c), istack if l == 0 else CP["X"][:, c])
                    ins.then_inc(m1_ps, 1)
                    if l:
                        inverse_transposed(p, l - 1)
                elif step == "m2":
                    p, l = arg
                    m = LEVELS * p + l
                    pe.wait_ge(m1_ready, m + 1)
                    pe.wait_ge(y_ready_inv, 2 * m)
                    for c in range(NCH):
                        ins = mm(col(4, c), blocks(BD["Y"], c), CP["M1"][:, c])
                    ins.then_inc(m2_ps, 1)
                elif step == "yt":
                    inverse_transposed(arg, LEVELS - 1)
                elif step == "guw":
                    p = arg
                    m = 6 * p + 6
                    pe.wait_ge(y_ready_inv, 2 * m)
                    for c in range(NCH):
                        mm(col(4, c), blocks(BD["Y"], c), CP["VP"][:, c])
                    for c in range(NCH):
                        ins = mm(ps[:, 2 * L + P * c:2 * L + P * c + P], blocks(BD["KW"], c), blocks(BD["Y"], c))
                    ins.then_inc(uw_ps, 1)
                elif step == "grec":
                    p, c = arg
                    if c == 0:
                        pe.wait_ge(u_ready, p + 1)
                        pe.wait_ge(wt_ready, p + 1)
                        mm(col(3, 0), blocks(BD["KD"], 0), CP["VP"][:, 0]).then_inc(kv_ps, 1)
                        mm(col(2, 0), blocks(BD["ATT"], 0), CP["VP"][:, 0]).then_inc(o_ps, 1)
                    else:
                        pe.wait_ge(state_ready, 7 * p + c)
                        former = state[:, 1 - c % 2, :]
                        mm(col(4, 0), blocks(BD["KN"], c), former).then_inc(ws_ps, 1)
                        mm(col(2, c), blocks(BD["QD"], c), former, True, False)
                        pe.wait_ge(vnew_ready, 7 * p + c)
                        vn = vnew[:, c % 2, :]
                        if c < NCH - 1:
                            mm(col(3, c % 2), blocks(BD["KD"], c), vn).then_inc(kv_ps, 1)
                        mm(col(2, c), blocks(BD["ATT"], c), vn, False, True).then_inc(o_ps, 1)
                elif step == "gouT":
                    p = arg
                    pe.wait_ge(o_norm, 2 * (p + 1))
                    for c in range(NCH):
                        ins = mm(col(4, c), blocks(BD["QD"], c), istack)
                    ins.then_inc(oT_ps, 1)
                elif step == "bu":
                    s = arg
                    f, q = s // 4, 32 * (s % 4)
                    pe.wait_ge(proj_copied, freed_by[PN[f"u{f}"]][1])
                    pe.wait_ge(bc_ready, 3)
                    if s:
                        pe.wait_ge(rot_prod, s)
                    for r in range(2):
                        ins = mm(bank(5 + r), bt[q:q + 32, r, f, :], su[f][q:q + 32, :])
                    ins.then_inc(bu_ps, 1)
                    if s:
                        s5_y(s - 1)
                elif step == "glu" and arg == 0:
                    s5_y(ST - 1)
                elif step == "glu":
                    pe.wait_ge(gelu_ready, 2)
                    pe.wait_ge(s_glu, 16)
                    pe.wait_ge(rot_prod, ST)
                    for f in range(2):
                        mm(bank(5 + f), gluw[:, 0, P * f:P * f + P], su[0], True, False)
                        mm(bank(5 + f), gluw[:, 1, P * f:P * f + P], su[1], False, True).then_inc(glu_ps, 1)
                elif step == "mla" and arg == 0:
                    pe.wait_ge(glu_sig, 2)
                    pe.wait_ge(mla_sq, 2)
                    mm(bank(5), C("ones"), mrs[0], True, False)
                    mm(bank(5), C("ones", hi=64), mrs[1][0:64], False, True).then_inc(mla_ss, 1)
                    pe.wait_ge(mla_sq, 3)
                    mm(bank(6), C("ones"), rope1).then_inc(mla_ss, 1)
                elif step == "mla" and arg == 1:
                    pe.wait_ge(mla_n, 3)
                    pe.wait_ge(wswap, 4)
                    pe.wait_ge(yd_ready, 2)
                    pe.wait_ge(*freed_by[NPROJ - 2])
                    pe.wait_ge(*freed_by[NPROJ - 1])
                    for m in range(4):
                        b, cols = MLA_BANKS[m], slice(P * m, P * m + P)
                        mm(bank(b), wuq[:, 0, cols], cq[0], True, False)
                        mm(bank(b), wuq[0:64, 1, cols], cq[1][0:64], False, True).then_inc(mla_ps, 1)
                elif step == "mla":
                    for m in range(2):
                        if m:
                            pe.wait_ge(mla_ev, 2)
                        mm(bank(MLA_BANKS[4 + m]), wukv[:, P * m:P * m + P], ckv).then_inc(mla_ps, 1)
                    for m in range(2):
                        if m == 0:
                            pe.wait_ge(mla_ev, 4)
                        else:
                            pe.wait_ge(krot, 1)
                        for t in range(2):
                            b = MLA_BANKS[6 + m]
                            tk = P * (2 * m + t)
                            ins = mm(ps[:, b * L + 256 * t:b * L + 256 * t + 256], ckv[:, tk:tk + P], wukv[:, 256:512])
                        ins.then_inc(mla_ps, 1)
                elif step == "att":
                    def score(u):
                        m, h, t = head_of(u)
                        if u == 0:
                            pe.wait_ge(mla_ev, 10)
                            pe.wait_ge(krot, 1)
                            pe.wait_ge(kcopy, 3)
                            pe.wait_ge(masks16, 2)
                        if u >= 2:
                            pe.wait_ge(p_exp, u - 1)
                        b = 5 + u % 2
                        qs = slice(P * t, P * t + P)
                        if m == 0:
                            r = slice(64 * (h % 2), 64 * (h % 2) + 64)
                            q_, k_ = moq[h // 2][r, qs], mok[h // 2][r]
                        else:
                            q_, k_ = q96[0:96, h, qs], k96[0:96, h]
                        if t:
                            mm(bank(b, P * t), q_, k_[:, 0:P * t])
                        diag = ps[:, b * L + P * t:b * L + P * t + P]
                        mm(diag, q_, k_[:, qs], True, False)
                        mm(diag, ident16[:], causal16[:], False, True).then_inc(sc_ps, 1)

                    def pv(u):
                        m, h, t = head_of(u)
                        pe.wait_ge(pT_ready, u + 1)
                        if u % 8 == 0 and u:
                            pe.wait_ge(attmix_l, u // 8)
                        e = h % 2
                        v_ = mov if m == 0 else mlav
                        out = ps[64 * e:64 * e + 64, MIX_BANK * L + P * t:MIX_BANK * L + P * t + P]
                        for k in range(t + 1):
                            ins = mm(out, v_[:, k, HD * h:HD * h + HD], probT[u % 2][:, k, :], k == 0, k == t)
                        ins.then_inc(pv_done, 1)

                    u = arg
                    if u < 0:
                        score(0)
                        score(1)
                    elif u < UNITS:
                        m, h, t = head_of(u)
                        pe.wait_ge(p_norm, u + 1)
                        if u >= 2:
                            pe.wait_ge(pT_ready, u - 1)
                        for k in range(t + 1):
                            at = transposed_bank(u) * L + P * k
                            ins = pe.transpose(ps[:, at:at + P], prob[u % 2][:, P * k:P * k + P], ident)
                        ins.then_inc(pT_ps, 1)
                        if u + 2 < UNITS:
                            score(u + 2)
                        if u:
                            pv(u - 1)
                    else:
                        pv(UNITS - 1)

            def tokens_out(k, s, left, first, last):
                for t in range(TT):
                    tk = slice(P * t, P * t + P)
                    for hf in range(2):
                        ins = split_products(bank(2 * t + hf), (hT_hi[:, left, tk], hT_lo[:, left, tk]),
                                             weights(s, slice(L * hf, L * hf + L)), first, last)
                ins.then_inc(w_used, 1)

            pe.wait_ge(s5mix_l, 2)
            pe.wait_ge(attmix_l, 4)
            pe.wait_ge(gmix_l, PAIRS)
            for k in range(KD):
                pe.wait_ge(w_l, N_OUT0 + k + 1)
                tokens_out(k, slot(N_OUT0 + k), k, k == 0, k == KD - 1)
            pe.wait_ge(x2_ready, TT)
            pe.wait_ge(n2_ready, TT)
            for k in range(KD):
                for t in range(TT):
                    ins = pe.transpose(ps[:, k * L + P * t:k * L + P * t + P], norm2[:, t, P * k:P * k + P], ident)
                ins.then_inc(h2_t, 1)
            pe.wait_ge(h2_l, KD)

            def up(i, b):
                for e in range(2):
                    n = N_UP0 + 4 * i + 2 * b + e
                    pe.wait_ge(w_l, n + 1)
                    if not isinstance(i, int):
                        pe.wait_ge(up_conv, 4 * i + 2 * b + e - 3)
                    for k in range(KD):
                        ins = split_products(bank(2 * b + e), weights(2 * b + e, slice(P * k, P * k + P)),
                                             (hT_hi[:, k, :], hT_lo[:, k, :]), k == 0, k == KD - 1)
                    ins.then_inc(w_used, 1)

            for b in range(2):
                up(0, b)
            with pe.Fori(1, JF // 2) as i:
                for b in range(2):
                    up(i, b)

            def down(k, s):
                pe.wait_ge(w_l, N_DOWN0 + k + 1)
                pe.wait_ge(g_l, k + 1)
                tokens_out(k, s, s, isinstance(k, int) and k == 0, isinstance(k, int) and k == JF - 1)

            for k in range(4):
                down(k, k)
            with pe.Fori(1, 5) as i:
                for b in range(4):
                    down(4 * i + b, b)
            for k in range(20, JF):
                down(k, k % 4)


_INS = ["x", "norm1_g", "w_in", "gdn_conv_w", "gdn_a_log", "gdn_dt_bias", "gdn_norm_g", "mla_q_norm_g",
        "mla_w_uq", "mla_kv_norm_g", "mla_w_ukv", "s5_lam_re", "s5_lam_im", "s5_b_re", "s5_b_im",
        "s5_c_re", "s5_c_im", "s5_d", "s5_log_dt", "s5_glu_w", "s5_glu_b", "w_out", "norm2_g",
        "ffn_w_up", "ffn_conv_w", "ffn_w_down", "final_norm_g"]


def kernel(**inputs):
    import numpy as _np
    import concourse.bacc as _bacc
    from concourse import mybir as _mybir
    from concourse.bass_utils import run_bass_kernel_spmd as _run

    nc = _bacc.Bacc("TRN2", target_bir_lowering=False, num_devices=1)
    arrays, aps = {}, {}
    for name in _INS:
        arr = _np.ascontiguousarray(inputs[name])
        arrays[f"in_{name}"] = arr
        aps[name] = nc.dram_tensor(f"in_{name}", arr.shape, _mybir.dt.from_np(arr.dtype), kind="ExternalInput").ap()
    arrays["constants"] = constants()
    aps["constants"] = nc.dram_tensor("constants", (P, CONST_COLS), F32, kind="ExternalInput").ap()
    aps["out"] = nc.dram_tensor("out", (1, L, D), F32, kind="ExternalOutput").ap()
    hybrid_trunk(nc, aps)
    r = _run(nc, [arrays], core_ids=[0])
    return r.results[0]["out"]
```

```python
import math
from contextlib import ExitStack

import numpy as np

import concourse.bass as bass
from concourse import mybir

F32 = mybir.dt.float32
F32R = mybir.dt.float32r
BF16 = mybir.dt.bfloat16
ALU = mybir.AluOpType
ACT = mybir.ActivationFunctionType
AX = mybir.AxisListType

P = 128
L = 512
TT = L // P
D = 1024
KD = D // P
H = 4
HD = 64
PAIRS = H // 2
CH = 64
NCH = L // CH
QLORA, KVLORA, ROPE, MLA_QK = 192, 128, 32, 96
G, GW, NS = 16, 16, 64
ST = G * NS // P
HALF = L // 2
DFF = 2816
JF = DFF // P
EPS = 1e-6
BIG = 1e30
ROUND = 1.5 * 2.0 ** 23
TWO_PI = (6.28125, 1.9350051879882812e-3, 3.0199159819567529e-7)

A_Q, A_K, A_V, A_Z, A_A, A_B, M_Q, M_K, M_V, C_Q, C_KV, C_KR, S_U = (
    0, 256, 512, 768, 1024, 1028, 1032, 1288, 1544, 1800, 1992, 2120, 2152)

PROJ = [
    ("q0", [(0, A_Q, 128)]), ("k0", [(0, A_K, 128)]), ("v0", [(0, A_V, 128)]),
    ("misc", [(0, C_KR, 32), (32, C_KR + 16, 16), (48, C_KR, 16), (64, A_A, 32), (96, A_B, 32)]),
    ("u0", [(0, S_U, 128)]), ("u1", [(0, S_U + 128, 128)]),
    ("q1", [(0, A_Q + 128, 128)]), ("k1", [(0, A_K + 128, 128)]), ("v1", [(0, A_V + 128, 128)]),
    ("z0", [(0, A_Z, 128)]), ("z1", [(0, A_Z + 128, 128)]),
    ("cq0", [(0, C_Q, 128)]), ("cq1", [(0, C_Q + 128, 64)]), ("ckv", [(0, C_KV, 128)]),
    ("mq0", [(0, M_Q, 128)]), ("mk0", [(0, M_K, 128)]), ("mv0", [(0, M_V, 128)]),
    ("mq1", [(0, M_Q + 128, 128)]), ("mk1", [(0, M_K + 128, 128)]), ("mv1", [(0, M_V + 128, 128)]),
]
LEVELS = 6
UNITS = 2 * H * TT
PN = {name: n for n, (name, _) in enumerate(PROJ)}
NPROJ = len(PROJ)
N_OUT0 = NPROJ
N_UP0 = N_OUT0 + KD
N_DOWN0 = N_UP0 + 2 * JF
RING = 4
RAW = 2

V_N1, V_N2, V_CONV, V_QN, V_KVN, V_GLUB, V_SD, V_GN, V_LRE, V_LIM, V_LDT, V_DTB, V_ALOG, V_ROWS = (
    0, 8, 16, 40, 42, 43, 45, 47, 48, 56, 64, 72, 73, 74)

_CONSTS = [("ident", 128), ("istack", 64), ("blockones", 128), ("ones", 128), ("dmask", 64),
           ("level", 6 * 64), ("selbc", 2 * 128), ("seltok", 2 * 8), ("scanmask", L), ("ropec", L),
           ("ropes", L), ("bmask", 2), ("cmask", 2), ("causal", 128)]
CO, _at = {}, 0
for _n, _w in _CONSTS:
    CO[_n] = _at
    _at += _w
CONST_COLS = _at


def constants():
    c = np.zeros((P, CONST_COLS), np.float32)

    def put(name, a):
        c[:a.shape[0], CO[name]:CO[name] + a.shape[1]] = a

    r = np.arange(P)
    j, i = r[:, None] % CH, np.arange(CH)[None, :]
    put("ident", np.eye(P, dtype=np.float32))
    put("istack", (j == i).astype(np.float32))
    put("blockones", (r[:, None] // HD == r[None, :] // HD).astype(np.float32))
    put("ones", np.ones((P, P), np.float32))
    put("dmask", np.where(i >= j, 0.0, -BIG).astype(np.float32))
    for l in range(6):
        s = 1 << l
        m = (j > i) & (i // (2 * s) == j // (2 * s)) & (i // s != j // s)
        c[:, CO["level"] + 64 * l:CO["level"] + 64 * (l + 1)] = m
    for p in range(PAIRS):
        for a in range(2):
            h = 2 * p + a
            for base in (0, 32):
                c[base + h, CO["selbc"] + 128 * p + 64 * a:CO["selbc"] + 128 * p + 64 * (a + 1)] = 1.0
            for q in range(4):
                c[32 * q + h, CO["seltok"] + 8 * a + 2 * q + p] = 1.0
    put("scanmask", np.broadcast_to((np.arange(L) % CH != 0).astype(np.float32), (P, L)))
    freq = np.float32(10000.0) ** (-np.arange(0, ROPE, 2, dtype=np.float32) / np.float32(ROPE))
    ang = np.arange(L, dtype=np.float32)[None, :] * freq.astype(np.float32)[:, None]
    cos, sin = np.cos(ang).astype(np.float32), np.sin(ang).astype(np.float32)
    put("ropec", np.tile(np.concatenate([cos, cos]), (4, 1)))
    put("ropes", np.tile(np.concatenate([-sin, sin]), (4, 1)))
    gg = np.arange(2)[None, :]
    put("bmask", (r[:, None] // NS == gg).astype(np.float32))
    put("cmask", ((r[:, None] // GW) % 2 == gg).astype(np.float32))
    put("causal", np.where(r[None, :] <= r[:, None], 0.0, -BIG).astype(np.float32))
    return c


def hybrid_trunk(nc, a):
    ctx = ExitStack()
    with ctx:
        def sb(name, shape, dt=F32):
            return ctx.enter_context(nc.sbuf_tensor(name, shape, dt))

        def sem(name):
            return ctx.enter_context(nc.semaphore(name))

        x_sb = sb("x_sb", [P, TT, D])
        hT_hi = sb("hT_hi", [P, KD, L], F32R)
        hT_lo = sb("hT_lo", [P, KD, L], F32R)
        w_raw = sb("w_raw", [P, RAW, D])
        w_hi = sb("w_hi", [P, RING, D], F32R)
        w_lo = sb("w_lo", [P, RING, D], F32R)
        const = sb("const", [P, CONST_COLS])
        ident16 = sb("ident16", [P, P], BF16)
        causal16 = sb("causal16", [P, P], BF16)
        vrows = sb("vrows", [P, P])
        ldt = sb("ldt", [P, 2])
        vec = sb("vec", [P, V_ROWS])
        taps_rows = sb("taps_rows", [P, 2, P])
        taps = sb("taps", [P, 3, 2 * JF, 1])
        fixed = sb("fixed", [P, 4])
        small = sb("small", [P, 8])

        FREE = nc.sbuf_bytes_remaining // 4 - 64
        arena = sb("arena", [P, FREE])
        top = [0]
        spans = {}

        def take(name, n, at=None):
            start = top[0] if at is None else at
            if at is None:
                top[0] += n
            assert start + n <= FREE, (name, start + n, FREE)
            spans[name] = (start, n)
            return arena[:, start:start + n]

        gq = [take(f"gq{p}", L) for p in range(PAIRS)]
        gk = [take(f"gk{p}", L) for p in range(PAIRS)]
        gv = [take(f"gv{p}", L) for p in range(PAIRS)]
        gz = [take(f"gz{p}", L) for p in range(PAIRS)]
        misc = take("misc", L)
        bd_names = ["KN", "QD", "ATT", "LT", "Y", "KW", "KD"]
        BD = {n: take("bd" + n, 2 * L).rearrange("p (c a i) -> p c a i", c=NCH, a=2) for n in bd_names}
        cp_names = ["DT", "X", "M1", "VP"]
        CP = {n: take("cp" + n, L).rearrange("p (c i) -> p c i", c=NCH) for n in cp_names}
        rows = take("rows", L)
        tok = take("tok", NCH * 8).rearrange("p (c q r) -> p c q r", c=NCH, q=4)
        glast = take("glast", NCH)
        state = take("state", 2 * HD).rearrange("p (b v) -> p b v", b=2)
        vnew = take("vnew", 2 * HD).rearrange("p (b v) -> p b v", b=2)
        onorm = take("onorm", 2 * NCH).rearrange("p (b c) -> p b c", b=2)
        su = [take(f"su{f}", L) for f in range(2)]
        work = [take(f"work{n}", L).rearrange("p (h t) -> p h t", h=2) for n in range(8)]
        bt = take("bt", 4 * P).rearrange("p (r f n) -> p r f n", r=2, f=2)
        ct = take("ct", 2 * ST * 32).rearrange("p (r s n) -> p r s n", r=2, s=ST)
        s5p = take("s5p", 24 * ST).rearrange("p (k s) -> p k s", s=ST)
        s5c = take("s5c", 4)
        gluw = take("gluw", 512).rearrange("p (k n) -> p k n", k=2)
        moq = [take(f"moq{p}", L) for p in range(PAIRS)]
        mok = [take(f"mok{p}", L) for p in range(PAIRS)]
        mov = take("mov", TT * 256).rearrange("p (t n) -> p t n", t=TT)
        cq = [take(f"cq{f}", L) for f in range(2)]
        ckv = take("ckv", L)
        smx = take("smx", 4 * 32).rearrange("p (k u) -> p k u", k=4)

        b_nat = work[0].rearrange("p h t -> p (h t)")[:, 0:2 * P].rearrange("p (r s c) -> p r s c", r=2, s=ST)
        bbar = work[1].rearrange("p h t -> p (h t)")[:, 0:2 * P].rearrange("p (r s c) -> p r s c", r=2, s=ST)
        btmp = work[2].rearrange("p h t -> p (h t)")[:, 0:P].rearrange("p (s c) -> p s c", s=ST)
        bbd = work[3].rearrange("p h t -> p (h t)").rearrange("p (r s g c) -> p r s g c", r=2, s=ST, g=2)
        c_nat = work[4].rearrange("p h t -> p (h t)")[:, 0:4 * NS].rearrange("p (r f n) -> p r f n", r=2, f=2)
        cbd = work[5].rearrange("p h t -> p (h t)").rearrange("p (r f g n) -> p r f g n", r=2, f=2, g=2)

        xw = x_sb[:].rearrange("p t d -> p (t d)")
        cosT = xw[:, 0:ST * HALF].rearrange("p (s t) -> p s t", s=ST)
        sinT = xw[:, ST * HALF:2 * ST * HALF].rearrange("p (s t) -> p s t", s=ST)

        q96 = xw[:, 0:H * L].rearrange("p (h t) -> p h t", h=H)
        k96 = xw[:, H * L:2 * H * L].rearrange("p (h t) -> p h t", h=H)
        def works(n, m):
            at = spans[f"work{n}"][0]
            return arena[:, at:at + m * L]

        mlav = works(0, 2).rearrange("p (t n) -> p t n", t=TT)
        wuq = works(2, 2).rearrange("p (k n) -> p k n", k=2)
        rope2, wukv, rope1, mrs = works(4, 1), works(6, 1), works(7, 1), (gq[0], gk[0])
        prob = [w_raw[:, 0, L * b:L * b + L] for b in range(2)]
        probT = [w_raw[:, 1, L * b:L * b + L].rearrange("p (k q) -> p k q", k=TT) for b in range(2)]

        g_sb = take("g_sb", JF * L, at=0).rearrange("p (j t) -> p j t", j=JF)
        F0 = JF * L
        conv = [take(f"conv{b}", L, at=F0 + b * L) for b in range(4)]
        fing = take("fing", D, at=F0 + 4 * L)
        norm2 = take("norm2", TT * D, at=0).rearrange("p (t d) -> p t d", t=TT)
        junk = take("junk", D, at=F0 + 4 * L + D)
        stat = take("stat", 32, at=F0 + 4 * L + 2 * D)

        ps = ctx.enter_context(nc.psum_tensor("ps", [P, 8 * L], F32))

        def bank(b, n=L):
            return ps[:, b * L:b * L + n]

        s_x = [sem(f"x_loaded{t}") for t in range(TT)]
        s_const = sem("const_loaded")
        s_vrows = sem("vrows_loaded")
        s_taps = sem("taps_loaded")
        s_s5in = sem("s5_params_loaded")
        s_glu = sem("glu_w_loaded")
        s_mlaw = sem("mla_w_loaded")
        s_xre = sem("x_reloaded")
        s_fing = sem("final_gain_loaded")
        s_store = sem("stored")
        w_loaded = [sem(f"w_loaded{s}") for s in range(RING)]
        w_h = sem("w_high_ready")
        w_l = sem("w_low_ready")
        w_used = sem("w_used")
        act_step = sem("scalar_step")
        dve_step = sem("vector_step")
        cleared = sem("tiles_cleared")
        vclear = sem("vrows_cleared")
        masks16 = sem("bf16_masks_ready")
        vec_t = sem("vec_transposed")
        vec_r = sem("vec_ready")
        xsq = sem("x_squares")
        xn = sem("x_normed")
        hT_t = sem("h_transposed")
        hT_h = sem("h_high_ready")
        hT_l = sem("h_low_ready")
        proj_free = [sem(f"proj_bank_free{b}") for b in range(2)]
        conv0 = sem("conv_first_tap")
        conv_done = sem("conv_done")
        silu_done = sem("silu_done")
        gsq = sem("gdn_squares")
        gss = sem("gdn_square_sums")
        grn = sem("gdn_norm_factors")
        row_act = sem("rows_by_scalar")
        row_dve = sem("rows_by_vector")
        gbc = sem("gate_broadcast")
        tok_ps = sem("token_scalars_in_psum")
        tok_ready = sem("token_scalars_ready")
        egam = sem("exp_gamma_ready")
        gpre = sem("gdn_operands_ready")
        knbd = sem("kn_blocks_ready")
        vbd_ready = sem("v_blocks_ready")
        dt_arg = sem("decay_argument")
        dt_ready = sem("decay_ready")
        gkk = sem("gdn_kk_kq_ktok")
        gvt = sem("gdn_vtok")
        m1_ps = sem("m1_in_psum")
        m1_ready = sem("m1_ready")
        m2_ps = sem("m2_in_psum")
        x_ready = sem("inverse_ready")
        yt_ps = sem("inverse_transposed")
        uw_ps = sem("u_w_in_psum")
        u_ready = sem("u_ready")
        wt_ready = sem("wt_ready")
        ws_ps = sem("w_state_in_psum")
        vnew_ready = sem("v_new_ready")
        kv_ps = sem("k_v_in_psum")
        state_ready = sem("state_ready")
        o_ps = sem("gdn_o_in_psum")
        o_sq = sem("gdn_o_squared")
        o_sum = sem("gdn_o_sums")
        o_fac = sem("gdn_o_factor")
        o_norm = sem("gdn_o_normed")
        oT_ps = sem("gdn_o_transposed")
        mix_tmp = sem("mix_value_ready")
        s5_act = sem("s5_scalar_steps")
        s5_dve = sem("s5_vector_steps")
        bbd_ready = sem("s5_b_blocks_ready")
        cbd_ready = sem("s5_c_blocks_ready")
        bc_t = sem("s5_bc_transposed")
        bc_ready = sem("s5_bc_ready")
        bu_ps = sem("s5_bu_in_psum")
        rot_prod = sem("s5_rotated_products")
        rot_sum = sem("s5_rotated_sums")
        unrot_prod = sem("s5_unrotated_products")
        xs_ready = sem("s5_states_ready")
        y_ps = sem("s5_y_in_psum")
        yd_ready = sem("s5_y_plus_d")
        gelu_ready = sem("s5_gelu_ready")
        glu_ps = sem("glu_in_psum")
        glu_sig = sem("glu_sigmoid_ready")
        mla_sq = sem("mla_squares")
        mla_ss = sem("mla_square_sums")
        mla_rn = sem("mla_norm_factors")
        mla_n = sem("mla_normed")
        mla_ps = sem("mla_product_in_psum")
        mla_ev = sem("mla_product_used")
        krot = sem("rope_key_ready")
        kcopy = sem("rope_key_copied")
        sc_ps = sem("scores_in_psum")
        sc_max = sem("scores_max")
        p_exp = sem("prob_exp")
        p_norm = sem("prob_normed")
        pT_ps = sem("prob_transposed")
        pT_ready = sem("probT_ready")
        pv_done = sem("pv_done")
        x2_ready = sem("x2_ready")
        x2_sq = sem("x2_squares")
        n2_ready = sem("norm2_ready")
        h2_t = sem("h2_transposed")
        h2_h = sem("h2_high_ready")
        h2_l = sem("h2_low_ready")
        up_tap = sem("up_first_tap")
        up_conv = sem("up_conv_done")
        up_silu = sem("up_silu_done")
        g_ready = sem("g_ready")
        g_h = sem("g_high_ready")
        g_l = sem("g_low_ready")
        x3_ready = sem("x3_ready")
        x3_sq = sem("x3_squares")
        y_ready = sem("out_ready")
        proj_copied = sem("proj_copied")
        bd_cleared = sem("blocks_cleared")
        gkk_used = sem("gdn_kk_kq_ktok_used")
        gnormed = sem("gdn_qk_normed")
        wswap = sem("rope_columns_swapped")
        z_ready = sem("z_silu_ready")
        gout_done = sem("gdn_output_ready")
        vp_ready = sem("beta_v_ready")
        s5mix_h = sem("s5_mix_high")
        attmix_h = sem("attention_mix_high")
        gmix_h = sem("gdn_mix_high")
        s5mix_l = sem("s5_mix_low")
        attmix_l = sem("attention_mix_low")
        gmix_l = sem("gdn_mix_low")
        invT_ready = sem("inverse_transposed_ready")
        out_done = sem("out_product_token_tile_done")
        down_done = sem("down_product_token_tile_done")
        h2_used = sem("h2_tile_used")
        mv_t = sem("moba_v_transposed")
        mv_ready = sem("moba_v_ready")
        s_ldt = sem("log_dt_loaded")
        s_vrows2 = sem("vrows_loaded_by_pool")
        ldt_rows = sem("log_dt_rows_ready")
        up_mid = sem("up_second_tap")

        def C(name, w=None, lo=0, hi=P, off=0):
            w = w or dict(_CONSTS)[name]
            return const[lo:hi, CO[name] + off:CO[name] + off + w]

        ident = C("ident")
        istack = C("istack")

        w_in_v = a["w_in"][0].rearrange("(k p) n -> p k n", p=P)
        w_up_v = a["ffn_w_up"][0].rearrange("(k p) n -> p k n", p=P)
        w_out_v = a["w_out"][0].rearrange("(k p) n -> k p n", p=P)
        w_dn_v = a["ffn_w_down"][0].rearrange("(k p) n -> k p n", p=P)
        x_v = a["x"][0].rearrange("(t p) d -> t p d", p=P)
        y_v = a["out"][0].rearrange("(t p) d -> t p d", p=P)

        def wk(t, slot, w=P):
            return t[:, slot, :].rearrange("p (k n) -> p k n", k=KD)[:, :, 0:w]

        def flat4(t):
            return t.rearrange("p c i -> p (c i)")[0:4, :]

        HT_BANKS = [4, 5, 2, 3, 0, 1, 4, 5]
        YT = ps[0:64, 2 * L:4 * L].rearrange("p (c n) -> p c n", c=NCH)
        rA, rB, rC, rD = flat4(CP["X"]), flat4(CP["M1"]), moq[1][0:4, :], moq[0][0:4, :]

        def slot(n):
            return n % RING

        def arrived(n):
            extra = 16 * (len(PROJ[PN["misc"]][1]) - 1) if n % RAW == PN["misc"] % RAW and n >= PN["misc"] else 0
            return w_loaded[n % RAW], 16 * (n // RAW + 1) + extra

        EXTRA = [16 * (len(PROJ[PN["misc"]][1]) - 1) if r == PN["misc"] % RAW else 0 for r in range(RAW)]

        CONV_TILES = [PN[f"{t}{p}"] for p in range(PAIRS) for t in "qkv"]
        VALUE_TILES = [PN[f"mv{p}"] for p in range(PAIRS)]
        freed_by = {}
        for n in range(NPROJ):
            if n in CONV_TILES:
                freed_by[n] = (conv_done, sum(c <= n for c in CONV_TILES))
            else:
                freed_by[n] = (proj_copied, sum(m <= n and m not in CONV_TILES for m in range(NPROJ)))
        copied = dict(freed_by)
        for p, n in enumerate(VALUE_TILES):
            freed_by[n] = (mv_ready, p + 1)
        mvT = gv[0]

        def blocks(t, c):
            return t[:, c].rearrange("p a i -> p (a i)")

        def flat(t):
            return t.rearrange("p c i -> p (c i)")

        def inverse_steps(p):
            levels = [(step, (p, l)) for l in range(1, LEVELS) for step in ("m1", "m2")]
            return [("m1", (p, 0))] + levels + [("yt", p), ("guw", p)]

        def recurrence(p):
            return [("grec", (p, c)) for c in range(NCH)] + [("gout", p), ("gfac", p), ("gouT", p)]

        def woven(chain, fill):
            out = []
            for m, step in enumerate(chain):
                part = fill[len(fill) * m // len(chain):len(fill) * (m + 1) // len(chain)]
                if part:
                    out += part[0][0]
                out.append(step)
                for n, (before, after) in enumerate(part):
                    out += (before if n else []) + after
            return out

        def proj(*names):
            return [("proj", PN[n]) for n in names]

        ORDER = proj("q0", "k0") + [("table", 0)] + proj("v0") + [("silu", 0), ("gsq", 0)] + proj("misc")
        ORDER += [("rows", 0), ("gnorm", 0)] + proj("u0") + [("rows", 1), ("table", 1)] + proj("u1") + [("gates", 0)]
        ORDER += proj("q1") + [("table", 2)] + proj("k1") + [("gkk", 0)] + proj("v1") + [("silu", 1), ("gv", 0)]
        later = [[("proj", n)] for n in range(PN["z0"], NPROJ)]
        for p in range(PAIRS):
            later[PN[f"mv{p}"] - PN["z0"]].append(("mvt", p))
        later[1].append(("zsilu", 0))
        fill = []
        for s in range(ST):
            fill += [[("bu", s)], later.pop(0) + [("scan", s)]]
        ORDER += [("m1", (0, 0))] + fill.pop(0)
        ORDER += woven(inverse_steps(0)[1:] + recurrence(0)[:-1], [([], f) for f in fill])
        ORDER += later[0] + [("gouT", 0), ("gnorm", 1)] + later[1] + [("gates", 1)] + later[2]
        ORDER += [("gkk", 1), ("mla", 0), ("gv", 1), ("glu", 0)]
        ORDER.insert(ORDER.index(("gout", 0)) + 1, ("gsq", 1))
        fill = [([], f) for f in ([("mla_norm", 0), ("glu", 1)], [("mla", 1)], [("gmix", 0)], [("mla", 2)])]
        fill += [([], [("att_t", -1), ("att_s", -1)])]
        fill += [([("att_s", u)], [("att_t", u)]) for u in range(UNITS + 1)]
        cut = 18
        ORDER += woven(inverse_steps(1), fill[:cut]) + woven(recurrence(1), fill[cut:]) + [("gmix", 1)]

        MLA_BANKS = [5, 6, 7, 0, 1, 5, 6, 7]

        def head_of(u):
            return u // 16, (u // 4) % 4, u % 4

        SCALE = (HD ** -0.5, MLA_QK ** -0.5)

        MIX_BANK = 0
        MIX_ORDER = [6, 7, 0, 2, 3, 4, 1, 5]

        def transposed_bank(u):
            return (7, 1)[u % 2]

        wtmp = arena[:, spans["work0"][0]:spans["work0"][0] + 4 * L]

        VECTORS = [
            (V_N1, 8, a["norm1_g"][0].rearrange("(k p) -> k p", p=P)),
            (V_N2, 8, a["norm2_g"][0].rearrange("(k p) -> k p", p=P)),
            (V_CONV, 24, a["gdn_conv_w"][0].rearrange("t (k p) -> (t k) p", p=P)),
            (V_QN, 1, a["mla_q_norm_g"][:, 0:P]),
            (V_QN + 1, 1, a["mla_q_norm_g"][:, P:QLORA], 0, QLORA - P),
            (V_KVN, 1, a["mla_kv_norm_g"]),
            (V_GLUB, 2, a["s5_glu_b"][0].rearrange("(k p) -> k p", p=P)),
            (V_SD, 2, a["s5_d"][0].rearrange("(k g) c -> k (g c)", k=2)),
            (V_GN, 1, a["gdn_norm_g"], 0, HD),
            (V_GN, 1, a["gdn_norm_g"], HD, HD),
            (V_LRE, 8, a["s5_lam_re"][0].rearrange("(s g) n -> s (g n)", s=ST)),
            (V_LIM, 8, a["s5_lam_im"][0].rearrange("(s g) n -> s (g n)", s=ST)),
            (V_DTB, 1, a["gdn_dt_bias"], 64, H),
            (V_ALOG, 1, a["gdn_a_log"], 0, H),
        ]

        def rows_from(queue, first, last, loaded=s_vrows):
            for r0, rows_n, src, *at in VECTORS[first:last]:
                c0, w = at or (0, P)
                queue.dma_start(vrows[r0:r0 + rows_n, c0:c0 + w], src).then_inc(loaded, 16)

        block = ctx.enter_context(nc.Block())

        @block.sync
        def _(sp):
            for t in range(TT):
                sp.dma_start(x_sb[:, t, :], x_v[t]).then_inc(s_x[t], 16)
            sp.dma_start(const[:], a["constants"]).then_inc(s_const, 16)

            def load(n, r, dst, src):
                if n is not None and not (isinstance(n, int) and n < RAW):
                    sp.wait_ge(w_l, n - RAW + 1)
                sp.dma_start(dst, src).then_inc(w_loaded[r], 16)

            def load_proj(n):
                r = n % RAW
                for m, (at, col, width) in enumerate(PROJ[n][1]):
                    load(n if m == 0 else None, r, wk(w_raw, r)[:, :, at:at + width],
                         w_in_v[:, :, col:col + width])

            def load_out(k):
                load(N_OUT0 + k, (N_OUT0 + k) % RAW, w_raw[:, (N_OUT0 + k) % RAW, :], w_out_v[MIX_ORDER[k]])

            def load_up(i, b, e):
                load(N_UP0 + 4 * i + 2 * b + e, e, wk(w_raw, e),
                     w_up_v[:, :, bass.ds((2 * i + b) * P + e * DFF, P)])

            def load_down(k, r):
                load(N_DOWN0 + k, r, w_raw[:, r, :], w_dn_v[k])

            for n in range(2):
                load_proj(n)
            sp.wait_ge(vclear, 1)
            rows_from(sp, 4, 9)
            for n in range(2, NPROJ):
                load_proj(n)
                if n == PN["u0"]:
                    sp.dma_start(gluw, a["s5_glu_w"][0].rearrange("(k p) n -> p k n", p=P)).then_inc(s_glu, 16)
            load_out(0)
            load_out(1)
            sp.wait_ge(xs_ready, 2 * ST)
            uq_v = a["mla_w_uq"][0].rearrange("r (h n) -> r h n", h=H)
            for k, r0, r1 in ((0, 0, P), (1, P, QLORA)):
                for c0, c1 in ((0, HD), (HD, MLA_QK)):
                    sp.dma_start(wuq[0:r1 - r0, k, H * c0:H * c1].rearrange("p (h n) -> p h n", h=H),
                                 uq_v[r0:r1, :, c0:c1]).then_inc(s_mlaw, 16)
            ukv_v = a["mla_w_ukv"][0].rearrange("r (h n) -> r h n", h=H)
            for c in range(2):
                sp.dma_start(wukv[:, 256 * c:256 * c + 256].rearrange("p (h n) -> p h n", h=H),
                             ukv_v[:, :, HD * c:HD * c + HD]).then_inc(s_mlaw, 16)
            load_out(2)
            load_out(3)
            sp.wait_ge(pv_done, UNITS)
            for k in range(4, KD):
                load_out(k)
                if k == 5:
                    for t in range(TT):
                        sp.dma_start(x_sb[:, t, :], x_v[t]).then_inc(s_xre, 16)
            for b in range(2):
                for e in range(2):
                    load_up(0, b, e)
            sp.wait_ge(w_used, N_UP0)
            sp.dma_start(fing, a["final_norm_g"].rearrange("(a n) -> a n", a=1).broadcast_to([P, D])).then_inc(s_fing, 16)
            with sp.Fori(1, JF // 2) as i:
                for b in range(2):
                    for e in range(2):
                        load_up(i, b, e)
            with sp.Fori(0, 5) as i:
                for b in range(4):
                    load_down(4 * i + b, b % 2)
            for k in range(20, JF):
                load_down(k, k % 2)
            for t in range(TT):
                sp.wait_ge(y_ready, t + 1)
                sp.dma_start(y_v[t], x_sb[:, t, :]).then_inc(s_store, 16)
            sp.wait_ge(s_store, 16 * TT)

        def rotated_sum(pool, s):
            pool.wait_ge(rot_prod, s + 1)
            if s:
                pool.wait_ge(y_ps, s)
            pool.tensor_tensor(work[4], work[0], work[1], ALU.add).then_inc(rot_sum, 1)
            pool.tensor_tensor(work[5], work[2], work[3], ALU.subtract).then_inc(rot_sum, 1)

        @block.gpsimd
        def _(pool):
            pool.memset(vrows[:], 0.0).then_inc(vclear, 1)
            pool.memset(taps_rows[:], 0.0).then_inc(vclear, 1)
            pool.memset(rows, 0.0).then_inc(cleared, 1)
            pool.memset(fixed[:, 0:1], EPS).then_inc(cleared, 1)
            pool.memset(fixed[:, 1:2], math.log(HD ** -0.5)).then_inc(cleared, 1)
            pool.memset(fixed[:, 2:3], 1.0).then_inc(cleared, 1)

            pool.wait_ge(vclear, 2)
            pool.dma_start(ldt[V_LDT:V_LDT + 8, :], a["s5_log_dt"][0].rearrange("(s g) -> s g", s=ST)).then_inc(s_ldt, 16)
            rows_from(pool, 9, len(VECTORS), s_vrows2)
            pool.dma_start(taps_rows[0:88, 0, :], a["ffn_conv_w"][0, 0:2].rearrange("t (k p) -> (t k) p", p=P)).then_inc(s_taps, 16)
            pool.dma_start(taps_rows[0:44, 1, :], a["ffn_conv_w"][0, 2].rearrange("(k p) -> k p", p=P)).then_inc(s_taps, 16)
            def low(n, r, s):
                pool.wait_ge(w_h, n + 1)
                pool.tensor_tensor(w_lo[:, s, :], w_raw[:, r, :], w_hi[:, s, :].bitcast(F32),
                                   ALU.subtract).then_inc(w_l, 1)

            def low_at(n):
                low(n, n % RAW, slot(n))

            pool.wait_ge(cleared, 4)
            pool.wait_ge(s_ldt, 16)
            pool.tensor_scalar(vrows[V_LDT:V_LDT + 8, :].rearrange("s (g n) -> s g n", g=2),
                               ldt[V_LDT:V_LDT + 8, :].unsqueeze(2).broadcast_to([ST, 2, NS]), 1.0, 0.0,
                               ALU.mult, ALU.add).then_inc(ldt_rows, 1)
            for r, name in enumerate(("s5_b_re", "s5_b_im")):
                pool.dma_start(b_nat[:, r], a[name][0].rearrange("(s g) n c -> (g n) s c", s=ST)).then_inc(s_s5in, 16)
            for r, name in enumerate(("s5_c_re", "s5_c_im")):
                pool.dma_start(c_nat[:, r], a[name][0].rearrange("(f g) c n -> (g c) f n", f=2)).then_inc(s_s5in, 16)

            pool.wait_ge(ldt_rows, 1)
            for n in range(3):
                low_at(n)
            nxt = 3

            def v_blocks(p):
                pool.wait_ge(silu_done, 3 * (p + 1))
                if p:
                    pool.wait_ge(uw_ps, p)
                vv = gv[p].rearrange("p (c i) -> p c i", c=NCH)
                pool.wait_ge(bd_cleared, 1)
                for e in range(2):
                    pool.tensor_scalar(BD["Y"][64 * e:64 * e + 64, :, e, :], vv[64 * e:64 * e + 64], 1.0, 0.0,
                                       ALU.mult, ALU.add).then_inc(vbd_ready, 1)
                    pool.wait_ge(vbd_ready, 2 * p + e + 1)

            for step, arg in ORDER:
                if step == "proj":
                    while nxt <= arg + RING:
                        low_at(nxt)
                        nxt += 1
                elif step == "gsq":
                    p = arg
                    if p:
                        pool.wait_ge(gkk_used, 4 * p)
                        pool.wait_ge(o_ps, NCH * p)
                    for m, (f, t) in enumerate((("DT", gq[p]), ("VP", gk[p]))):
                        pool.wait_ge(silu_done, 3 * p + m + 1)
                        pool.tensor_tensor(flat(CP[f]), t, t, ALU.mult).then_inc(gsq, 1)
                elif step == "gkk":
                    v_blocks(arg)
                elif step == "bu":
                    rotated_sum(pool, arg)
            for n in range(nxt, N_UP0):
                low_at(n)
            with pool.Fori(0, JF // 2) as i:
                for b in range(2):
                    for e in range(2):
                        low(N_UP0 + 4 * i + 2 * b + e, e, 2 * b + e)
            with pool.Fori(0, 5) as i:
                for b in range(4):
                    low(N_DOWN0 + 4 * i + b, b % 2, b)
            for k in range(20, JF):
                low(N_DOWN0 + k, k % 2, k % 4)

        @block.scalar
        def _(act):
            chain = [0]

            def link(ins):
                chain[0] += 1
                ins.then_inc(act_step, 1)
                act.wait_ge(act_step, chain[0])

            act.wait_ge(vclear, 1)

            rows_from(act, 0, 4)
            def use_ln_exp():
                act.preload_act_table_set("natural_log_exp_and_others")

            use_ln_exp()
            act.wait_ge(cleared, 4)
            for t in range(TT):
                act.wait_ge(s_x[t], 16)
                link(act.activation(ps[:, 0:D], x_sb[:, t, :], ACT.Square, accum_out=small[:, t:t + 1]))
            act.wait_ge(cleared, 4)
            link(act.activation(small[:, 4:8], small[:, 0:4], ACT.Ln, scale=1.0 / D, bias=fixed[:, 0:1]))
            act.activation(small[:, 4:8], small[:, 4:8], ACT.Exp, scale=-0.5).then_inc(xsq, 1)

            def high(n, r, s, where=None):
                sem_, val = where or arrived(n)
                act.wait_ge(sem_, val)
                if not (isinstance(n, int) and n < RING):
                    act.wait_ge(w_used, n - RING + 1)
                act.activation(w_hi[:, s, :], w_raw[:, r, :], ACT.Copy).then_inc(w_h, 1)

            def high_at(n):
                high(n, n % RAW, slot(n))

            high_at(0)
            high_at(1)
            act.wait_ge(s_const, 16)
            act.activation(ident16[:], ident, ACT.Copy).then_inc(masks16, 1)
            act.activation(causal16[:], C("causal"), ACT.Copy).then_inc(masks16, 1)
            act.wait_ge(vec_r, 1)
            for k in range(KD):
                act.wait_ge(hT_t, k + 1)
                act.activation(hT_hi[:, k, :], bank(HT_BANKS[k]), ACT.Copy,
                               scale=vec[:, V_N1 + k:V_N1 + k + 1]).then_inc(hT_h, 1)
            high_at(2)
            S = lambda k: s5p[:, k, :]
            act.activation(S(2), vec[:, V_LDT:V_LDT + 8], ACT.Exp).then_inc(s5_act, 1)
            act.wait_ge(s5_dve, 1)
            act.activation(S(9), S(3), ACT.Exp).then_inc(s5_act, 1)
            act.wait_ge(s5_dve, 2)
            act.activation(S(7), S(6), ACT.Sin).then_inc(s5_act, 1)
            act.activation(S(8), S(16), ACT.Sin).then_inc(s5_act, 1)
            def mix_high(pr):
                act.wait_ge(pv_done, 8 * (pr + 1))
                act.activation(hT_hi[:, 2 + pr, :], bank(MIX_BANK), ACT.Copy).then_inc(attmix_h, 1)

            nxt = 3
            COPY_TO = {"u0": su[0], "u1": su[1], "z0": gz[0], "z1": gz[1], "cq0": cq[0], "cq1": cq[1], "ckv": ckv,
                       "mq0": moq[0], "mq1": moq[1], "mk0": mok[0], "mk1": mok[1], "misc": misc}
            for step, arg in ORDER:
                if step == "proj":
                    n = arg
                    name = PROJ[n][0]
                    act.wait_ge(w_used, n + 1)
                    if n in CONV_TILES:
                        p, j = int(name[1]), "qkv".index(name[0])
                        dst = (gq, gk, gv)[j][p]
                        col = V_CONV + 6 * 3 + 2 * j + p
                        act.activation(dst, bank(n % 2), ACT.Copy, scale=vec[:, col:col + 1]).then_inc(conv0, 1)
                    elif n in VALUE_TILES:
                        if n == VALUE_TILES[0]:
                            act.wait_ge(vbd_ready, 2)
                        else:
                            act.wait_ge(mv_t, 1)
                        act.activation(mvT, bank(n % 2), ACT.Copy).then_inc(proj_copied, 1)
                    else:
                        act.activation(COPY_TO[name], bank(n % 2), ACT.Copy).then_inc(proj_copied, 1)
                    while nxt <= n + RING:
                        high_at(nxt)
                        nxt += 1
                elif step == "table" and arg == 0:
                    act.wait_ge(bc_t, 1)
                    act.activation(bt.rearrange("p r f n -> p (r f n)"), bank(6), ACT.Copy).then_inc(bc_ready, 1)
                    act.wait_ge(bc_t, 2)
                    act.activation(ct[:, 0].rearrange("p s n -> p (s n)"), bank(7, 256), ACT.Copy).then_inc(bc_ready, 1)
                    act.activation(ct[:, 1].rearrange("p s n -> p (s n)"), ps[:, 7 * L + 256:8 * L], ACT.Copy,
                                   scale=-1.0).then_inc(bc_ready, 1)
                elif step == "silu":
                    p = arg
                    act.preload_act_table(ACT.Silu)
                    for j, t in enumerate((gq[p], gk[p], gv[p])):
                        act.wait_ge(conv_done, 3 * p + j + 1)
                        act.activation(t, t, ACT.Silu).then_inc(silu_done, 1)
                elif step == "gnorm":
                    p = arg
                    use_ln_exp()
                    act.wait_ge(gss, 2 * p + 1)
                    link(act.activation(flat(CP["DT"]), bank(2), ACT.Ln, bias=fixed[:, 0:1]))
                    act.wait_ge(gss, 2 * p + 2)
                    link(act.activation(flat(CP["VP"]), bank(3), ACT.Ln, bias=fixed[:, 0:1]))
                    act.activation(flat(CP["DT"]), flat(CP["DT"]), ACT.Exp, scale=-0.5,
                                   bias=fixed[:, 1:2]).then_inc(grn, 1)
                    act.activation(flat(CP["VP"]), flat(CP["VP"]), ACT.Exp, scale=-0.5).then_inc(grn, 1)
                elif step == "zsilu":
                    for z in range(PAIRS):
                        act.wait_ge(proj_copied, freed_by[PN[f"z{z}"]][1])
                        act.activation(gz[z], gz[z], ACT.Silu).then_inc(z_ready, 1)
                    use_ln_exp()
                elif step == "mvt":
                    act.wait_ge(mv_t, arg + 1)
                    act.activation(mov[:, :, P * arg:P * arg + P],
                                   bank(VALUE_TILES[arg] % 2).rearrange("p (t n) -> p t n", t=TT),
                                   ACT.Copy).then_inc(mv_ready, 1)
                elif step == "rows" and arg == 0:
                    act.wait_ge(proj_copied, freed_by[PN["misc"]][1])
                    act.activation(rA, misc[64:68, :], ACT.Identity, bias=vec[64:68, V_DTB:V_DTB + 1]).then_inc(row_act, 1)
                    act.activation(rC, misc[96:100, :], ACT.Tanh, scale=0.5).then_inc(row_act, 1)
                    act.wait_ge(row_act, 1)
                    link(act.activation(rB, rA, ACT.Abs))
                    use_ln_exp()
                    act.activation(small[0:4, 0:1], vec[0:4, V_ALOG:V_ALOG + 1], ACT.Exp).then_inc(row_act, 1)
                    link(act.activation(rB, rB, ACT.Exp, scale=-1.0))
                    act.activation(rB, rB, ACT.Ln, bias=fixed[0:4, 2:3]).then_inc(row_act, 1)
                elif step == "rows":
                    act.wait_ge(row_dve, 2)
                    act.activation(rB, rows[0:4, :], ACT.Exp).then_inc(row_act, 1)
                    act.activation(rows[96:100, :], rD, ACT.Exp).then_inc(row_act, 1)
                elif step == "gates":
                    p = arg
                    act.wait_ge(gbc, 2 * p + 1)
                    act.activation(flat(CP["M1"]), bank(2), ACT.Exp).then_inc(egam, 1)
                    act.activation(glast, bank(2).rearrange("p (c i) -> p c i", c=NCH)[:, :, CH - 1], ACT.Exp).then_inc(egam, 1)
                    act.wait_ge(gnormed, 2 * p + 2)
                    kk = gk[p].rearrange("p (c i) -> p c i", c=NCH)
                    act.wait_ge(bd_cleared, 1)
                    if p:
                        act.wait_ge(o_ps, NCH * p)
                    for e in range(2):
                        act.activation(BD["KN"][64 * e:64 * e + 64, :, e, :], kk[64 * e:64 * e + 64], ACT.Copy).then_inc(knbd, 1)
                    act.wait_ge(dt_arg, p + 1)
                    act.activation(flat(CP["DT"]), flat(CP["DT"]), ACT.Exp).then_inc(dt_ready, 1)
                elif step in ("m1", "yt"):
                    if step == "yt" or arg[1]:
                        act.wait_ge(yt_ps, LEVELS * (arg if step == "yt" else arg[0]) + (LEVELS if step == "yt" else arg[1]))
                        for e in range(2):
                            act.activation(BD["Y"][64 * e:64 * e + 64, :, e, :], YT[:, :, CH * e:CH * e + CH],
                                           ACT.Copy).then_inc(invT_ready, 1)
                elif step == "guw":
                    p = arg
                    act.wait_ge(uw_ps, p + 1)
                    act.activation(flat(CP["VP"]), bank(4), ACT.Copy).then_inc(u_ready, 1)
                    act.activation(BD["KN"].rearrange("p c a i -> p (c a i)"), ps[:, 2 * L:4 * L], ACT.Copy).then_inc(wt_ready, 1)
                elif step == "gout":
                    p = arg
                    act.wait_ge(o_ps, NCH * (p + 1))
                    act.activation(flat(CP["M1"]), bank(2), ACT.Square).then_inc(o_sq, 1)
                elif step == "gfac":
                    p = arg
                    act.wait_ge(o_sum, p + 1)
                    link(act.activation(onorm[:, 1], onorm[:, 0], ACT.Ln, scale=1.0 / HD, bias=fixed[:, 0:1]))
                    act.activation(onorm[:, 1], onorm[:, 1], ACT.Exp, scale=-0.5).then_inc(o_fac, 1)
                elif step == "glu" and arg == 0:
                    act.preload_act_table(ACT.Gelu_apprx_tanh)
                    for f in range(2):
                        act.wait_ge(yd_ready, f + 1)
                        act.activation(su[f], su[f], ACT.Gelu_apprx_tanh).then_inc(gelu_ready, 1)
                elif step == "glu":
                    act.preload_act_table(ACT.Sigmoid)
                    for f in range(2):
                        act.wait_ge(glu_ps, f + 1)
                        act.activation(work[f].rearrange("p h t -> p (h t)"), bank(f), ACT.Sigmoid,
                                       bias=vec[:, V_GLUB + f:V_GLUB + f + 1]).then_inc(glu_sig, 1)
                    act.wait_ge(w_used, NPROJ)
                    for f in range(2):
                        act.wait_ge(mix_tmp, f + 1)
                        act.activation(hT_hi[:, 6 + f, :], su[f], ACT.Copy).then_inc(s5mix_h, 1)
                elif step == "gmix":
                    p = arg
                    act.wait_ge(gout_done, p + 1)
                    act.wait_ge(w_used, NPROJ)
                    act.activation(hT_hi[:, p, :], gz[p], ACT.Copy).then_inc(gmix_h, 1)
                elif step == "mla" and arg == 0:
                    act.preload_act_table(ACT.Ln)
                    act.wait_ge(gkk, 3)
                    act.wait_ge(xs_ready, 2 * ST)
                    act.activation(mrs[0], cq[0], ACT.Square).then_inc(mla_sq, 1)
                    act.activation(mrs[1][0:64], cq[1][0:64], ACT.Square).then_inc(mla_sq, 1)
                    act.activation(rope1, ckv, ACT.Square).then_inc(mla_sq, 1)
                    act.wait_ge(mla_ss, 1)
                    link(act.activation(mrs[0], bank(5), ACT.Ln, scale=1.0 / QLORA, bias=fixed[:, 0:1]))
                    act.wait_ge(mla_ss, 2)
                    link(act.activation(mrs[1], bank(6), ACT.Ln, scale=1.0 / KVLORA, bias=fixed[:, 0:1]))
                    act.activation(mrs[0], mrs[0], ACT.Exp, scale=-0.5).then_inc(mla_rn, 1)
                    act.activation(mrs[1], mrs[1], ACT.Exp, scale=-0.5).then_inc(mla_rn, 1)
                    act.wait_ge(s_mlaw, 96)
                    for k, kr in ((0, P), (1, 64)):
                        w4 = wuq[0:kr, k, H * HD:H * MLA_QK].rearrange("p (h n) -> p h n", h=H)
                        sw = wuq[0:kr, k, H * MLA_QK:].rearrange("p (h n) -> p h n", h=H)
                        act.activation(sw[:, :, 0:16], w4[:, :, 16:32], ACT.Copy).then_inc(wswap, 1)
                        act.activation(sw[:, :, 16:32], w4[:, :, 0:16], ACT.Copy).then_inc(wswap, 1)
                elif step == "mla" and arg == 1:
                    for pair in range(2):
                        act.wait_ge(mla_ps, 1 + pair)
                        b = MLA_BANKS[pair]
                        act.activation(q96[0:64, 2 * pair, :], bank(b)[0:64], ACT.Copy).then_inc(mla_ev, 1)
                        act.activation(q96[0:64, 2 * pair + 1, :], bank(b)[64:128], ACT.Copy).then_inc(mla_ev, 1)
                elif step == "mla":
                    for pair in range(2):
                        act.wait_ge(mla_ps, 5 + pair)
                        b = MLA_BANKS[4 + pair]
                        act.activation(k96[0:64, 2 * pair, :], bank(b)[0:64], ACT.Copy).then_inc(mla_ev, 1)
                        act.activation(k96[0:64, 2 * pair + 1, :], bank(b)[64:128], ACT.Copy).then_inc(mla_ev, 1)
                    act.wait_ge(krot, 1)
                    for h in range(1, H):
                        act.activation(k96[64:96, h, :], k96[64:96, 0, :], ACT.Copy).then_inc(kcopy, 1)
                    act.wait_ge(s5mix_l, 2)
                    for m in range(2):
                        act.wait_ge(mla_ps, 7 + m)
                        act.activation(mlav[:, 2 * m:2 * m + 2, :].rearrange("p t n -> p (t n)"), bank(MLA_BANKS[6 + m]),
                                       ACT.Copy).then_inc(mla_ev, 1)
                elif step == "att_s":
                    u = arg
                    if u < 0:
                        use_ln_exp()
                        act.wait_ge(w_l, N_OUT0 + RAW + 2)
                    if u + 1 < UNITS:
                        m, h, t = head_of(u + 1)
                        act.wait_ge(sc_max, u + 2)
                        if u >= 1:
                            act.wait_ge(pT_ps, u)
                        act.activation(prob[(u + 1) % 2][:, 0:P * (t + 1)], bank(5 + (u + 1) % 2, P * (t + 1)), ACT.Exp,
                                       bias=smx[:, 1, u + 1:u + 2], scale=SCALE[m],
                                       accum_out=smx[:, 2, u + 1:u + 2]).then_inc(p_exp, 1)
                elif step == "att_t":
                    u = arg
                    if 0 <= u < UNITS:
                        m, h, t = head_of(u)
                        act.wait_ge(pT_ps, u + 1)
                        if u >= 2:
                            act.wait_ge(pv_done, u - 1)
                        act.activation(probT[u % 2][:, 0:t + 1, :].rearrange("p k q -> p (k q)"),
                                       bank(transposed_bank(u), P * (t + 1)), ACT.Copy).then_inc(pT_ready, 1)
                    if u % 8 == 0 and u > 0:
                        mix_high(u // 8 - 1)

            for n in range(nxt, N_UP0):
                high_at(n)

            def up_split(i, b):
                for e in range(2):
                    n = N_UP0 + 4 * i + 2 * b + e
                    high(n, e, 2 * b + e, (w_loaded[e], 16 * (N_UP0 // 2 + 2 * i + b + 1) + EXTRA[e]))

            up_split(0, 0)
            use_ln_exp()
            def token_norm(t, ready, squared, col):
                act.wait_ge(ready, t + 1)
                act.activation(junk, x_sb[:, t, :], ACT.Square, accum_out=stat[:, col + t:col + t + 1]).then_inc(squared, 1)
                act.wait_ge(squared, 2 * t + 1)
                link(act.activation(stat[:, col + 4 + t:col + 5 + t], stat[:, col + t:col + t + 1], ACT.Ln,
                                    scale=1.0 / D, bias=fixed[:, 0:1]))
                act.activation(stat[:, col + 4 + t:col + 5 + t], stat[:, col + 4 + t:col + 5 + t], ACT.Exp,
                               scale=-0.5).then_inc(squared, 1)

            act.wait_ge(w_used, N_UP0 - 1)
            for t in range(TT):
                token_norm(t, x2_ready, x2_sq, 0)
            for k in range(KD):
                act.wait_ge(h2_t, k + 1)
                act.activation(hT_hi[:, k, :], bank(k), ACT.Copy, scale=vec[:, V_N2 + k:V_N2 + k + 1]).then_inc(h2_h, 1)

            def up_evac(i, b):
                j = 2 * i + b
                act.wait_ge(w_used, N_UP0 + 2 * j + 2)
                if not (isinstance(j, int) and j < 2):
                    act.wait_ge(g_ready, j - 1)
                for e in range(2):
                    act.activation(conv[2 * b + e], bank(2 * b + e), ACT.Copy,
                                   scale=taps[:, 2, e * JF + j, :]).then_inc(up_tap, 1)
                act.wait_ge(up_conv, 2 * j + 1)
                act.activation(conv[2 * b], conv[2 * b], ACT.Silu).then_inc(up_silu, 1)

            act.preload_act_table(ACT.Silu)
            up_split(0, 1)
            up_evac(0, 0)
            up_split(1, 0)
            up_evac(0, 1)
            up_split(1, 1)
            up_evac(1, 0)
            with act.Fori(2, JF // 2) as i:
                up_split(i, 0)
                up_evac(i - 1, 1)
                up_split(i, 1)
                up_evac(i, 0)

            def g_high(k, s):
                act.activation(hT_hi[:, s, :], g_sb[:, k, :], ACT.Copy).then_inc(g_h, 1)

            for k in range(2):
                high(N_DOWN0 + k, k, k, (w_loaded[k], 16 * (N_DOWN0 // 2 + 1) + EXTRA[k]))
            for k in range(4):
                act.wait_ge(g_ready, k + 1)
                act.wait_ge(h2_used, k + 1)
                g_high(k, k)
            up_evac(JF // 2 - 1, 1)
            for k in range(4):
                if k >= 2:
                    high(N_DOWN0 + k, k % 2, k, (w_loaded[k % 2], 16 * (N_DOWN0 // 2 + k // 2 + 1) + EXTRA[k % 2]))
            act.wait_ge(g_ready, JF)
            with act.Fori(1, 5) as i:
                for b in range(4):
                    act.wait_ge(w_used, N_DOWN0 + 4 * i + b - RING + 1)
                    g_high(4 * i + b, b)
                    high(N_DOWN0 + 4 * i + b, b % 2, b,
                         (w_loaded[b % 2], 16 * (N_DOWN0 // 2 + 2 * i + b // 2 + 1) + EXTRA[b % 2]))
            for k in range(20, JF):
                act.wait_ge(w_used, N_DOWN0 + k - RING + 1)
                g_high(k, k % 4)
                high(N_DOWN0 + k, k % 2, k % 4, (w_loaded[k % 2], 16 * (N_DOWN0 // 2 + k // 2 + 1) + EXTRA[k % 2]))
            use_ln_exp()
            for t in range(TT):
                token_norm(t, x3_ready, x3_sq, 8)

        @block.vector
        def _(dve):
            chain = [0]

            def link(ins):
                chain[0] += 1
                ins.then_inc(dve_step, 1)
                dve.wait_ge(dve_step, chain[0])

            S = lambda k: s5p[:, k, :]
            for m, n in enumerate(bd_names):
                ins = dve.memset(BD[n].rearrange("p c a i -> p (c a i)"), 0.0)
            ins.then_inc(bd_cleared, 1)

            dve.wait_ge(xsq, 1)
            for t in range(TT):
                dve.tensor_scalar(x_sb[:, t, :], x_sb[:, t, :], small[:, 4 + t:5 + t], None, ALU.mult).then_inc(xn, 1)
            dve.wait_ge(vec_t, 1)
            dve.tensor_copy(vec[:], bank(6, V_ROWS)).then_inc(vec_r, 1)
            dve.wait_ge(vec_r, 1)

            for k in range(KD):
                dve.wait_ge(hT_h, k + 1)
                dve.scalar_tensor_tensor(hT_lo[:, k, :], bank(HT_BANKS[k]), vec[:, V_N1 + k:V_N1 + k + 1],
                                         hT_hi[:, k, :].bitcast(F32), ALU.mult, ALU.subtract).then_inc(hT_l, 1)

            dve.wait_ge(vec_t, 3)
            dve.tensor_copy(taps[:].rearrange("p t j a -> p (t j a)"), bank(7, 6 * JF)).then_inc(vec_r, 1)

            dve.tensor_scalar(S(0), vec[:, V_LRE:V_LRE + 8], -1e-4, None, ALU.min)
            link(dve.tensor_copy(S(1), vec[:, V_LIM:V_LIM + 8]))
            dve.wait_ge(s5_act, 1)
            dve.tensor_tensor(S(3), S(0), S(2), ALU.mult).then_inc(s5_dve, 1)
            link(dve.tensor_tensor(S(4), S(1), S(2), ALU.mult))
            link(dve.tensor_scalar(S(5), S(4), 1.0 / (2.0 * math.pi), ROUND, ALU.mult, ALU.add))
            link(dve.tensor_scalar(S(5), S(5), ROUND, None, ALU.subtract))
            src = S(4)
            for part in TWO_PI:
                link(dve.scalar_tensor_tensor(S(6), S(5), -part, src, ALU.mult, ALU.add))
                src = S(6)
            link(dve.tensor_scalar(S(6), S(6), math.pi, -math.pi, ALU.min, ALU.max))
            link(dve.scalar_tensor_tensor(S(16), S(6), -1.0, S(6), ALU.mult, ALU.max))
            dve.tensor_scalar(S(16), S(16), -1.0, math.pi / 2, ALU.mult, ALU.add).then_inc(s5_dve, 1)
            link(dve.tensor_tensor(S(12), S(0), S(0), ALU.mult))
            link(dve.tensor_tensor(S(13), S(1), S(1), ALU.mult))
            link(dve.tensor_tensor(S(12), S(12), S(13), ALU.add))
            link(dve.reciprocal(S(13), S(12)))
            dve.wait_ge(s5_act, 4)
            link(dve.tensor_tensor(S(10), S(9), S(8), ALU.mult))
            link(dve.tensor_tensor(S(11), S(9), S(7), ALU.mult))
            link(dve.tensor_scalar(S(10), S(10), 1.0, None, ALU.subtract))
            dve.tensor_tensor(S(14), S(10), S(0), ALU.mult)
            dve.tensor_tensor(S(17), S(11), S(1), ALU.mult)
            dve.tensor_tensor(S(15), S(11), S(0), ALU.mult)
            link(dve.tensor_tensor(S(18), S(10), S(1), ALU.mult))
            dve.tensor_tensor(S(14), S(14), S(17), ALU.add)
            link(dve.tensor_tensor(S(15), S(15), S(18), ALU.subtract))
            dve.tensor_tensor(S(14), S(14), S(13), ALU.mult)
            link(dve.tensor_tensor(S(15), S(15), S(13), ALU.mult))
            cr = S(14).unsqueeze(2).broadcast_to([P, ST, GW])
            ci = S(15).unsqueeze(2).broadcast_to([P, ST, GW])
            dve.wait_ge(s_s5in, 64)
            dve.tensor_tensor(bbar[:, 0], b_nat[:, 0], cr, ALU.mult)
            link(dve.tensor_tensor(btmp, b_nat[:, 1], ci, ALU.mult))
            link(dve.tensor_tensor(bbar[:, 0], bbar[:, 0], btmp, ALU.subtract))
            dve.tensor_tensor(bbar[:, 1], b_nat[:, 1], cr, ALU.mult)
            link(dve.tensor_tensor(btmp, b_nat[:, 0], ci, ALU.mult))
            link(dve.tensor_tensor(bbar[:, 1], bbar[:, 1], btmp, ALU.add))
            for r in range(2):
                for g in range(2):
                    dve.tensor_scalar(bbd[:, r, :, g, :], bbar[:, r], C("bmask", 1, off=g), None,
                                      ALU.mult).then_inc(bbd_ready, 1)
            for g in range(2):
                for r in range(2):
                    dve.tensor_scalar(cbd[:, r, :, g, :], c_nat[:, r], C("cmask", 1, off=g), None,
                                      ALU.mult).then_inc(cbd_ready, 1)

            def table_level(n):
                lo = slice(0, n)
                up = slice(n, 2 * n)
                cb = cosT[:, :, n - 1:n].broadcast_to([P, ST, n])
                sb_ = sinT[:, :, n - 1:n].broadcast_to([P, ST, n])
                t1 = wtmp[:, 0:ST * n].rearrange("p (s t) -> p s t", s=ST)
                t2 = wtmp[:, ST * n:2 * ST * n].rearrange("p (s t) -> p s t", s=ST)
                dve.tensor_tensor(cosT[:, :, up], cosT[:, :, lo], cb, ALU.mult)
                dve.tensor_tensor(t1, sinT[:, :, lo], sb_, ALU.mult)
                dve.tensor_tensor(sinT[:, :, up], sinT[:, :, lo], cb, ALU.mult)
                link(dve.tensor_tensor(t2, cosT[:, :, lo], sb_, ALU.mult))
                dve.tensor_tensor(cosT[:, :, up], cosT[:, :, up], t1, ALU.subtract)
                link(dve.tensor_tensor(sinT[:, :, up], sinT[:, :, up], t2, ALU.add))

            def conv_taps(p, j, m, n):
                dst = (gq, gk, gv)[j][p]
                dve.wait_ge(conv0, m + 1)
                for tap, back in ((2, 1), (1, 2), (0, 3)):
                    col = V_CONV + 6 * tap + 2 * j + p
                    ins = dve.scalar_tensor_tensor(dst[:, back:], bank(n % 2)[:, 0:L - back], vec[:, col:col + 1],
                                                   dst[:, back:], ALU.mult, ALU.add)
                    if back < 3:
                        link(ins)
                ins.then_inc(conv_done, 1)

            def y_plus_d(f):
                dve.wait_ge(y_ps, 4 * f + 4)
                dve.scalar_tensor_tensor(su[f], su[f], vec[:, V_SD + f:V_SD + f + 1], bank(7), ALU.mult,
                                         ALU.add).then_inc(yd_ready, 1)

            def mix_low(pr):
                dve.wait_ge(attmix_h, 1 + pr)
                dve.tensor_tensor(hT_lo[:, 2 + pr, :], bank(MIX_BANK), hT_hi[:, 2 + pr, :].bitcast(F32),
                                  ALU.subtract).then_inc(attmix_l, 1)

            def tokc(q, p, e=None):
                v = tok if e is None else tok[64 * e:64 * e + 64]
                return v[:, :, q, p:p + 1].broadcast_to([P if e is None else 64, NCH, CH])

            def half(t, e):
                return t[64 * e:64 * e + 64]

            def ps3(b):
                return bank(b).rearrange("p (c i) -> p c i", c=NCH)

            n_conv = 0
            n_state = 0
            for step, arg in ORDER:
                if step == "proj":
                    n = arg
                    name = PROJ[n][0]
                    if n in CONV_TILES:
                        conv_taps(int(name[1]), "qkv".index(name[0]), n_conv, n)
                        n_conv += 1
                elif step == "table":
                    if arg == 0:
                        dve.wait_ge(hT_t, KD)
                        dve.wait_ge(bc_t, 2)
                        dve.tensor_copy(cosT[:, :, 0], S(8))
                        link(dve.tensor_copy(sinT[:, :, 0], S(7)))
                        for l in range(6):
                            table_level(1 << l)
                    else:
                        table_level(1 << (5 + arg))
                elif step == "rows" and arg == 0:
                    dve.wait_ge(row_act, 4)
                    dve.wait_ge(cleared, 1)
                    link(dve.scalar_tensor_tensor(rA, rA, 0.0, rB, ALU.max, ALU.add))
                    link(dve.tensor_scalar(rA, rA, small[0:4, 0:1], -1.0, ALU.mult, ALU.mult))
                    dve.tensor_scalar(rC, rC, 0.5, 0.5, ALU.mult, ALU.add).then_inc(dve_step, 1)
                    chain[0] += 1
                    dve.tensor_tensor_scan(rows[0:4, :], C("scanmask", lo=0, hi=4), rA, 0.0, ALU.mult, ALU.add).then_inc(row_dve, 1)
                    dve.wait_ge(dve_step, chain[0])
                    dve.tensor_copy(rows[32:36, :], rC)
                    dve.wait_ge(row_dve, 1)
                    gam = rows[0:4, :].rearrange("p (c i) -> p c i", c=NCH)
                    dve.tensor_tensor(rD.rearrange("p (c i) -> p c i", c=NCH), gam[:, :, CH - 1:CH].broadcast_to([4, NCH, CH]),
                                      gam, ALU.subtract).then_inc(row_dve, 1)
                elif step == "rows":
                    dve.wait_ge(row_act, 5)
                    dve.tensor_tensor(rows[64:68, :], rC, rB, ALU.mult).then_inc(row_dve, 1)
                elif step == "gates":
                    p = arg
                    dve.wait_ge(grn, 2 * p + 1)
                    dve.tensor_tensor(gq[p], gq[p], flat(CP["DT"]), ALU.mult).then_inc(gnormed, 1)
                    dve.wait_ge(grn, 2 * p + 2)
                    dve.tensor_tensor(gk[p], gk[p], flat(CP["VP"]), ALU.mult).then_inc(gnormed, 1)
                    if p == 0:
                        dve.wait_ge(tok_ps, 1)
                        dve.tensor_copy(tok.rearrange("p c q r -> p (c q r)"), bank(4, 8 * NCH)).then_inc(tok_ready, 1)
                        dve.wait_ge(tok_ready, 1)
                    dve.wait_ge(egam, 2 * p + 2)
                    dve.wait_ge(gnormed, 2 * p + 2)
                    link(dve.tensor_tensor(CP["DT"], ps3(2), tokc(0, p), ALU.subtract))
                    dve.scalar_tensor_tensor(CP["DT"], CP["DT"], 0.0, C("dmask").unsqueeze(1).broadcast_to([P, NCH, CH]),
                                             ALU.min, ALU.add).then_inc(dt_arg, 1)
                    for e in range(2):
                        dve.tensor_tensor(half(BD["QD"], e)[:, :, e, :], half(gq[p], e).rearrange("p (c i) -> p c i", c=NCH),
                                          half(CP["M1"], e), ALU.mult).then_inc(dve_step, 1)
                        chain[0] += 1
                    dve.wait_ge(dve_step, chain[0])
                    dve.wait_ge(gbc, 2 * p + 2)
                    dve.tensor_tensor(flat(CP["M1"]), gk[p], bank(3), ALU.mult).then_inc(gpre, 1)
                elif step == "gkk":
                    p = arg
                    dve.wait_ge(gkk, 3 * p + 2)
                    dve.wait_ge(dt_ready, p + 1)
                    for e in range(2):
                        ins = dve.tensor_tensor(half(BD["ATT"], e)[:, :, e, :], half(ps3(3), e), half(CP["DT"], e), ALU.mult)
                    ins.then_inc(gkk_used, 1)
                    for e in range(2):
                        ins = dve.tensor_tensor(half(BD["LT"], e)[:, :, e, :], half(ps3(2), e), half(CP["DT"], e), ALU.mult)
                    ins.then_inc(gkk_used, 1)
                    dve.wait_ge(gkk, 3 * p + 3)
                    for q, n in ((2, "KW"), (3, "KD")):
                        for e in range(2):
                            ins = dve.tensor_tensor(half(BD[n], e)[:, :, e, :], half(ps3(4), e), tokc(q, p, e), ALU.mult)
                        ins.then_inc(gkk_used, 1)
                elif step == "gv":
                    p = arg
                    dve.wait_ge(gvt, p + 1)
                    dve.tensor_tensor(CP["VP"], ps3(2), tokc(1, p), ALU.mult).then_inc(vp_ready, 1)
                elif step == "m1":
                    p, l = arg
                    dve.wait_ge(m1_ps, LEVELS * p + l + 1)
                    mask = C("level", 64, off=64 * l).unsqueeze(1).broadcast_to([P, NCH, CH])
                    dve.tensor_tensor(CP["M1"], ps3(4), mask, ALU.mult).then_inc(m1_ready, 1)
                    if l == 0:
                        dve.wait_ge(m1_ready, LEVELS * p + 1)
                        dve.tensor_tensor(CP["X"], istack.unsqueeze(1).broadcast_to([P, NCH, CH]), CP["M1"],
                                          ALU.subtract).then_inc(x_ready, 1)
                elif step == "m2":
                    p, l = arg
                    dve.wait_ge(m2_ps, (LEVELS - 1) * p + l)
                    dve.tensor_tensor(CP["X"], CP["X"], ps3(4), ALU.subtract).then_inc(x_ready, 1)
                elif step == "grec":
                    p, c = arg
                    if c:
                        dve.wait_ge(ws_ps, 7 * p + c)
                        dve.wait_ge(u_ready, p + 1)
                        dve.tensor_tensor(vnew[:, c % 2, :], CP["VP"][:, c, :], bank(4, HD), ALU.subtract).then_inc(vnew_ready, 1)
                    if c < NCH - 1:
                        dve.wait_ge(kv_ps, 7 * p + c + 1)
                        kv = ps[:, 3 * L + HD * (c % 2):3 * L + HD * (c % 2) + HD]
                        if c == 0:
                            if p:
                                dve.wait_ge(o_ps, NCH * p)
                            dve.tensor_copy(state[:, 0, :], kv).then_inc(state_ready, 1)
                        else:
                            dve.wait_ge(o_ps, NCH * p + c)
                            dve.scalar_tensor_tensor(state[:, c % 2, :], state[:, 1 - c % 2, :], glast[:, c:c + 1], kv,
                                                     ALU.mult, ALU.add).then_inc(state_ready, 1)
                        n_state += 1
                        dve.wait_ge(state_ready, n_state)
                elif step == "gout":
                    p = arg
                    dve.wait_ge(o_sq, p + 1)
                    dve.reduce_sum(onorm[:, 0], CP["M1"], axis=AX.X).then_inc(o_sum, 1)
                elif step == "gfac":
                    p = arg
                    dve.wait_ge(o_fac, p + 1)
                    for e in range(2):
                        dve.tensor_tensor(half(BD["QD"], e)[:, :, e, :], half(ps3(2), e),
                                          half(onorm, e)[:, 1, :].unsqueeze(2).broadcast_to([64, NCH, HD]),
                                          ALU.mult).then_inc(o_norm, 1)
                elif step == "gouT":
                    p = arg
                    dve.wait_ge(oT_ps, p + 1)
                    dve.wait_ge(z_ready, p + 1)
                    dve.scalar_tensor_tensor(gz[p], bank(4), vec[:, V_GN:V_GN + 1], gz[p], ALU.mult,
                                             ALU.mult).then_inc(gout_done, 1)
                elif step == "bu":
                    s = arg
                    dve.wait_ge(bu_ps, s + 1)
                    if s:
                        dve.wait_ge(xs_ready, 2 * s)
                    c2 = cosT[:, s:s + 1, :].broadcast_to([P, 2, HALF])
                    s2 = sinT[:, s:s + 1, :].broadcast_to([P, 2, HALF])
                    bur = bank(5).rearrange("p (h t) -> p h t", h=2)
                    bui = bank(6).rearrange("p (h t) -> p h t", h=2)
                    dve.tensor_tensor(work[0], bur, c2, ALU.mult)
                    dve.tensor_tensor(work[1], bui, s2, ALU.mult)
                    dve.tensor_tensor(work[2], bui, c2, ALU.mult)
                    dve.tensor_tensor(work[3], bur, s2, ALU.mult).then_inc(rot_prod, 1)
                elif step == "scan":
                    s = arg
                    mag = S(9)[:, s:s + 1].broadcast_to([P, HALF])
                    for e in range(2):
                        dve.wait_ge(rot_sum, 2 * s + 1 + e)
                        dve.tensor_tensor_scan(work[6 + e][:, 0, :], mag, work[4 + e][:, 0, :], 0.0, ALU.mult, ALU.add).then_inc(dve_step, 1)
                        chain[0] += 1
                    dve.wait_ge(dve_step, chain[0])
                    ce, se = cosT[:, s, HALF - 1:HALF], sinT[:, s, HALF - 1:HALF]
                    wr, wi = work[6][:, 0, HALF - 1:HALF], work[7][:, 0, HALF - 1:HALF]
                    dve.tensor_tensor(s5c[:, 0:1], wi, se, ALU.mult)
                    link(dve.tensor_tensor(s5c[:, 1:2], wi, ce, ALU.mult))
                    dve.scalar_tensor_tensor(s5c[:, 2:3], wr, ce, s5c[:, 0:1], ALU.mult, ALU.subtract)
                    link(dve.scalar_tensor_tensor(s5c[:, 3:4], wr, se, s5c[:, 1:2], ALU.mult, ALU.add))
                    for e in range(2):
                        ins = dve.tensor_tensor_scan(work[6 + e][:, 1, :], mag, work[4 + e][:, 1, :], s5c[:, 2 + e:3 + e],
                                                     ALU.mult, ALU.add)
                    link(ins)
                    c2 = cosT[:, s:s + 1, :].broadcast_to([P, 2, HALF])
                    s2 = sinT[:, s:s + 1, :].broadcast_to([P, 2, HALF])
                    dve.tensor_tensor(work[0], work[6], c2, ALU.mult)
                    dve.tensor_tensor(work[1], work[7], s2, ALU.mult)
                    dve.tensor_tensor(work[2], work[6], s2, ALU.mult)
                    dve.tensor_tensor(work[3], work[7], c2, ALU.mult).then_inc(unrot_prod, 1)
                    dve.wait_ge(unrot_prod, s + 1)
                    dve.tensor_tensor(work[4], work[0], work[1], ALU.subtract).then_inc(xs_ready, 1)
                    dve.tensor_tensor(work[5], work[2], work[3], ALU.add).then_inc(xs_ready, 1)
                    if s == ST // 2:
                        y_plus_d(0)
                elif step == "glu" and arg == 0:
                    y_plus_d(1)
                elif step == "glu":
                    dve.wait_ge(w_used, NPROJ)
                    dve.wait_ge(glu_ps, 2)
                    for f in range(2):
                        dve.wait_ge(glu_sig, f + 1)
                        dve.tensor_tensor(su[f], su[f], work[f].rearrange("p h t -> p (h t)"), ALU.mult).then_inc(mix_tmp, 1)
                    for f in range(2):
                        dve.wait_ge(mix_tmp, f + 1)
                        dve.wait_ge(s5mix_h, f + 1)
                        dve.tensor_tensor(hT_lo[:, 6 + f, :], su[f], hT_hi[:, 6 + f, :].bitcast(F32), ALU.subtract).then_inc(s5mix_l, 1)
                elif step == "gmix":
                    p = arg
                    dve.wait_ge(gout_done, p + 1)
                    dve.wait_ge(gmix_h, p + 1)
                    dve.tensor_tensor(hT_lo[:, p, :], gz[p], hT_hi[:, p, :].bitcast(F32), ALU.subtract).then_inc(gmix_l, 1)
                elif step == "mla_norm":
                    for m, (t, g, f) in enumerate(((cq[0], V_QN, mrs[0]), (cq[1][0:64], V_QN + 1, mrs[0][0:64]), (ckv, V_KVN, mrs[1]))):
                        dve.wait_ge(mla_rn, 1 if m < 2 else 2)
                        n_ = t.shape[0]
                        dve.scalar_tensor_tensor(t, t, vec[0:n_, g:g + 1], f, ALU.mult, ALU.mult).then_inc(mla_n, 1)
                elif step == "mla" and arg == 1:
                    dve.wait_ge(mla_ps, 3)
                    dve.tensor_tensor(rope1, bank(MLA_BANKS[2]), C("ropec"), ALU.mult)
                    dve.wait_ge(mla_ps, 4)
                    link(dve.tensor_tensor(rope2, bank(MLA_BANKS[3]), C("ropes"), ALU.mult))
                    for h in range(H):
                        ins = dve.tensor_tensor(q96[64:96, h, :], rope1[32 * h:32 * h + 32], rope2[32 * h:32 * h + 32], ALU.add)
                    link(ins)
                    dve.tensor_tensor(rope1[0:32], misc[0:32], C("ropec", lo=0, hi=32), ALU.mult)
                    link(dve.tensor_tensor(rope2[0:32], misc[32:64], C("ropes", lo=32, hi=64), ALU.mult))
                    dve.tensor_tensor(k96[64:96, 0, :], rope1[0:32], rope2[0:32], ALU.add).then_inc(krot, 1)
                elif step == "att_s":
                    u = arg
                    if 0 <= u < UNITS:
                        m, h, t = head_of(u)
                        dve.wait_ge(p_exp, u + 1)
                        link(dve.reciprocal(smx[:, 3, u:u + 1], smx[:, 2, u:u + 1]))
                        pr = prob[u % 2][:, 0:P * (t + 1)]
                        dve.tensor_scalar(pr, pr, smx[:, 3, u:u + 1], None, ALU.mult).then_inc(p_norm, 1)
                    if u + 1 < UNITS:
                        m, h, t = head_of(u + 1)
                        dve.wait_ge(sc_ps, u + 2)
                        link(dve.reduce_max(smx[:, 0, u + 1:u + 2], bank(5 + (u + 1) % 2, P * (t + 1)), axis=AX.X))
                        dve.tensor_scalar(smx[:, 1, u + 1:u + 2], smx[:, 0, u + 1:u + 2], -SCALE[m], None,
                                          ALU.mult).then_inc(sc_max, 1)
                elif step == "att_t":
                    if arg == UNITS or arg % 8 == 1 and arg > 8:
                        mix_low(arg // 8 - 1)

            def summed(t, done, all_done):
                if t < TT - 1:
                    dve.wait_ge(done, t + 1)
                else:
                    dve.wait_ge(w_used, all_done)
                for hf in range(2):
                    xs = x_sb[:, t, L * hf:L * hf + L]
                    ins = dve.tensor_tensor(xs, xs, bank(2 * t + hf), ALU.add)
                return ins

            def normed(t):
                dve.wait_ge(x2_ready, t + 1)
                dve.wait_ge(x2_sq, 2 * t + 2)
                dve.tensor_scalar(norm2[:, t, :], x_sb[:, t, :], stat[:, 4 + t:5 + t], None, ALU.mult).then_inc(n2_ready, 1)

            dve.wait_ge(s_xre, 16 * TT)
            for t in range(TT):
                summed(t, out_done, N_UP0).then_inc(x2_ready, 1)
                if t == TT - 1:
                    normed(0)
            for t in range(1, TT):
                normed(t)
            for k in range(KD):
                dve.wait_ge(h2_h, k + 1)
                dve.scalar_tensor_tensor(hT_lo[:, k, :], bank(k), vec[:, V_N2 + k:V_N2 + k + 1],
                                         hT_hi[:, k, :].bitcast(F32), ALU.mult, ALU.subtract).then_inc(h2_l, 1)

            def up(i, b):
                j = 2 * i + b
                for e in range(2):
                    t = conv[2 * b + e]
                    dve.wait_ge(up_tap, 2 * j + e + 1)
                    dve.scalar_tensor_tensor(t[:, 1:], bank(2 * b + e)[:, 0:L - 1], taps[:, 1, e * JF + j, :], t[:, 1:],
                                             ALU.mult, ALU.add).then_inc(up_mid, 1)
                    dve.wait_ge(up_mid, 2 * j + e + 1)
                    dve.scalar_tensor_tensor(t[:, 2:], bank(2 * b + e)[:, 0:L - 2], taps[:, 0, e * JF + j, :], t[:, 2:],
                                             ALU.mult, ALU.add).then_inc(up_conv, 1)
                dve.wait_ge(up_conv, 2 * j + 2)
                dve.wait_ge(up_silu, j + 1)
                dve.tensor_tensor(g_sb[:, j, :], conv[2 * b], conv[2 * b + 1], ALU.mult).then_inc(g_ready, 1)

            with dve.Fori(0, JF // 2 - 1) as i:
                for b in range(2):
                    up(i, b)
            up(JF // 2 - 1, 0)

            def g_low(k, s):
                dve.wait_ge(g_h, k + 1)
                dve.tensor_tensor(hT_lo[:, s, :], g_sb[:, k, :], hT_hi[:, s, :].bitcast(F32), ALU.subtract).then_inc(g_l, 1)

            for k in range(4):
                g_low(k, k)
            up(JF // 2 - 1, 1)
            dve.wait_ge(g_ready, JF)
            with dve.Fori(1, 5) as i:
                for b in range(4):
                    g_low(4 * i + b, b)
            for k in range(20, JF):
                g_low(k, k % 4)
            dve.wait_ge(s_fing, 16)

            def final(t):
                dve.wait_ge(x3_sq, 2 * t + 2)
                dve.scalar_tensor_tensor(x_sb[:, t, :], x_sb[:, t, :], stat[:, 12 + t:13 + t], fing, ALU.mult,
                                         ALU.mult).then_inc(y_ready, 1)

            for t in range(TT):
                summed(t, down_done, N_DOWN0 + JF).then_inc(x3_ready, 1)
                if t:
                    final(t - 1)
            final(TT - 1)

        @block.tensor
        def _(pe):
            def mm(out, lhsT, rhs, start=True, stop=True):
                return pe.matmul(out, lhsT, rhs, start=start, stop=stop)

            pe.wait_ge(s_const, 16)
            pe.wait_ge(xn, TT)
            for k in range(KD):
                if k == 4:
                    pe.wait_ge(s_vrows, 16 * 9)
                    pe.wait_ge(s_vrows2, 16 * (len(VECTORS) - 9))
                    pe.wait_ge(ldt_rows, 1)
                    pe.transpose(bank(6, V_ROWS), vrows[0:V_ROWS, :], C("ident", V_ROWS, hi=V_ROWS)).then_inc(vec_t, 1)
                b = HT_BANKS[k]
                if k >= 6:
                    pe.wait_ge(hT_l, k - 5)
                for t in range(TT):
                    ins = pe.transpose(ps[:, b * L + P * t:b * L + P * t + P], x_sb[:, t, P * k:P * k + P], ident)
                ins.then_inc(hT_t, 1)
            pe.wait_ge(s_taps, 32)
            pe.wait_ge(vec_r, 1)
            pe.transpose(bank(7, 88), taps_rows[0:88, 0, :], C("ident", 88, hi=88)).then_inc(vec_t, 1)
            pe.transpose(ps[:, 7 * L + 88:7 * L + 132], taps_rows[0:44, 1, :], C("ident", 44, hi=44)).then_inc(vec_t, 1)

            def split_products(out, lhs, rhs, first, last):
                for m, (l_, r_) in enumerate(((0, 0), (1, 0), (0, 1))):
                    ins = mm(out, lhs[l_], rhs[r_], start=first and m == 0, stop=last and m == 2)
                return ins

            def weights(s, cols=slice(0, D)):
                return w_hi[:, s, cols], w_lo[:, s, cols]

            def project(n):
                s = slot(n)
                pe.wait_ge(w_l, n + 1)
                if n < 2:
                    pe.wait_ge(hT_l, 5 + n)
                else:
                    pe.wait_ge(*freed_by[n - 2])
                for k in range(KD):
                    if n == 0:
                        pe.wait_ge(hT_l, k + 1)
                    ins = split_products(bank(n % 2), weights(s, slice(P * k, P * k + P)),
                                         (hT_hi[:, k, :], hT_lo[:, k, :]), k == 0, k == KD - 1)
                ins.then_inc(w_used, 1)

            def col(b, c, w=CH):
                return ps[:, b * L + w * c:b * L + w * c + w]

            def s5_y(s):
                pe.wait_ge(xs_ready, 2 * s + 2)
                if s == 4:
                    pe.wait_ge(yd_ready, 1)
                if s == 0:
                    pe.wait_ge(bc_ready, 3)
                q = 32 * (s % 4)
                out = ps[q:q + 32, 7 * L:8 * L]
                mm(out, ct[:, 0, s, :], work[4].rearrange("p h t -> p (h t)"), True, False)
                mm(out, ct[:, 1, s, :], work[5].rearrange("p h t -> p (h t)"), False, True).then_inc(y_ps, 1)

            def inverse_transposed(p, l):
                pe.wait_ge(x_ready, LEVELS * p + l + 1)
                if l == 0:
                    pe.wait_ge(vp_ready, p + 1)
                for c in range(NCH):
                    ins = pe.transpose(YT[:, c, :], CP["X"][:, c], ident)
                ins.then_inc(yt_ps, 1)

            for step, arg in ORDER:
                if step == "proj":
                    project(arg)
                elif step == "mvt":
                    n = VALUE_TILES[arg]
                    pe.wait_ge(*copied[n])
                    for t in range(TT):
                        at = n % 2 * L + P * t
                        ins = pe.transpose(ps[:, at:at + P], mvT[:, P * t:P * t + P], ident)
                    ins.then_inc(mv_t, 1)
                elif step == "table" and arg == 0:
                    pe.wait_ge(vec_r, 2)
                    pe.wait_ge(bbd_ready, 4)
                    for r in range(2):
                        for f in range(2):
                            at = 6 * L + P * (2 * r + f)
                            ins = pe.transpose(ps[:, at:at + P], bbd[:, r, 4 * f:4 * f + 4].rearrange("p s g c -> p (s g c)"), ident)
                    ins.then_inc(bc_t, 1)
                    pe.wait_ge(cbd_ready, 4)
                    for r in range(2):
                        for f in range(2):
                            at = 7 * L + P * (2 * r + f)
                            ins = pe.transpose(ps[:, at:at + P], cbd[:, r, f].rearrange("p g n -> p (g n)"), ident)
                    ins.then_inc(bc_t, 1)
                elif step == "gnorm":
                    p = arg
                    if p:
                        pe.wait_ge(o_norm, 2 * p)
                    for m, t in enumerate(("DT", "VP")):
                        pe.wait_ge(gsq, 2 * p + m + 1)
                        mm(bank(2 + m), C("blockones"), flat(CP[t])).then_inc(gss, 1)
                elif step == "gates":
                    p = arg
                    pe.wait_ge(row_act, 6)
                    pe.wait_ge(row_dve, 3)
                    pe.wait_ge(grn, 2 * p + 2)
                    mm(bank(2), C("selbc", P, lo=0, hi=4, off=P * p), rows[0:4, :]).then_inc(gbc, 1)
                    mm(bank(3), C("selbc", P, lo=32, hi=36, off=P * p), rows[32:36, :]).then_inc(gbc, 1)
                    if p == 0:
                        for c in range(NCH):
                            for e in range(2):
                                ins = mm(ps[64 * e:64 * e + 64, 4 * L + 8 * c:4 * L + 8 * c + 8],
                                         rows[0:100, CH * c:CH * c + CH], C("seltok", 8, lo=0, hi=100, off=8 * e))
                        ins.then_inc(tok_ps, 1)
                elif step == "gkk":
                    p = arg
                    pe.wait_ge(knbd, 2 * (p + 1))
                    pe.wait_ge(gpre, p + 1)
                    pe.wait_ge(egam, 2 * (p + 1))
                    pe.wait_ge(tok_ready, 1)
                    if p:
                        pe.wait_ge(gout_done, p)
                    for c in range(NCH):
                        ins = mm(col(2, c), blocks(BD["KN"], c), CP["M1"][:, c])
                    ins.then_inc(gkk, 1)
                    for c in range(NCH):
                        ins = mm(col(3, c), blocks(BD["KN"], c), gq[p][:, CH * c:CH * c + CH])
                    ins.then_inc(gkk, 1)
                    for c in range(NCH):
                        ins = mm(col(4, c), blocks(BD["KN"], c), istack)
                    ins.then_inc(gkk, 1)
                elif step == "gv":
                    p = arg
                    pe.wait_ge(vbd_ready, 2 * (p + 1))
                    pe.wait_ge(gkk_used, 4 * p + 2)
                    for c in range(NCH):
                        ins = mm(col(2, c), blocks(BD["Y"], c), istack)
                    ins.then_inc(gvt, 1)
                elif step == "m1":
                    p, l = arg
                    m = LEVELS * p + l
                    if l == 0:
                        pe.wait_ge(gkk_used, 4 * (p + 1))
                    else:
                        pe.wait_ge(x_ready, m)
                        inverse_transposed(p, l - 1)
                    for c in range(NCH):
                        ins = mm(col(4, c), blocks(BD["LT"], c), istack if l == 0 else CP["X"][:, c])
                    ins.then_inc(m1_ps, 1)
                elif step == "m2":
                    p, l = arg
                    m = LEVELS * p + l
                    pe.wait_ge(m1_ready, m + 1)
                    pe.wait_ge(invT_ready, 2 * m)
                    for c in range(NCH):
                        ins = mm(col(4, c), blocks(BD["Y"], c), CP["M1"][:, c])
                    ins.then_inc(m2_ps, 1)
                elif step == "yt":
                    inverse_transposed(arg, LEVELS - 1)
                elif step == "guw":
                    p = arg
                    m = 6 * p + 6
                    pe.wait_ge(invT_ready, 2 * m)
                    for c in range(NCH):
                        mm(col(4, c), blocks(BD["Y"], c), CP["VP"][:, c])
                    for c in range(NCH):
                        ins = mm(ps[:, 2 * L + P * c:2 * L + P * c + P], blocks(BD["KW"], c), blocks(BD["Y"], c))
                    ins.then_inc(uw_ps, 1)
                elif step == "grec":
                    p, c = arg
                    if c == 0:
                        pe.wait_ge(u_ready, p + 1)
                        pe.wait_ge(wt_ready, p + 1)
                        mm(col(3, 0), blocks(BD["KD"], 0), CP["VP"][:, 0]).then_inc(kv_ps, 1)
                        mm(col(2, 0), blocks(BD["ATT"], 0), CP["VP"][:, 0]).then_inc(o_ps, 1)
                    else:
                        pe.wait_ge(state_ready, 7 * p + c)
                        former = state[:, 1 - c % 2, :]
                        mm(col(4, 0), blocks(BD["KN"], c), former).then_inc(ws_ps, 1)
                        mm(col(2, c), blocks(BD["QD"], c), former, True, False)
                        pe.wait_ge(vnew_ready, 7 * p + c)
                        vn = vnew[:, c % 2, :]
                        if c < NCH - 1:
                            mm(col(3, c % 2), blocks(BD["KD"], c), vn).then_inc(kv_ps, 1)
                        mm(col(2, c), blocks(BD["ATT"], c), vn, False, True).then_inc(o_ps, 1)
                elif step == "gouT":
                    p = arg
                    pe.wait_ge(o_norm, 2 * (p + 1))
                    for c in range(NCH):
                        ins = mm(col(4, c), blocks(BD["QD"], c), istack)
                    ins.then_inc(oT_ps, 1)
                elif step == "bu":
                    s = arg
                    f, q = s // 4, 32 * (s % 4)
                    pe.wait_ge(proj_copied, freed_by[PN[f"u{f}"]][1])
                    pe.wait_ge(bc_ready, 3)
                    if s:
                        pe.wait_ge(rot_prod, s)
                    for r in range(2):
                        ins = mm(bank(5 + r), bt[q:q + 32, r, f, :], su[f][q:q + 32, :])
                    ins.then_inc(bu_ps, 1)
                    if s:
                        s5_y(s - 1)
                elif step == "glu" and arg == 0:
                    s5_y(ST - 1)
                elif step == "glu":
                    pe.wait_ge(gelu_ready, 2)
                    pe.wait_ge(s_glu, 16)
                    pe.wait_ge(*freed_by[NPROJ - 2])
                    pe.wait_ge(*freed_by[NPROJ - 1])
                    for f in range(2):
                        mm(bank(f), gluw[:, 0, P * f:P * f + P], su[0], True, False)
                        mm(bank(f), gluw[:, 1, P * f:P * f + P], su[1], False, True).then_inc(glu_ps, 1)
                elif step == "mla" and arg == 0:
                    pe.wait_ge(rot_prod, ST)
                    pe.wait_ge(mla_sq, 2)
                    mm(bank(5), C("ones"), mrs[0], True, False)
                    mm(bank(5), C("ones", hi=64), mrs[1][0:64], False, True).then_inc(mla_ss, 1)
                    pe.wait_ge(mla_sq, 3)
                    mm(bank(6), C("ones"), rope1).then_inc(mla_ss, 1)
                elif step == "mla" and arg == 1:
                    pe.wait_ge(mla_n, 3)
                    pe.wait_ge(wswap, 4)
                    pe.wait_ge(yd_ready, 2)
                    pe.wait_ge(glu_sig, 2)
                    for m in range(4):
                        b, cols = MLA_BANKS[m], slice(P * m, P * m + P)
                        mm(bank(b), wuq[:, 0, cols], cq[0], True, False)
                        mm(bank(b), wuq[0:64, 1, cols], cq[1][0:64], False, True).then_inc(mla_ps, 1)
                elif step == "mla":
                    for m in range(2):
                        if m:
                            pe.wait_ge(mla_ev, 2)
                        mm(bank(MLA_BANKS[4 + m]), wukv[:, P * m:P * m + P], ckv).then_inc(mla_ps, 1)
                    for m in range(2):
                        if m == 0:
                            pe.wait_ge(mla_ev, 4)
                        else:
                            pe.wait_ge(krot, 1)
                        for t in range(2):
                            b = MLA_BANKS[6 + m]
                            tk = P * (2 * m + t)
                            ins = mm(ps[:, b * L + 256 * t:b * L + 256 * t + 256], ckv[:, tk:tk + P], wukv[:, 256:512])
                        ins.then_inc(mla_ps, 1)
                elif step == "att_t":
                    def score(u):
                        m, h, t = head_of(u)
                        if u == 0:
                            pe.wait_ge(mla_ev, 10)
                            pe.wait_ge(krot, 1)
                            pe.wait_ge(kcopy, 3)
                            pe.wait_ge(masks16, 2)
                        if u >= 2:
                            pe.wait_ge(p_exp, u - 1)
                        b = 5 + u % 2
                        qs = slice(P * t, P * t + P)
                        if m == 0:
                            r = slice(64 * (h % 2), 64 * (h % 2) + 64)
                            q_, k_ = moq[h // 2][r, qs], mok[h // 2][r]
                        else:
                            q_, k_ = q96[0:96, h, qs], k96[0:96, h]
                        if t:
                            mm(bank(b, P * t), q_, k_[:, 0:P * t])
                        diag = ps[:, b * L + P * t:b * L + P * t + P]
                        mm(diag, q_, k_[:, qs], True, False)
                        mm(diag, ident16[:], causal16[:], False, True).then_inc(sc_ps, 1)

                    def pv(u):
                        m, h, t = head_of(u)
                        pe.wait_ge(pT_ready, u + 1)
                        if u % 8 == 0 and u:
                            pe.wait_ge(attmix_l, u // 8)
                        e = h % 2
                        v_ = mov if m == 0 else mlav
                        out = ps[64 * e:64 * e + 64, MIX_BANK * L + P * t:MIX_BANK * L + P * t + P]
                        for k in range(t + 1):
                            ins = mm(out, v_[:, k, HD * h:HD * h + HD], probT[u % 2][:, k, :], k == 0, k == t)
                        ins.then_inc(pv_done, 1)

                    u = arg
                    if u < 0:
                        score(0)
                        score(1)
                    elif u < UNITS:
                        m, h, t = head_of(u)
                        pe.wait_ge(p_norm, u + 1)
                        if u >= 2:
                            pe.wait_ge(pT_ready, u - 1)
                        for k in range(t + 1):
                            at = transposed_bank(u) * L + P * k
                            ins = pe.transpose(ps[:, at:at + P], prob[u % 2][:, P * k:P * k + P], ident)
                        ins.then_inc(pT_ps, 1)
                        if u + 2 < UNITS:
                            score(u + 2)
                        if u:
                            pv(u - 1)
                    else:
                        pv(UNITS - 1)

            def tokens_out(k, s, left, first, last, done):
                down_first = first and done is down_done
                out_first = first and done is out_done
                for t in (0, 2, 3, 1) if down_first else (1, 2, 3, 0) if out_first else range(TT):
                    tk = slice(P * t, P * t + P)
                    if down_first and t == 1:
                        pe.wait_ge(up_conv, 2 * JF)
                    if out_first and t == 0:
                        pe.wait_ge(attmix_l, 4)
                    for hf in range(2):
                        ins = split_products(bank(2 * t + hf), (hT_hi[:, left, tk], hT_lo[:, left, tk]),
                                             weights(s, slice(L * hf, L * hf + L)), first, last)
                    if last and t < TT - 1:
                        ins.then_inc(done, 1)
                ins.then_inc(w_used, 1)

            pe.wait_ge(gout_done, PAIRS)
            split = {6: (s5mix_l, 2), 0: (gmix_l, 1), 2: (attmix_l, 3), 1: (gmix_l, 2), 5: (attmix_l, 4)}
            for k in range(KD):
                pe.wait_ge(w_l, N_OUT0 + k + 1)
                if MIX_ORDER[k] in split:
                    pe.wait_ge(*split[MIX_ORDER[k]])
                tokens_out(k, slot(N_OUT0 + k), MIX_ORDER[k], k == 0, k == KD - 1, out_done)
            pe.wait_ge(x2_ready, TT)
            pe.wait_ge(n2_ready, TT)
            for k in range(KD):
                for t in range(TT):
                    ins = pe.transpose(ps[:, k * L + P * t:k * L + P * t + P], norm2[:, t, P * k:P * k + P], ident)
                ins.then_inc(h2_t, 1)

            def up(i, b):
                for e in range(2):
                    n = N_UP0 + 4 * i + 2 * b + e
                    pe.wait_ge(w_l, n + 1)
                    if not isinstance(i, int) or i:
                        pe.wait_ge(up_conv, 4 * i + 2 * b + e - 3)
                    for k in range(KD):
                        if isinstance(i, int) and i == b == e == 0:
                            pe.wait_ge(h2_l, k + 1)
                        ins = split_products(bank(2 * b + e), weights(2 * b + e, slice(P * k, P * k + P)),
                                             (hT_hi[:, k, :], hT_lo[:, k, :]), k == 0, k == KD - 1)
                        if isinstance(i, int) and i == JF // 2 - 1 and b == e == 1 and k < 4:
                            ins.then_inc(h2_used, 1)
                    ins.then_inc(w_used, 1)

            for b in range(2):
                up(0, b)
            with pe.Fori(1, JF // 2 - 1) as i:
                for b in range(2):
                    up(i, b)
            for b in range(2):
                up(JF // 2 - 1, b)

            def down(k, s):
                pe.wait_ge(w_l, N_DOWN0 + k + 1)
                pe.wait_ge(g_l, k + 1)
                tokens_out(k, s, s, isinstance(k, int) and k == 0, isinstance(k, int) and k == JF - 1, down_done)

            for k in range(4):
                down(k, k)
            with pe.Fori(1, 5) as i:
                for b in range(4):
                    down(4 * i + b, b)
            for k in range(20, JF):
                down(k, k % 4)


_INS = ["x", "norm1_g", "w_in", "gdn_conv_w", "gdn_a_log", "gdn_dt_bias", "gdn_norm_g", "mla_q_norm_g",
        "mla_w_uq", "mla_kv_norm_g", "mla_w_ukv", "s5_lam_re", "s5_lam_im", "s5_b_re", "s5_b_im",
        "s5_c_re", "s5_c_im", "s5_d", "s5_log_dt", "s5_glu_w", "s5_glu_b", "w_out", "norm2_g",
        "ffn_w_up", "ffn_conv_w", "ffn_w_down", "final_norm_g"]


def kernel(**inputs):
    import numpy as _np
    import concourse.bacc as _bacc
    from concourse import mybir as _mybir
    from concourse.bass_utils import run_bass_kernel_spmd as _run

    nc = _bacc.Bacc("TRN2", target_bir_lowering=False, num_devices=1)
    arrays, aps = {}, {}
    for name in _INS:
        arr = _np.ascontiguousarray(inputs[name])
        arrays[f"in_{name}"] = arr
        aps[name] = nc.dram_tensor(f"in_{name}", arr.shape, _mybir.dt.from_np(arr.dtype), kind="ExternalInput").ap()
    arrays["constants"] = constants()
    aps["constants"] = nc.dram_tensor("constants", (P, CONST_COLS), F32, kind="ExternalInput").ap()
    aps["out"] = nc.dram_tensor("out", (1, L, D), F32, kind="ExternalOutput").ap()
    hybrid_trunk(nc, aps)
    r = _run(nc, [arrays], core_ids=[0])
    return r.results[0]["out"]
```
